# Optimizing a Trainium2 kernel written in Bass

```python
import math
import jax, jax.numpy as jnp
from jax import lax
import numpy as np

D_MODEL = 1024
BATCH = 1
SEQ = 256
DEPTH = 2

GRID_W = 64
CTX_LEN = 256

MLA_HEADS = 8
QK_NOPE = 64
QK_ROPE = 32
V_DIM = 64
Q_LORA = 256
KV_LORA = 128
Q_BLOCK = 128
ROPE_BASE = 10000.0
ATTN_SCALE = (QK_NOPE + QK_ROPE) ** -0.5
ATTN_W = MLA_HEADS * V_DIM

POOL_WINDOWS = (2, 4, 8, 16)
POOL_GROUPS = 4
POOL_W = D_MODEL // 2
POOL_GC = POOL_W // POOL_GROUPS

IN_W = Q_LORA + KV_LORA + QK_ROPE + POOL_W
IN_SPLITS = (Q_LORA, Q_LORA + KV_LORA, Q_LORA + KV_LORA + QK_ROPE)
MIX_W = ATTN_W + POOL_W

FNET_GROUPS = 4
FNET_GC = D_MODEL // FNET_GROUPS

D_FF_DENSE = 2816
N_EXPERTS = 8
TOP_K = 2
D_FF_EXPERT = 3584

N_EVEN = (DEPTH + 1) // 2
N_ODD = DEPTH // 2
EPS = 1e-6

kernel_name = "hybrid_mla_pool_fnet_moe_prefix_dit"

def rmsnorm(x, g):
    x32 = x.astype(jnp.float32)
    y = x32 * lax.rsqrt(jnp.mean(x32 * x32, axis=-1, keepdims=True) + EPS)
    return (y * g.astype(jnp.float32)).astype(x.dtype)

def modulate(x, g, shift, scale):
    return rmsnorm(x, g) * (1.0 + scale) + shift

def axial_rope_tables(rows, dtype):
    row = jnp.repeat(jnp.arange(rows), GRID_W).astype(jnp.float32)
    col = jnp.tile(jnp.arange(GRID_W), rows).astype(jnp.float32)
    half = QK_ROPE // 2
    inv = 1.0 / (ROPE_BASE ** (jnp.arange(0, half, 2, dtype=jnp.float32) / half))
    ang_r = row[:, None] * inv[None, :]
    ang_c = col[:, None] * inv[None, :]
    return (jnp.cos(ang_r).astype(dtype), jnp.sin(ang_r).astype(dtype),
            jnp.cos(ang_c).astype(dtype), jnp.sin(ang_c).astype(dtype))

def rotate(x, cos, sin):
    x1, x2 = jnp.split(x, 2, axis=-1)
    return jnp.concatenate([x1 * cos - x2 * sin, x1 * sin + x2 * cos], axis=-1)

def axial_rope(x, tabs):
    cos_r, sin_r, cos_c, sin_c = tabs
    xr, xc = jnp.split(x, 2, axis=-1)
    return jnp.concatenate([rotate(xr, cos_r, sin_r), rotate(xc, cos_c, sin_c)], axis=-1)

def mla_q(c_q, g_cq, w_uq):
    B, L, _ = c_q.shape
    q = (rmsnorm(c_q, g_cq) @ w_uq).reshape(B, L, MLA_HEADS, QK_NOPE + QK_ROPE)
    return q[..., :QK_NOPE], q[..., QK_NOPE:]

def mla_kv(c_kv, g_ckv, w_ukv):
    B, L, _ = c_kv.shape
    kv = (rmsnorm(c_kv, g_ckv) @ w_ukv).reshape(B, L, MLA_HEADS, QK_NOPE + V_DIM)
    return kv[..., :QK_NOPE], kv[..., QK_NOPE:]

def mla_attend(q_nope, q_rope, k_nope, k_rope, v):
    s = (jnp.einsum('bqhd,bkhd->bhqk', q_nope, k_nope)
         + jnp.einsum('bqhr,bkr->bhqk', q_rope, k_rope))
    p = jax.nn.softmax(s.astype(jnp.float32) * ATTN_SCALE, axis=-1).astype(v.dtype)
    return jnp.einsum('bhqk,bkhd->bqhd', p, v)

def mla_blocked(q_nope, q_rope, k_nope, k_rope, v):
    B, L, H, _ = q_nope.shape
    nb = L // Q_BLOCK

    def to_blocks(t):
        return jnp.moveaxis(t.reshape(B, nb, Q_BLOCK, *t.shape[2:]), 1, 0)

    out = lax.map(lambda qs: mla_attend(qs[0], qs[1], k_nope, k_rope, v),
                  (to_blocks(q_nope), to_blocks(q_rope)))
    return jnp.moveaxis(out, 0, 1).reshape(B, L, H * V_DIM)

def multiscale_pool(p, pool_w, pool_scale):
    B, L, _ = p.shape
    pg = p.reshape(B, L, POOL_GROUPS, POOL_GC)
    csum = jnp.cumsum(pg.astype(jnp.float32), axis=1)
    csum = jnp.concatenate([jnp.zeros_like(csum[:, :1]), csum], axis=1)
    t = jnp.arange(L)[:, None]
    w = jnp.array(POOL_WINDOWS)[None, :]
    lo = jnp.clip(t - w // 2, 0, L)
    hi = jnp.clip(t - w // 2 + w, 0, L)
    g = jnp.arange(POOL_GROUPS)[None, :]
    win_sum = csum[:, hi, g, :] - csum[:, lo, g, :]
    mean = win_sum / (hi - lo).astype(jnp.float32)[:, :, None]
    mixed = (mean - pg.astype(jnp.float32)).astype(p.dtype)
    y = jnp.einsum('blgc,gcd->blgd', mixed, pool_w).reshape(B, L, POOL_W)
    return y * pool_scale

def fourier_mix(h, w_out):
    B, L, D = h.shape
    hg = h.astype(jnp.float32).reshape(B, L, FNET_GROUPS, FNET_GC)
    f = jnp.fft.fft2(hg, axes=(1, 3), norm='ortho').real.astype(h.dtype)
    return f.reshape(B, L, D) @ w_out

def swiglu(h, w1, w3, w2):
    return (jax.nn.silu(h @ w1) * (h @ w3)) @ w2

def moe_swiglu(h, router_w, w1, w3, w2):
    logits = (h @ router_w).astype(jnp.float32)
    top_v, top_i = lax.top_k(logits, TOP_K)
    top_p = jax.nn.softmax(top_v, axis=-1)
    gates = jnp.sum(jax.nn.one_hot(top_i, N_EXPERTS, dtype=jnp.float32) * top_p[..., None],
                    axis=-2).astype(h.dtype)
    y = jnp.zeros_like(h)
    for e in range(N_EXPERTS):
        y = y + gates[..., e:e + 1] * swiglu(h, w1[e], w3[e], w2[e])
    return y

def setup_inputs(seed: int = 0) -> dict:
    key = jax.random.key(seed)
    ks = iter(jax.random.split(key, 32))
    D = D_MODEL
    HQ = MLA_HEADS * (QK_NOPE + QK_ROPE)
    HKV = MLA_HEADS * (QK_NOPE + V_DIM)

    def nrm(shape, scale):
        return jax.random.normal(next(ks), shape, jnp.float32) * scale

    return {
        "x": nrm((BATCH, SEQ, D), 1.0),
        "c": nrm((BATCH, D), 1.0),
        "ctx": nrm((BATCH, CTX_LEN, D), 1.0),
        "c_ctx": nrm((D,), 1.0),
        "ada_w": nrm((DEPTH, D, 6 * D), 0.5 * D ** -0.5),
        "ada_b": nrm((DEPTH, 6 * D), 0.02),
        "norm_mix_g": 1.0 + nrm((DEPTH, D), 0.02),
        "norm_ffn_g": 1.0 + nrm((DEPTH, D), 0.02),
        "mix_in_w": nrm((N_EVEN, D, IN_W), D ** -0.5),
        "cq_norm_g": 1.0 + nrm((N_EVEN, Q_LORA), 0.02),
        "ckv_norm_g": 1.0 + nrm((N_EVEN, KV_LORA), 0.02),
        "w_uq": nrm((N_EVEN, Q_LORA, HQ), Q_LORA ** -0.5),
        "w_ukv": nrm((N_EVEN, KV_LORA, HKV), KV_LORA ** -0.5),
        "pool_w": nrm((N_EVEN, POOL_GROUPS, POOL_GC, POOL_GC), POOL_GC ** -0.5),
        "pool_scale": 1.0 + nrm((N_EVEN, POOL_W), 0.02),
        "mix_out_w": nrm((N_EVEN, MIX_W, D), MIX_W ** -0.5),
        "ffn_w1": nrm((N_EVEN, D, D_FF_DENSE), D ** -0.5),
        "ffn_w3": nrm((N_EVEN, D, D_FF_DENSE), D ** -0.5),
        "ffn_w2": nrm((N_EVEN, D_FF_DENSE, D), D_FF_DENSE ** -0.5),
        "fnet_out_w": nrm((N_ODD, D, D), D ** -0.5),
        "router_w": nrm((N_ODD, D, N_EXPERTS), D ** -0.5),
        "moe_w1": nrm((N_ODD, N_EXPERTS, D, D_FF_EXPERT), D ** -0.5),
        "moe_w3": nrm((N_ODD, N_EXPERTS, D, D_FF_EXPERT), D ** -0.5),
        "moe_w2": nrm((N_ODD, N_EXPERTS, D_FF_EXPERT, D), D_FF_EXPERT ** -0.5),
        "final_g": 1.0 + nrm((D,), 0.02),
    }

def reference(x, c, ctx, c_ctx, ada_w, ada_b, norm_mix_g, norm_ffn_g, mix_in_w, cq_norm_g,
              ckv_norm_g, w_uq, w_ukv, pool_w, pool_scale, mix_out_w, ffn_w1, ffn_w3, ffn_w2,
              fnet_out_w, router_w, moe_w1, moe_w3, moe_w2, final_g):
    B, L, D = x.shape
    Lc = ctx.shape[1]
    ROWS = L // GRID_W
    tabs = axial_rope_tables(ROWS, x.dtype)
    tabs_q = tuple(t[:, None, :] for t in tabs)
    s_lat = jax.nn.silu(c)
    s_ctx = jax.nn.silu(c_ctx)[None, :]

    for i in range(DEPTH):
        sh1, sc1, g1, sh2, sc2, g2 = jnp.split((s_lat @ ada_w[i] + ada_b[i])[:, None, :], 6, axis=-1)
        cs1, cc1, cg1, cs2, cc2, cg2 = jnp.split((s_ctx @ ada_w[i] + ada_b[i])[:, None, :], 6, axis=-1)
        ctx_needed = any(j % 2 == 0 for j in range(i + 1, DEPTH))

        h = modulate(x, norm_mix_g[i], sh1, sc1)
        if i % 2 == 0:
            e = i // 2
            hc = modulate(ctx, norm_mix_g[i], cs1, cc1)
            cq_c, ckv_c, kr_c, pool_c = jnp.split(hc @ mix_in_w[e], IN_SPLITS, axis=-1)
            kn_c, v_c = mla_kv(ckv_c, ckv_norm_g[e], w_ukv[e])
            cq_l, ckv_l, kr_l, pool_l = jnp.split(h @ mix_in_w[e], IN_SPLITS, axis=-1)
            qn_l, qr_l = mla_q(cq_l, cq_norm_g[e], w_uq[e])
            kn_l, v_l = mla_kv(ckv_l, ckv_norm_g[e], w_ukv[e])
            qr_l = axial_rope(qr_l, tabs_q)
            kr_l = axial_rope(kr_l, tabs)
            attn_l = mla_blocked(qn_l, qr_l,
                                 jnp.concatenate([kn_l, kn_c], axis=1),
                                 jnp.concatenate([kr_l, kr_c], axis=1),
                                 jnp.concatenate([v_l, v_c], axis=1))
            pool_out_l = multiscale_pool(pool_l, pool_w[e], pool_scale[e])
            mix_l = jnp.concatenate([attn_l, pool_out_l], axis=-1) @ mix_out_w[e]
            if ctx_needed:
                qn_c, qr_c = mla_q(cq_c, cq_norm_g[e], w_uq[e])
                attn_c = mla_attend(qn_c, qr_c, kn_c, kr_c, v_c).reshape(B, Lc, ATTN_W)
                pool_out_c = multiscale_pool(pool_c, pool_w[e], pool_scale[e])
                mix_c = jnp.concatenate([attn_c, pool_out_c], axis=-1) @ mix_out_w[e]
        else:
            o = i // 2
            mix_l = fourier_mix(h, fnet_out_w[o])
            if ctx_needed:
                hc = modulate(ctx, norm_mix_g[i], cs1, cc1)
                mix_c = fourier_mix(hc, fnet_out_w[o])

        x = x + g1 * mix_l
        h = modulate(x, norm_ffn_g[i], sh2, sc2)
        if i % 2 == 0:
            x = x + g2 * swiglu(h, ffn_w1[i // 2], ffn_w3[i // 2], ffn_w2[i // 2])
        else:
            x = x + g2 * moe_swiglu(h, router_w[i // 2], moe_w1[i // 2], moe_w3[i // 2], moe_w2[i // 2])

        if ctx_needed:
            ctx = ctx + cg1 * mix_c
            hc = modulate(ctx, norm_ffn_g[i], cs2, cc2)
            if i % 2 == 0:
                ctx = ctx + cg2 * swiglu(hc, ffn_w1[i // 2], ffn_w3[i // 2], ffn_w2[i // 2])
            else:
                ctx = ctx + cg2 * moe_swiglu(hc, router_w[i // 2], moe_w1[i // 2], moe_w3[i // 2], moe_w2[i // 2])

    return rmsnorm(x, final_g)


_drawn_inputs = setup_inputs


def setup_inputs(seed=0):
    import zlib

    import numpy as np

    out = dict(_drawn_inputs(seed))
    spreads = {}
    factors = {'ctx': 4.238,
     'norm_mix_g': 6.921,
     'norm_ffn_g': 4.216,
     'cq_norm_g': 8.0,
     'ckv_norm_g': 8.0,
     'pool_scale': 6.458,
     'final_g': 2.851}
    for name, (base, spread) in spreads.items():
        noise = np.random.default_rng([zlib.crc32(name.encode()), seed]).standard_normal(out[name].shape)
        drawn = base * np.exp(spread * noise) if base else spread * noise
        out[name] = __import__('jax').numpy.asarray(drawn.astype(out[name].dtype))
    for name, factor in factors.items():
        out[name] = (out[name] * factor).astype(out[name].dtype)
    return out
```

```python
import math
from contextlib import ExitStack

import numpy as np

import concourse.bass as bass
from concourse import mybir

F32 = mybir.dt.float32
I32 = mybir.dt.int32
ALU = mybir.AluOpType
ACT = mybir.ActivationFunctionType
AX_X = mybir.AxisListType.X

P = 128
D = 1024
KD = D // P
T = 256
TC = 256
TA = T + TC
GRID_W = 64
HEADS, NOPE, ROPE, VD = 8, 64, 32, 64
QK = NOPE + ROPE
Q_LORA, KV_LORA = 256, 128
WINDOWS = (2, 4, 8, 16)
NG = 4
GC = D // NG
F_DENSE, F_EXPERT, EXPERTS = 2816, 3584, 8
PAIR = 2 * P
GROUPS_DENSE = F_DENSE // PAIR
GROUPS = F_EXPERT // PAIR
SCALE = float(QK) ** -0.5
EPS = 1e-6

CAP = 96
MAX_ROUNDS = -(-T // CAP)
TABLE = EXPERTS * (MAX_ROUNDS + 1)

SLOT = 3 * KD * PAIR
SLOTS = 7
STREAM_SLOTS = 4
ADA_COLS = SLOT // KD
ADA_UNITS = 6 * D // ADA_COLS
ADA_CHUNKS = ADA_COLS // P
PAD = 16
PADDED = T + 2 * PAD

VEC = {}
_at = 0
for _name, _n in (("mix_g", 16), ("ffn_g", 16), ("final_g", 8), ("cq_g", 2), ("ckv_g", 1), ("pool_scale", 4),
                  ("ada_b", 96), ("cond", 16)):
    VEC[_name] = (_at, _at + _n)
    _at += _n
VECS = _at

CON = {}
_at = 0
for _name, _n in (("ident", P), ("mean", P), ("before", P), ("ones", P), ("rot", QK), ("iota8", EXPERTS),
                  ("iota", CAP), ("eps", 1)):
    CON[_name] = (_at, _at + _n)
    _at += _n
CONS = _at


def constants():
    con = np.zeros((P, CONS), np.float32)

    def put(name, a):
        con[:a.shape[0], CON[name][0]:CON[name][1]] = a

    put("ident", np.eye(P))
    put("mean", np.full((P, P), 1.0 / D))
    put("before", np.triu(np.ones((P, P)), 1))
    put("ones", np.ones((P, P)))
    rot = np.zeros((QK, QK))
    half = ROPE // 4
    for b in (NOPE, NOPE + ROPE // 2):
        for j in range(half):
            rot[b + half + j, b + j] = -1.0
            rot[b + j, b + half + j] = 1.0
    put("rot", rot)
    put("iota8", np.tile(np.arange(EXPERTS), (P, 1)))
    put("iota", np.tile(np.arange(CAP), (P, 1)))
    put("eps", np.full((P, 1), EPS))

    t = np.arange(T)
    inv = (1.0 / (np.float32(10000.0) ** (np.arange(0, ROPE // 2, 2, dtype=np.float32) / np.float32(ROPE // 2))))
    inv = inv.astype(np.float32)
    angle = np.zeros((ROPE, T), np.float32)
    for b, position in ((0, t // GRID_W), (ROPE // 2, t % GRID_W)):
        a = inv[:, None] * position.astype(np.float32)[None, :]
        angle[b:b + half] = a
        angle[b + half:b + 2 * half] = a
    rope = np.concatenate([np.cos(angle), np.sin(angle)], axis=1).astype(np.float32)

    count = np.zeros((NG, T))
    for g, w in enumerate(WINDOWS):
        count[g] = np.clip(t - w // 2 + w, 0, T) - np.clip(t - w // 2, 0, T)
    invcount = np.tile((1.0 / count).reshape(1, NG * T), (P, 1)).astype(np.float32)

    c = np.arange(GC)
    a = 2.0 * np.pi * ((c[:, None] * c[None, :]) % GC) / GC
    chan = np.concatenate([np.cos(a), np.sin(a)], axis=1).reshape(2, P, 2 * GC).transpose(1, 0, 2).reshape(P, -1)
    a = 2.0 * np.pi * ((t[:, None] * t[None, :]) % T) / T
    norm = 1.0 / math.sqrt(T * GC)
    row = np.stack([np.cos(a) * norm, -np.sin(a) * norm]).reshape(2, 2, P, T).transpose(2, 0, 1, 3).reshape(P, -1)
    dft = np.concatenate([chan, row], axis=1).astype(np.float32)
    return con, rope, invcount, dft


def build(nc, vec_d, con_d, rope_d, invcount_d, x_d, ctx_d, ada_d, mixa_d, mixb_d, attn_d, mixout_d, ffn_d,
          dft_d, fnet_d, router_d, moe_d, out_d):
    ctx = ExitStack()
    with ctx:
        def sb(name, cols, dt=F32):
            return ctx.enter_context(nc.sbuf_tensor(name, [P, cols], dt))

        def sem(name):
            return ctx.enter_context(nc.semaphore(name))

        ring = sb("ring", SLOTS * SLOT)
        xT = sb("xT", KD * T)
        con = sb("con", CONS)
        vec = sb("vec", VECS)
        ada = sb("ada", 2 * 96)
        moda = sb("moda", 5 * KD)
        rstd = sb("rstd", TA)
        small = sb("small", 256)
        loops = sb("loops", 2, I32)
        work = sb("work", 6208)
        bank = [ctx.enter_context(nc.psum_tensor(f"bank{b}", [P, 512], F32)) for b in range(8)]

        def view(t, at, *dims):
            n = int(np.prod(dims))
            v = t[:, at:at + n]
            if len(dims) == 2:
                return v.rearrange("p (a b) -> p a b", a=dims[0])
            if len(dims) == 3:
                return v.rearrange("p (a b c) -> p a b c", a=dims[0], b=dims[1])
            return v

        def C(name):
            return con[:, CON[name][0]:CON[name][1]]

        def V(name):
            return vec[:, VEC[name][0]:VEC[name][1]]

        x = view(xT, 0, KD, T)
        cond = view(small, 0, KD, 2)
        scratch = STREAM_SLOTS * SLOT
        square = view(ring, scratch, KD, TA)
        keys = view(ring, scratch, HEADS, TA)
        h_all = view(ring, scratch + 4096, KD, TA)
        values = view(ring, scratch + 4096, 4, HEADS * VD)
        probs = view(ring, scratch + 6144, 4, TA)
        ctxT = view(ring, scratch + 8192, KD, TC)
        queries = view(ring, scratch + 8192, HEADS, T)
        lora_sq = view(ring, scratch + 10240, 2, 512)
        rope_tmp = view(ring, scratch + 10240, 512)
        probsT = view(ring, scratch + 10240, 2, 4, T)
        mixed = view(ring, scratch + 12288, KD, T)
        cqT = view(ring, scratch + 14336, 2, T)
        ckvT = view(ring, scratch + 14848, TA)
        krT = view(ring, scratch + 15360, TA)
        pool0 = view(ring, scratch + 15872, NG, PADDED)
        invcount = view(ring, scratch + 17024, NG, T)
        square_l = view(ring, scratch, KD, T)
        h = view(ring, scratch + 4096, KD, T)
        gate_tmp = view(ring, scratch + 6144, 2, 2, T)
        hidden = view(ring, scratch + 7168, 2, 2, T)
        spectrum = view(ring, scratch + 8192, 2, NG, 2 * GC)
        fourier = view(ring, scratch + 12288, KD, T)
        w_uq = view(work, 0, 2, HEADS * QK)
        w_ukv = view(work, 1536, 2, HEADS * VD)
        pool_w = view(work, 2560, NG, P)
        pool1 = view(work, 3072, NG, PADDED)
        pool2 = view(work, 4224, NG, PADDED)
        rope = view(work, 5376, 2, T)
        h_tok = view(work, 0, 2, D)
        h_exp = view(work, 2048, KD, CAP)
        gate_e = view(work, 2816, 2, 2, CAP)
        hidden_e = view(work, 3200, 2, 2, CAP)
        yT = view(work, 3584, KD, CAP)
        y_tok = work[0:CAP, 4352:5376]
        pick = view(work, 5376, 2, CAP)
        pick_gated = view(work, 5568, 2, CAP)
        spread = work[0:CAP, 5760:6016]
        rank_at = view(work, 6016, 2, TABLE)
        gate_at = view(work, 6080, 2, TABLE)
        router = view(work, 6144, KD, EXPERTS)
        assert TABLE == 32 and SLOTS * SLOT - scratch >= 18048

        vec_in, con_in, x_in, ctx_in = sem("vec_in"), sem("con_in"), sem("x_in"), sem("ctx_in")
        attn_in, rope_in, count_in, router_in = sem("attn_in"), sem("rope_in"), sem("count_in"), sem("router_in")
        slot_in = [sem(f"slot_in{i}") for i in range(SLOTS)]
        slot_free = [sem(f"slot_free{i}") for i in range(STREAM_SLOTS)]
        scratch_free = sem("scratch_free")
        cond_ready = sem("cond_ready")
        ada_ready, ada_taken = sem("ada_ready"), sem("ada_taken")
        squared, mean_ready, root_ready = sem("squared"), sem("mean_ready"), sem("root_ready")
        scaled, h_ready = sem("scaled"), sem("h_ready")
        pads_zero = sem("pads_zero")
        mixa_ready, mixa_taken = sem("mixa_ready"), sem("mixa_taken")
        mixb_ready, cq_taken, kv_taken = sem("mixb_ready"), sem("cq_taken"), sem("kv_taken")
        lora_squared, lora_mean, lora_root, lora_ready = (
            sem("lora_squared"), sem("lora_mean"), sem("lora_root"), sem("lora_ready"))
        prep_ready, prep_act, prep_dve = sem("prep_ready"), sem("prep_act"), sem("prep_dve")
        kr_roped, kr_spread, pooled = sem("kr_roped"), sem("kr_spread"), sem("pooled")
        scores_ready, max_ready, exp_ready, probs_ready = (
            sem("scores_ready"), sem("max_ready"), sem("exp_ready"), sem("probs_ready"))
        probsT_ready, probsT_taken = sem("probsT_ready"), sem("probsT_taken")
        pv_ready, pv_taken = sem("pv_ready"), sem("pv_taken")
        pool_ready, pool_taken = sem("pool_ready"), sem("pool_taken")
        proj_ready, residual = sem("proj_ready"), sem("residual")
        up_ready, gate_ready, hidden_ready, down_done = (
            sem("up_ready"), sem("gate_ready"), sem("hidden_ready"), sem("down_done"))
        spec_ready, spec_act, spec_dve = sem("spec_ready"), sem("spec_act"), sem("spec_dve")
        four_ready, four_act, four_dve = sem("four_ready"), sem("four_act"), sem("four_dve")
        logits_ready, tok_ready, tok_act, tok_dve = (
            sem("logits_ready"), sem("tok_ready"), sem("tok_act"), sem("tok_dve"))
        gap_ready, odds_ready, mask_ready, rank_ready, loops_ready = (
            sem("gap_ready"), sem("odds_ready"), sem("mask_ready"), sem("rank_ready"), sem("loops_ready"))
        pick_ready, gathered, h_exp_act, h_exp_dve = (
            sem("pick_ready"), sem("gathered"), sem("h_exp_act"), sem("h_exp_dve"))
        e_up, e_gate, e_hidden, e_down = sem("e_up"), sem("e_gate"), sem("e_hidden"), sem("e_down")
        y_ready, yT_taken, y_turned, y_taken = sem("y_ready"), sem("yT_taken"), sem("y_turned"), sem("y_taken")
        gated_ready, spread_turned, spread_taken = (
            sem("gated_ready"), sem("spread_turned"), sem("spread_taken"))
        part_ready, part_added = sem("part_ready"), sem("part_added")
        dve_step, pool_step = sem("dve_step"), sem("pool_step")
        out_ready, stored = sem("out_ready"), sem("stored")

        units, first_unit = [], {}

        def add(name, src, cols):
            first_unit.setdefault(name, len(units))
            units.append((src, cols))

        def add_ada(layer, lo, hi):
            for u in range(lo, hi):
                add(f"ada{layer}_{u}", ada_d[layer, u], SLOT)

        add_ada(0, 0, 3)
        add("mixa", mixa_d, KD * 512)
        add("mixb", mixb_d, KD * 416)
        add_ada(0, 3, ADA_UNITS)
        for n in range(2):
            add("mixout", mixout_d[n], KD * 512)
        add_ada(1, 0, 5)
        for g in range(GROUPS_DENSE):
            add("ffn", ffn_d[g], SLOT)
        add_ada(1, 5, ADA_UNITS)
        add("dft", dft_d, 4 * 512)
        for n in range(2):
            add("fnet", fnet_d[n], KD * 512)
        stream_uses = [len(range(s, len(units), STREAM_SLOTS)) for s in range(STREAM_SLOTS)]

        def unit_slot(n):
            return n % STREAM_SLOTS

        def unit_wait(eng, n):
            eng.wait_ge(slot_in[unit_slot(n)], 16 * (n // STREAM_SLOTS + 1))

        def slot_base(s):
            return 16 * stream_uses[s] if s < STREAM_SLOTS else 0

        ADA_PARTS = [(0, 0, 3, 7), (0, 3, 8, 6), (1, 0, 3, 7), (1, 3, 5, 6), (1, 5, 8, 0)]

        PREP = [("kr", 0)] + [("q", p) for p in range(4)] + [("k", p) for p in range(4)] \
            + [("rot", p) for p in range(4)] + [("v", p) for p in range(4)]
        PREP_BY = ["act" if kind in ("q", "k") else "dve" for kind, _ in PREP]
        NPREP = 6

        def prep_taken(eng, n):
            s = prep_act if PREP_BY[n] == "act" else prep_dve
            eng.wait_ge(s, sum(b == PREP_BY[n] for b in PREP_BY[:n + 1]))

        ITEMS = [(hd, q) for hd in range(HEADS) for q in range(2)]

        block = ctx.enter_context(nc.Block())

        @block.sync
        def _(sp):
            for n, (src, cols) in enumerate(units):
                s = unit_slot(n)
                if n >= STREAM_SLOTS:
                    sp.wait_ge(slot_free[s], n // STREAM_SLOTS)
                sp.dma_start(ring[:, s * SLOT:s * SLOT + cols], src).then_inc(slot_in[s], 16)

            def expert_loads(e, i):
                for g in range(GROUPS):
                    s = g % SLOTS
                    if not isinstance(i, int):
                        sp.wait_ge(e_down, GROUPS * i + (g - SLOTS + 1))
                    elif g >= SLOTS:
                        sp.wait_ge(e_down, g - SLOTS + 1)
                    elif s < STREAM_SLOTS:
                        sp.wait_ge(slot_free[s], stream_uses[s])
                    elif s == STREAM_SLOTS:
                        sp.wait_ge(scratch_free, 1)
                    sp.dma_start(ring[:, s * SLOT:(s + 1) * SLOT], moe_d[e, g]).then_inc(slot_in[s], 16)

            expert_loads(0, 0)
            with sp.Fori(1, EXPERTS) as e:
                expert_loads(e, e)
            sp.wait_ge(loops_ready, 1)
            rounds = sp.value_load(loops[0:1, 1:2], min_val=1, max_val=MAX_ROUNDS)
            with sp.If(rounds > 1):
                with sp.Fori(1, rounds) as r:
                    with sp.Fori(0, EXPERTS) as e:
                        expert_loads(e, EXPERTS * r + e)
            sp.wait_ge(out_ready, KD)
            sp.dma_start(out_d, view(ring, scratch + 4096, KD * T)).then_inc(stored, 16)
            sp.wait_ge(stored, 16)

        @block.gpsimd
        def _(pool):
            n_step = [0]

            def link(ins):
                n_step[0] += 1
                ins.then_inc(pool_step, 1)
                pool.wait_ge(pool_step, n_step[0])

            nc.gpsimd.memset(pool0[:, :, 0:PAD], 0.0).then_inc(pads_zero, 1)
            nc.gpsimd.memset(pool0[:, :, PAD + T:], 0.0).then_inc(pads_zero, 1)
            pool.wait_ge(pads_zero, 2)
            pool.wait_ge(mixa_taken, 2)
            pool.wait_ge(count_in, 16)
            n2, n4, n8, n16 = PADDED - 1, PADDED - 3, PADDED - 7, PADDED - 15
            link(nc.gpsimd.tensor_tensor(pool1[:, :, 0:n2], pool0[:, :, 0:n2], pool0[:, :, 1:1 + n2], ALU.add))
            link(nc.gpsimd.tensor_tensor(pool2[:, 1:, 0:n4], pool1[:, 1:, 0:n4], pool1[:, 1:, 2:2 + n4], ALU.add))
            link(nc.gpsimd.tensor_tensor(pool1[:, 2:, 0:n8], pool2[:, 2:, 0:n8], pool2[:, 2:, 4:4 + n8], ALU.add))
            link(nc.gpsimd.tensor_tensor(pool2[:, 3:, 0:n16], pool1[:, 3:, 0:n16], pool1[:, 3:, 8:8 + n16], ALU.add))
            for g, w in enumerate(WINDOWS):
                at = (pool1 if g % 2 == 0 else pool2)[:, g, PAD - w // 2:PAD - w // 2 + T]
                link(nc.gpsimd.tensor_tensor(at, at, invcount[:, g, :], ALU.mult))
                nc.gpsimd.tensor_tensor(at, at, pool0[:, g, PAD:PAD + T], ALU.subtract).then_inc(pooled, 1)
            pool.wait_ge(pooled, NG)
            pool.wait_ge(kr_roped, 1)
            for hd in range(HEADS):
                nc.gpsimd.tensor_copy(keys[NOPE:QK, hd, :], krT[NOPE:QK, :]).then_inc(kr_spread, 1)
                pool.wait_ge(kr_spread, hd + 1)

        @block.scalar
        def _(act):
            act.dma_start(vec[:, :], vec_d).then_inc(vec_in, 16)
            act.dma_start(xT[:, :], x_d).then_inc(x_in, 16)
            act.dma_start(ctxT, ctx_d).then_inc(ctx_in, 16)
            act.dma_start(con[:, :], con_d).then_inc(con_in, 16)
            act.dma_start(work[:, 0:3072], attn_d).then_inc(attn_in, 16)
            act.dma_start(work[NOPE:QK, 5376:5888], rope_d).then_inc(rope_in, 16)
            act.dma_start(view(ring, scratch + 17024, NG * T), invcount_d).then_inc(count_in, 16)
            act.dma_start(view(work, 6144, KD * EXPERTS), router_d).then_inc(router_in, 16)

            act.wait_ge(vec_in, 16)
            nc.scalar.activation(view(small, 0, 16), V("cond"), ACT.Silu).then_inc(cond_ready, 1)
            act.wait_ge(x_in, 16)
            nc.scalar.activation(square[:, :, 0:T], x, ACT.Square).then_inc(squared, 1)
            act.wait_ge(ctx_in, 16)
            nc.scalar.activation(square[:, :, T:TA], ctxT, ACT.Square).then_inc(squared, 1)
            act.wait_ge(con_in, 16)

            def root(stage, source):
                act.wait_ge(mean_ready, stage + 1)
                nc.scalar.activation(rstd[:, 0:source.shape[-1]], source, ACT.Sqrt, bias=C("eps")).then_inc(root_ready, 1)

            def shifts(done, target, halves):
                for k in range(KD):
                    for n, (lo, shift) in enumerate(halves):
                        act.wait_ge(scaled, done + k * len(halves) + n + 1)
                        nc.scalar.activation(target[:, k, lo:lo + T], target[:, k, lo:lo + T], ACT.Identity,
                                             bias=shift(k)).then_inc(h_ready, 1)

            def adac(layer, part, k, who=0):
                at = 96 * layer + 2 * (KD * part + k) + who
                return ada[:, at:at + 1]

            root(0, bank[0][:, :])
            act.wait_ge(ada_taken, 1)
            shifts(0, h_all, [(0, lambda k: adac(0, 0, k)), (T, lambda k: adac(0, 0, k, 1))])
            act.wait_ge(pads_zero, 2)
            for n in range(2):
                act.wait_ge(mixa_ready, n + 1)
                nc.scalar.activation(pool0[:, 2 * n:2 * n + 2, PAD:PAD + T],
                                     bank[1 + n][:, :].rearrange("p (a b) -> p a b", a=2), ACT.Copy).then_inc(mixa_taken, 1)
            act.wait_ge(mixb_ready, 2)
            nc.scalar.activation(lora_sq[:, 0, :], bank[3][:, :], ACT.Square).then_inc(lora_squared, 1)
            nc.scalar.activation(lora_sq[:, 1, :], bank[4][:, :], ACT.Square).then_inc(lora_squared, 1)
            act.wait_ge(lora_mean, 2)
            nc.scalar.activation(rstd[:, 0:T], bank[0][:, 0:T], ACT.Sqrt, bias=C("eps"),
                                 scale=float(D) / Q_LORA).then_inc(lora_root, 1)
            nc.scalar.activation(lora_sq[:, 1, :], bank[1][:, :], ACT.Sqrt, bias=C("eps"),
                                 scale=float(D) / KV_LORA).then_inc(lora_root, 1)
            for n, (kind, p) in enumerate(PREP):
                if PREP_BY[n] != "act":
                    continue
                act.wait_ge(prep_ready, n + 1)
                b = bank[n % NPREP]
                if kind == "q":
                    nc.scalar.activation(queries[0:QK, 2 * p:2 * p + 2, :],
                                         b[0:QK, :].rearrange("p (a b) -> p a b", a=2), ACT.Copy).then_inc(prep_act, 1)
                else:
                    nc.scalar.activation(keys[0:NOPE, 2 * p, :], b[0:NOPE, :], ACT.Copy)
                    nc.scalar.activation(keys[0:NOPE, 2 * p + 1, :], b[NOPE:P, :], ACT.Copy).then_inc(prep_act, 1)

            def turn_probs(n):
                hd, q = ITEMS[n]
                act.wait_ge(probsT_ready, n + 1)
                if hd >= 2:
                    act.wait_ge(pv_ready, hd - 1)
                nc.scalar.activation(probsT[:, hd % 2, :, q * P:(q + 1) * P],
                                     bank[3 + n % 2][:, :].rearrange("p (a b) -> p a b", a=4), ACT.Copy).then_inc(probsT_taken, 1)

            for n in range(len(ITEMS)):
                act.wait_ge(max_ready, n + 1)
                if n >= 4:
                    act.wait_ge(probsT_ready, n - 3)
                nc.scalar.activation(probs[:, n % 4, :], bank[n % 3][:, :], ACT.Exp, bias=small[:, 32 + n:33 + n],
                                     scale=SCALE, accum_out=small[:, 48 + n:49 + n]).then_inc(exp_ready, 1)
                if n >= 3:
                    turn_probs(n - 3)
            for n in range(len(ITEMS) - 3, len(ITEMS)):
                turn_probs(n)
            for g in range(NG):
                act.wait_ge(pool_ready, g // 2 + 1)
                nc.scalar.activation(mixed[:, NG + g, :], bank[6 + g // 2][:, (g % 2) * T:(g % 2) * T + T], ACT.Copy,
                                     scale=V("pool_scale")[:, g:g + 1]).then_inc(pool_taken, 1)

            def squares(stage, need):
                act.wait_ge(residual, need)
                nc.scalar.activation(square_l, x, ACT.Square).then_inc(squared, 1)

            squares(1, KD)
            root(1, bank[4][:, 0:T])
            act.wait_ge(ada_taken, 2)
            shifts(16, h, [(0, lambda k: adac(0, 3, k))])
            for g in range(GROUPS_DENSE):
                act.wait_ge(up_ready, g + 1)
                if g >= 2:
                    act.wait_ge(hidden_ready, g - 1)
                nc.scalar.activation(gate_tmp[:, g % 2], bank[2 * (g % 2)][:, :].rearrange("p (a b) -> p a b", a=2),
                                     ACT.Silu).then_inc(gate_ready, 1)
            squares(2, 2 * KD)
            root(2, bank[1][:, 0:T])
            act.wait_ge(ada_taken, 3)
            shifts(24, h, [(0, lambda k: adac(1, 0, k))])
            for f in range(0, 8, 2):
                act.wait_ge(spec_ready, f + 1)
                nc.scalar.activation(spectrum[:, f // NG, f % NG, :], bank[2 + f % 4][:, :], ACT.Copy).then_inc(spec_act, 1)
            for f in (0, 2):
                act.wait_ge(four_ready, f + 1)
                nc.scalar.activation(fourier[:, 2 * f:2 * f + 2, :],
                                     bank[(6, 7, 0, 1)[f]][:, :].rearrange("p (a b) -> p a b", a=2), ACT.Copy).then_inc(four_act, 1)
            squares(3, 3 * KD)
            root(3, bank[6][:, 0:T])
            act.wait_ge(ada_taken, 5)
            shifts(32, h, [(0, lambda k: adac(1, 3, k))])
            for f in (0, 2):
                act.wait_ge(tok_ready, f + 1)
                nc.scalar.activation(h_tok[:, f // 2, (f % 2) * 512:(f % 2) * 512 + 512], bank[f][:, :], ACT.Copy).then_inc(tok_act, 1)
            for t in range(2):
                act.wait_ge(gap_ready, t + 1)
                nc.scalar.activation(small[:, 66 + t:67 + t], small[:, 64 + t:65 + t], ACT.Exp).then_inc(odds_ready, 1)

            def take_gathered(i):
                act.wait_ge(gathered, i + 1)
                nc.scalar.activation(h_exp[:, 0:4, :], bank[4][:, 0:4 * CAP].rearrange("p (a b) -> p a b", a=4),
                                     ACT.Copy).then_inc(h_exp_act, 1)

            def expert(i):
                first = isinstance(i, int)
                for g in range(GROUPS):
                    act.wait_ge(e_up, GROUPS * i + (g + 1))
                    if not (first and g < 2):
                        act.wait_ge(e_hidden, GROUPS * i + (g - 1))
                    nc.scalar.activation(gate_e[:, g % 2], bank[g % 2][:, 0:2 * CAP].rearrange("p (a b) -> p a b", a=2),
                                         ACT.Silu).then_inc(e_gate, 1)
                    if g == 6:
                        act.wait_ge(spread_turned, i + 1)
                        nc.scalar.activation(spread, bank[6][0:CAP, 0:T], ACT.Copy).then_inc(spread_taken, 1)
                take_gathered(i + 1)
                act.wait_ge(y_ready, i + 1)
                for b in range(2):
                    ins = nc.scalar.activation(yT[:, 4 * b:4 * b + 4, :],
                                               bank[2 + b][:, 0:4 * CAP].rearrange("p (a b) -> p a b", a=4), ACT.Copy)
                ins.then_inc(yT_taken, 1)

            take_gathered(0)
            expert(0)
            turns = act.value_load(loops[0:1, 0:1], min_val=EXPERTS, max_val=EXPERTS * MAX_ROUNDS)
            with act.Fori(1, turns) as i:
                expert(i)
            act.wait_ge(part_added, KD * turns)
            nc.scalar.activation(square_l, x, ACT.Square).then_inc(squared, 1)
            root(4, bank[0][:, 0:T])

        @block.vector
        def _(dve):
            n_step = [0]

            def link(ins):
                n_step[0] += 1
                ins.then_inc(dve_step, 1)
                dve.wait_ge(dve_step, n_step[0])

            def modulation(slot, name, lo, layer, part, who=0):
                at = 96 * layer + 2 * KD * part + who
                scale = ada[:, at:at + 2 * KD - who].rearrange("p (a b) -> p a b", b=2)[:, :, 0] if who == 0 else \
                    ada[:, at - 1:at - 1 + 2 * KD].rearrange("p (a b) -> p a b", b=2)[:, :, 1]
                link(nc.vector.scalar_tensor_tensor(out=moda[:, slot * KD:(slot + 1) * KD], in0=scale, scalar=1.0,
                                                    in1=V(name)[:, lo:lo + KD], op0=ALU.add, op1=ALU.mult))

            def take_ada(part):
                layer, lo, hi, b = ADA_PARTS[part]
                a, z = 2 * ADA_CHUNKS * lo, 2 * ADA_CHUNKS * hi
                dve.wait_ge(ada_ready, part + 1)
                bias = V("ada_b")[:, 48 * layer + a // 2:48 * layer + z // 2]
                for who in range(2):
                    out = ada[:, 96 * layer + a:96 * layer + z].rearrange("p (a b) -> p a b", b=2)[:, :, who]
                    src = bank[b][:, a:z].rearrange("p (a b) -> p a b", b=2)[:, :, who]
                    ins = nc.vector.tensor_tensor(out, src, bias, ALU.add)
                ins.then_inc(ada_taken, 1)
                dve.wait_ge(ada_taken, part + 1)

            def reciprocal(stage, n):
                dve.wait_ge(root_ready, stage + 1)
                link(nc.vector.reciprocal(rstd[:, 0:n], rstd[:, 0:n]))

            def scale(source, target, slot, lo=0):
                for k in range(KD):
                    nc.vector.scalar_tensor_tensor(out=target[:, k, lo:lo + T], in0=source[:, k, :],
                                                   scalar=moda[:, slot * KD + k:slot * KD + k + 1],
                                                   in1=rstd[:, lo:lo + T], op0=ALU.mult, op1=ALU.mult).then_inc(scaled, 1)

            def add_projected(n, src, layer, part):
                for k in range(KD):
                    if k % 2 == 0 and n is not None:
                        dve.wait_ge(proj_ready, 4 * n + k // 2 + 1)
                    at = 96 * layer + 2 * (KD * part + k)
                    nc.vector.scalar_tensor_tensor(out=x[:, k, :], in0=bank[src + k // 2][:, (k % 2) * T:(k % 2) * T + T],
                                                   scalar=ada[:, at:at + 1], in1=x[:, k, :],
                                                   op0=ALU.mult, op1=ALU.add).then_inc(residual, 1)

            dve.wait_ge(vec_in, 16)
            take_ada(0)
            modulation(0, "mix_g", 0, 0, 1)
            modulation(1, "mix_g", 0, 0, 1, who=1)
            reciprocal(0, TA)
            for k in range(KD):
                for n, source in enumerate((x, ctxT)):
                    nc.vector.scalar_tensor_tensor(out=h_all[:, k, n * T:(n + 1) * T], in0=source[:, k, :],
                                                   scalar=moda[:, n * KD + k:n * KD + k + 1],
                                                   in1=rstd[:, n * T:(n + 1) * T], op0=ALU.mult, op1=ALU.mult).then_inc(scaled, 1)
            dve.wait_ge(mixb_ready, 3)
            dve.wait_ge(lora_squared, 2)
            nc.vector.tensor_copy(cqT, bank[3][:, :].rearrange("p (a b) -> p a b", a=2)).then_inc(cq_taken, 1)
            nc.vector.tensor_copy(ckvT, bank[4][:, :]).then_inc(kv_taken, 1)
            nc.vector.tensor_copy(krT[0:QK, :], bank[5][0:QK, :]).then_inc(kv_taken, 1)
            dve.wait_ge(cq_taken, 1)
            dve.wait_ge(kv_taken, 2)
            dve.wait_ge(lora_root, 2)
            link(nc.vector.reciprocal(rstd[:, 0:T], rstd[:, 0:T]))
            for k in range(2):
                nc.vector.scalar_tensor_tensor(out=cqT[:, k, :], in0=cqT[:, k, :], scalar=V("cq_g")[:, k:k + 1],
                                               in1=rstd[:, 0:T], op0=ALU.mult, op1=ALU.mult).then_inc(lora_ready, 1)
            link(nc.vector.reciprocal(lora_sq[:, 1, :], lora_sq[:, 1, :]))
            nc.vector.scalar_tensor_tensor(out=ckvT, in0=ckvT, scalar=V("ckv_g"), in1=lora_sq[:, 1, :],
                                           op0=ALU.mult, op1=ALU.mult).then_inc(lora_ready, 1)
            take_ada(1)
            modulation(2, "ffn_g", 0, 0, 4)
            dve.wait_ge(rope_in, 16)

            def roped(target, turned, tmp, cols):
                r = slice(NOPE, QK)
                cos, sin = rope[r, 0, :], rope[r, 1, :]
                for c in range(cols):
                    last = nc.vector.tensor_tensor(tmp[r, c * T:(c + 1) * T], turned[r, c * T:(c + 1) * T], sin, ALU.mult)
                for c in range(cols):
                    last = nc.vector.tensor_tensor(target(c), target(c), cos, ALU.mult)
                link(last)
                for c in range(cols):
                    last = nc.vector.tensor_tensor(target(c), target(c), tmp[r, c * T:(c + 1) * T], ALU.add)
                return last

            for n, (kind, p) in enumerate(PREP):
                if PREP_BY[n] != "dve":
                    continue
                dve.wait_ge(prep_ready, n + 1)
                b = bank[n % NPREP]
                if kind == "kr":
                    ins = roped(lambda c: krT[NOPE:QK, 0:T], b, rope_tmp, 1)
                    ins.then_inc(kr_roped, 1)
                    dve.wait_ge(kr_roped, 1)
                    nc.vector.memset(small[:, 30:31], 0.0).then_inc(prep_dve, 1)
                elif kind == "rot":
                    roped(lambda c: queries[NOPE:QK, 2 * p + c, :], b, rope_tmp, 2).then_inc(prep_dve, 1)
                    dve.wait_ge(prep_dve, PREP_BY[:n + 1].count("dve"))
                else:
                    nc.vector.tensor_copy(values[:, p, :], b[:, :]).then_inc(prep_dve, 1)

            def attended(hd):
                dve.wait_ge(pv_ready, hd + 1)
                lo = (hd % 2) * VD
                nc.vector.tensor_copy(mixed[lo:lo + VD, hd // 2, :], bank[5][lo:lo + VD, 0:T]).then_inc(pv_taken, 1)

            def normalised(n):
                dve.wait_ge(exp_ready, n + 1)
                link(nc.vector.reciprocal(small[:, 48 + n:49 + n], small[:, 48 + n:49 + n]))
                nc.vector.tensor_scalar(probs[:, n % 4, :], probs[:, n % 4, :], small[:, 48 + n:49 + n], None,
                                        ALU.mult).then_inc(probs_ready, 1)

            for n in range(len(ITEMS)):
                dve.wait_ge(scores_ready, n + 1)
                link(nc.vector.tensor_reduce(small[:, 32 + n:33 + n], bank[n % 3][:, :], AX_X, ALU.max))
                nc.vector.tensor_scalar(small[:, 32 + n:33 + n], small[:, 32 + n:33 + n], -SCALE, None,
                                        ALU.mult).then_inc(max_ready, 1)
                if n >= 1:
                    normalised(n - 1)
                if n >= 7 and n % 2:
                    attended((n - 7) // 2)
            normalised(len(ITEMS) - 1)
            for hd in range(5, HEADS):
                attended(hd)
            add_projected(0, 0, 0, 2)
            reciprocal(1, T)
            scale(x, h, 2)
            take_ada(2)
            modulation(3, "mix_g", KD, 1, 1)
            take_ada(3)

            for g in range(GROUPS_DENSE):
                dve.wait_ge(gate_ready, g + 1)
                if g >= 2:
                    dve.wait_ge(down_done, g - 1)
                nc.vector.tensor_tensor(hidden[:, g % 2], gate_tmp[:, g % 2],
                                        bank[2 * (g % 2) + 1][:, :].rearrange("p (a b) -> p a b", a=2),
                                        ALU.mult).then_inc(hidden_ready, 1)
            dve.wait_ge(down_done, GROUPS_DENSE)
            add_projected(None, 4, 0, 5)
            reciprocal(2, T)
            scale(x, h, 3)
            take_ada(4)
            modulation(4, "ffn_g", KD, 1, 4)
            for f in range(1, 8, 2):
                dve.wait_ge(spec_ready, f + 1)
                nc.vector.tensor_copy(spectrum[:, f // NG, f % NG, :], bank[2 + f % 4][:, :]).then_inc(spec_dve, 1)
            for f in (1, 3):
                dve.wait_ge(four_ready, f + 1)
                nc.vector.tensor_copy(fourier[:, 2 * f:2 * f + 2, :],
                                      bank[(6, 7, 0, 1)[f]][:, :].rearrange("p (a b) -> p a b", a=2)).then_inc(four_dve, 1)
            add_projected(1, 2, 1, 2)
            reciprocal(3, T)
            scale(x, h, 4)
            for f in (1, 3):
                dve.wait_ge(tok_ready, f + 1)
                nc.vector.tensor_copy(h_tok[:, f // 2, 512:1024], bank[f][:, :]).then_inc(tok_dve, 1)

            dve.wait_ge(logits_ready, 1)

            def cols(at, n):
                return small[:, at:at + n]

            for t in range(2):
                logit, best, key, hot1, hot2 = (cols(72 + 56 * t + 8 * j, 8) for j in range(5))
                top1, top2, kmin = (cols(72 + 56 * t + 40 + j, 1) for j in range(3))
                link(nc.vector.tensor_copy(logit, bank[4][:, 8 * t:8 * t + 8]))
                for hot, top in ((hot1, top1), (hot2, top2)):
                    link(nc.vector.tensor_reduce(top, logit, AX_X, ALU.max))
                    link(nc.vector.tensor_scalar(best, logit, top, None, ALU.is_equal))
                    link(nc.vector.scalar_tensor_tensor(out=key, in0=best, scalar=-64.0, in1=C("iota8"),
                                                        op0=ALU.mult, op1=ALU.add))
                    link(nc.vector.tensor_reduce(kmin, key, AX_X, ALU.min))
                    link(nc.vector.tensor_scalar(hot, key, kmin, None, ALU.is_equal))
                    if hot is hot1:
                        link(nc.vector.scalar_tensor_tensor(out=logit, in0=hot, scalar=-3e38, in1=logit,
                                                            op0=ALU.mult, op1=ALU.add))
                nc.vector.tensor_tensor(cols(184 + 8 * t, 8), hot1, hot2, ALU.add).then_inc(mask_ready, 1)
                nc.vector.tensor_tensor(cols(64 + t, 1), top2, top1, ALU.subtract).then_inc(gap_ready, 1)
            for t in range(2):
                _, best, key, hot1, hot2 = (cols(72 + 56 * t + 8 * j, 8) for j in range(5))
                odds, share1, share2 = cols(66 + t, 1), cols(72 + 56 * t + 43, 1), cols(72 + 56 * t + 44, 1)
                dve.wait_ge(odds_ready, t + 1)
                link(nc.vector.tensor_scalar(share1, odds, 1.0, None, ALU.add))
                link(nc.vector.reciprocal(share1, share1))
                link(nc.vector.tensor_tensor(share2, odds, share1, ALU.mult))
                link(nc.vector.tensor_scalar(best, hot1, share1, None, ALU.mult))
                link(nc.vector.scalar_tensor_tensor(out=best, in0=hot2, scalar=share2, in1=best,
                                                    op0=ALU.mult, op1=ALU.add))
                for r in range(MAX_ROUNDS + 1):
                    link(nc.vector.tensor_copy(gate_at[:, t, EXPERTS * r:EXPERTS * (r + 1)], best))
            dve.wait_ge(rank_ready, 1)
            for t in range(2):
                key = cols(72 + 56 * t + 16, 8)
                link(nc.vector.scalar_tensor_tensor(out=key, in0=bank[5][:, 8 * t:8 * t + 8], scalar=1.0,
                                                    in1=cols(184 + 8 * t, 8), op0=ALU.add, op1=ALU.mult))
                for r in range(MAX_ROUNDS + 1):
                    link(nc.vector.tensor_scalar(rank_at[:, t, EXPERTS * r:EXPERTS * (r + 1)], key,
                                                 -1.0 - CAP * r, None, ALU.add))
            full, more = cols(200, 1), cols(201, MAX_ROUNDS - 1)
            link(nc.vector.tensor_reduce(full, bank[5][:, 16:24], AX_X, ALU.max))
            for r in range(1, MAX_ROUNDS):
                link(nc.vector.tensor_scalar(cols(200 + r, 1), full, CAP * r + 0.5, None, ALU.is_gt))
            link(nc.vector.tensor_reduce(cols(210, 1), more, AX_X, ALU.add))
            link(nc.vector.tensor_scalar(cols(211, 1), cols(210, 1), float(EXPERTS), float(EXPERTS), ALU.mult, ALU.add))
            link(nc.vector.tensor_scalar(cols(212, 1), cols(210, 1), 1.0, None, ALU.add))
            link(nc.vector.tensor_copy(loops[:, :], cols(211, 2)))
            nc.vector.memset(small[:, 31:32], 0.0).then_inc(loops_ready, 1)

            def picks(i, target, sem_out, gated):
                for t in range(2):
                    if gated:
                        ins = nc.vector.tensor_scalar(target[:, t, :], C("iota"), rank_at[:, t, bass.ds(i, 1)],
                                                      gate_at[:, t, bass.ds(i, 1)], ALU.is_equal, ALU.mult)
                    else:
                        ins = nc.vector.tensor_scalar(target[:, t, :], C("iota"), rank_at[:, t, bass.ds(i, 1)], None,
                                                      ALU.is_equal)
                ins.then_inc(sem_out, 1)

            def take_gathered(i):
                dve.wait_ge(gathered, i + 1)
                nc.vector.tensor_copy(h_exp[:, 4:8, :], bank[5][:, 0:4 * CAP].rearrange("p (a b) -> p a b", a=4))\
                    .then_inc(h_exp_dve, 1)

            def take_turned(i):
                dve.wait_ge(y_turned, i + 1)
                for b in range(2):
                    ins = nc.vector.tensor_copy(y_tok[:, 512 * b:512 * b + 512], bank[4 + b][0:CAP, :])
                ins.then_inc(y_taken, 1)

            def add_part(i, half):
                for j in range(4):
                    k = 4 * half + j
                    if j % 2 == 0 and i is not None:
                        dve.wait_ge(part_ready, 4 * i + (k // 2 + 1))
                    b = (6, 7, 4, 5)[k // 2]
                    at = 96 + 2 * (KD * 5 + k)
                    nc.vector.scalar_tensor_tensor(out=x[:, k, :], in0=bank[b][:, (k % 2) * T:(k % 2) * T + T],
                                                   scalar=ada[:, at:at + 1], in1=x[:, k, :],
                                                   op0=ALU.mult, op1=ALU.add).then_inc(part_added, 1)

            def expert(i):
                first = isinstance(i, int)
                for g in range(GROUPS):
                    dve.wait_ge(e_gate, GROUPS * i + (g + 1))
                    if not (first and g < 2):
                        dve.wait_ge(e_down, GROUPS * i + (g - 1))
                    nc.vector.tensor_tensor(hidden_e[:, g % 2], gate_e[:, g % 2],
                                            bank[g % 2][:, 2 * CAP:4 * CAP].rearrange("p (a b) -> p a b", a=2),
                                            ALU.mult).then_inc(e_hidden, 1)
                    if not first:
                        if g == 2:
                            take_turned(i - 1)
                        if g in (3, 4):
                            add_part(i - 1, g - 3)
                    if g == 5:
                        picks(i, pick_gated, gated_ready, True)
                    if g == 7:
                        picks(i + 1, pick, pick_ready, False)
                take_gathered(i + 1)

            picks(0, pick, pick_ready, False)
            take_gathered(0)
            expert(0)
            turns = dve.value_load(loops[0:1, 0:1], min_val=EXPERTS, max_val=EXPERTS * MAX_ROUNDS)
            with dve.Fori(1, turns) as i:
                expert(i)
            take_turned(turns - 1)
            dve.wait_ge(part_ready, 4 * turns)
            for half in range(2):
                add_part(None, half)
            reciprocal(4, T)
            o = view(ring, scratch + 4096, KD, T)
            for k in range(KD):
                nc.vector.scalar_tensor_tensor(out=o[:, k, :], in0=x[:, k, :], scalar=V("final_g")[:, k:k + 1],
                                               in1=rstd[:, 0:T], op0=ALU.mult, op1=ALU.mult).then_inc(out_ready, 1)

        @block.tensor
        def _(pe):
            mm = nc.tensor.matmul

            def unit(n, cols):
                s = unit_slot(n)
                return view(ring, s * SLOT, KD, cols)

            def ada_part(part):
                layer, lo, hi, b = ADA_PARTS[part]
                for u in range(lo, hi):
                    n = first_unit[f"ada{layer}_{u}"]
                    unit_wait(pe, n)
                    w = unit(n, ADA_COLS)
                    for j in range(ADA_CHUNKS):
                        at = 2 * (u * ADA_CHUNKS + j)
                        for k in range(KD):
                            last = mm(bank[b][:, at:at + 2], w[:, k, j * P:(j + 1) * P], cond[:, k, :],
                                      start=(k == 0), stop=(k == KD - 1))
                    last.then_inc(slot_free[unit_slot(n)], 1)
                pe.wait_ge(slot_free[unit_slot(n)], n // STREAM_SLOTS + 1)
                pe.nop().then_inc(ada_ready, 1)

            def mean(stage, n_squares, source, out):
                pe.wait_ge(squared, n_squares)
                for k in range(KD):
                    last = mm(out, C("mean"), source[:, k, :], start=(k == 0), stop=(k == KD - 1))
                last.then_inc(mean_ready, 1)

            def project(name, source, base, ready_sem):
                for n in range(2):
                    u = first_unit[name] + n
                    unit_wait(pe, u)
                    w = unit(u, 512)
                    for j in range(4):
                        c = 4 * n + j
                        for k in range(KD):
                            last = mm(bank[base + c // 2][:, (c % 2) * T:(c % 2) * T + T], w[:, k, j * P:(j + 1) * P],
                                      source[:, k, :], start=(k == 0), stop=(k == KD - 1))
                        if c % 2:
                            last.then_inc(ready_sem, 1)
                    pe.wait_ge(ready_sem, 0 + ready_count[0] + 2)
                    ready_count[0] += 2
                    pe.nop().then_inc(slot_free[unit_slot(u)], 1)

            ready_count = [0]

            pe.wait_ge(con_in, 16)
            mean(0, 2, square, bank[0][:, :])
            pe.wait_ge(cond_ready, 1)
            ada_part(0)
            pe.wait_ge(h_ready, 16)
            u = first_unit["mixa"]
            unit_wait(pe, u)
            w = unit(u, 512)
            for c in range(4):
                for k in range(KD):
                    last = mm(bank[1 + c // 2][:, (c % 2) * T:(c % 2) * T + T], w[:, k, c * P:(c + 1) * P],
                              h_all[:, k, 0:T], start=(k == 0), stop=(k == KD - 1))
                if c % 2:
                    last.then_inc(mixa_ready, 1)
            pe.wait_ge(mixa_ready, 2)
            pe.nop().then_inc(slot_free[unit_slot(u)], 1)
            u = first_unit["mixb"]
            unit_wait(pe, u)
            w = unit(u, 416)
            for c in range(2):
                for k in range(KD):
                    last = mm(bank[3][:, c * T:c * T + T], w[:, k, c * P:(c + 1) * P], h_all[:, k, 0:T],
                              start=(k == 0), stop=(k == KD - 1))
            last.then_inc(mixb_ready, 1)
            for k in range(KD):
                last = mm(bank[4][:, :], w[:, k, 256:384], h_all[:, k, :], start=(k == 0), stop=(k == KD - 1))
            last.then_inc(mixb_ready, 1)
            for k in range(KD):
                last = mm(bank[5][0:QK, :], w[:, k, 320:416], h_all[:, k, :], start=(k == 0), stop=(k == KD - 1))
            last.then_inc(mixb_ready, 1)
            pe.wait_ge(mixb_ready, 3)
            pe.nop().then_inc(slot_free[unit_slot(u)], 1)
            pe.wait_ge(lora_squared, 2)
            for k in range(2):
                last = mm(bank[0][:, 0:T], C("mean"), lora_sq[:, 0, k * T:(k + 1) * T], start=(k == 0), stop=(k == 1))
            last.then_inc(lora_mean, 1)
            pe.wait_ge(mixa_taken, 2)
            mm(bank[1][:, :], C("mean"), lora_sq[:, 1, :], start=True, stop=True).then_inc(lora_mean, 1)
            ada_part(1)
            pe.wait_ge(attn_in, 16)
            pe.wait_ge(lora_ready, 3)
            pe.wait_ge(kv_taken, 2)
            for n, (kind, p) in enumerate(PREP):
                b = bank[n % NPREP]
                if n >= NPREP:
                    prep_taken(pe, n - NPREP)
                if kind == "kr":
                    last = mm(b[0:QK, 0:T], C("rot")[0:QK, :], krT[0:QK, 0:T], start=True, stop=True)
                elif kind == "q":
                    for j in range(2):
                        hd = 2 * p + j
                        for k in range(2):
                            last = mm(b[0:QK, j * T:(j + 1) * T], w_uq[:, k, hd * QK:(hd + 1) * QK], cqT[:, k, :],
                                      start=(k == 0), stop=(k == 1))
                elif kind == "k":
                    last = mm(b[:, :], w_ukv[:, 0, p * P:(p + 1) * P], ckvT, start=True, stop=True)
                elif kind == "rot":
                    if p == 0:
                        pe.wait_ge(prep_act, 4)
                    last = mm(b[0:QK, :], C("rot")[0:QK, :], queries[0:QK, 2 * p:2 * p + 2, :], start=True, stop=True)
                else:
                    last = mm(b[:, :], ckvT[:, p * P:(p + 1) * P], w_ukv[:, 1, :], start=True, stop=True)
                last.then_inc(prep_ready, 1)

            pe.wait_ge(prep_act, PREP_BY.count("act"))
            pe.wait_ge(prep_dve, PREP_BY.count("dve"))
            pe.wait_ge(kr_spread, HEADS)

            def turn(n):
                pe.wait_ge(probs_ready, n + 1)
                if n >= 2:
                    pe.wait_ge(probsT_taken, n - 1)
                for kt in range(4):
                    last = nc.tensor.transpose(bank[3 + n % 2][:, kt * P:(kt + 1) * P],
                                               probs[:, n % 4, kt * P:(kt + 1) * P], C("ident"))
                last.then_inc(probsT_ready, 1)

            def attend(hd):
                pe.wait_ge(probsT_taken, 2 * hd + 2)
                if hd >= 1:
                    pe.wait_ge(pv_taken, hd)
                lo = (hd % 2) * VD
                for kt in range(4):
                    last = mm(bank[5][lo:lo + VD, 0:T], values[:, kt, hd * VD:(hd + 1) * VD], probsT[:, hd % 2, kt, :],
                              start=(kt == 0), stop=(kt == 3))
                last.then_inc(pv_ready, 1)

            for n, (hd, q) in enumerate(ITEMS):
                if n >= 3:
                    pe.wait_ge(exp_ready, n - 2)
                mm(bank[n % 3][:, :], queries[0:QK, hd, q * P:(q + 1) * P], keys[0:QK, hd, :],
                   start=True, stop=True).then_inc(scores_ready, 1)
                if n >= 2:
                    turn(n - 2)
                if n >= 5 and n % 2:
                    attend((n - 5) // 2)
            for n in range(len(ITEMS) - 2, len(ITEMS)):
                turn(n)
            attend(HEADS - 2)
            attend(HEADS - 1)
            pe.wait_ge(pooled, NG)
            pe.wait_ge(ada_taken, 2)
            for g, wnd in enumerate(WINDOWS):
                src = (pool1 if g % 2 == 0 else pool2)[:, g, PAD - wnd // 2:PAD - wnd // 2 + T]
                last = mm(bank[6 + g // 2][:, (g % 2) * T:(g % 2) * T + T], pool_w[:, g, :], src, start=True, stop=True)
                if g % 2:
                    last.then_inc(pool_ready, 1)
            pe.wait_ge(pool_taken, NG)
            pe.wait_ge(pv_taken, HEADS)
            project("mixout", mixed, 0, proj_ready)
            ada_part(2)
            mean(1, 3, square_l, bank[4][:, 0:T])
            ada_part(3)
            pe.wait_ge(h_ready, 24)
            pe.wait_ge(ada_taken, 4)

            def ffn_up(g):
                u = first_unit["ffn"] + g
                unit_wait(pe, u)
                if g >= 2:
                    pe.wait_ge(hidden_ready, g - 1)
                for v in range(2):
                    w = view(ring, unit_slot(u) * SLOT + v * KD * PAIR, KD, PAIR)
                    for j in range(2):
                        for k in range(KD):
                            last = mm(bank[2 * (g % 2) + v][:, j * T:(j + 1) * T], w[:, k, j * P:(j + 1) * P], h[:, k, :],
                                      start=(k == 0), stop=(k == KD - 1))
                last.then_inc(up_ready, 1)

            def ffn_down(g):
                u = first_unit["ffn"] + g
                pe.wait_ge(hidden_ready, g + 1)
                w = view(ring, unit_slot(u) * SLOT + 2 * KD * PAIR, 2, D)
                for j in range(2):
                    for k in range(KD):
                        last = mm(bank[4 + k // 2][:, (k % 2) * T:(k % 2) * T + T], w[:, j, k * P:(k + 1) * P],
                                  hidden[:, g % 2, j, :], start=(g == 0 and j == 0 and k % 2 == 0),
                                  stop=(g == GROUPS_DENSE - 1 and j == 1), skip_group_check=True)
                last.then_inc(down_done, 1)
                pe.wait_ge(down_done, g + 1)
                pe.nop().then_inc(slot_free[unit_slot(u)], 1)

            for g in range(GROUPS_DENSE):
                ffn_up(g)
                if g >= 1:
                    ffn_down(g - 1)
            ffn_down(GROUPS_DENSE - 1)
            ada_part(4)
            mean(2, 4, square_l, bank[1][:, 0:T])
            u = first_unit["dft"]
            unit_wait(pe, u)
            chan = view(ring, unit_slot(u) * SLOT, 2, 2 * GC)
            rows = view(ring, unit_slot(u) * SLOT + 4 * GC, 2, 2, T)
            pe.wait_ge(h_ready, 32)
            for f in range(8):
                t, g = f // NG, f % NG
                if f >= 4:
                    pe.wait_ge(spec_dve if f % 2 else spec_act, f // 2 - 1)
                for k in range(2):
                    last = mm(bank[2 + f % 4][:, :], h[:, 2 * g + k, t * P:(t + 1) * P], chan[:, k, :],
                              start=(k == 0), stop=(k == 1))
                last.then_inc(spec_ready, 1)
            pe.wait_ge(spec_act, 4)
            pe.wait_ge(spec_dve, 4)
            pe.wait_ge(ada_taken, 5)
            for c in range(KD):
                n = 0
                for t in range(2):
                    for part in range(2):
                        at = part * GC + (c % 2) * P
                        last = mm(bank[(6, 7, 0, 1)[c // 2]][:, (c % 2) * T:(c % 2) * T + T],
                                  spectrum[:, t, c // 2, at:at + P], rows[:, part, t, :], start=(n == 0), stop=(n == 3))
                        n += 1
                if c % 2:
                    last.then_inc(four_ready, 1)
            pe.wait_ge(four_ready, 4)
            pe.nop().then_inc(slot_free[unit_slot(u)], 1)
            pe.wait_ge(four_act, 2)
            pe.wait_ge(four_dve, 2)
            project("fnet", fourier, 2, proj_ready)
            mean(3, 5, square_l, bank[6][:, 0:T])
            pe.wait_ge(router_in, 16)
            pe.wait_ge(h_ready, 40)
            for t in range(2):
                for k in range(KD):
                    last = mm(bank[4][:, 8 * t:8 * t + 8], h[:, k, t * P:(t + 1) * P], router[:, k, :],
                              start=(k == 0), stop=(k == KD - 1))
            last.then_inc(logits_ready, 1)
            for f in range(4):
                for j in range(4):
                    last = nc.tensor.transpose(bank[f][:, j * P:(j + 1) * P],
                                               h[:, 4 * (f % 2) + j, (f // 2) * P:(f // 2 + 1) * P], C("ident"))
                last.then_inc(tok_ready, 1)
            pe.wait_ge(tok_ready, 4)
            pe.nop().then_inc(scratch_free, 1)
            pe.wait_ge(mask_ready, 2)
            m0, m1 = small[:, 184:192], small[:, 192:200]
            mm(bank[5][:, 0:8], C("before"), m0, start=True, stop=True)
            mm(bank[5][:, 8:16], C("ones"), m0, start=True, stop=False)
            mm(bank[5][:, 8:16], C("before"), m1, start=False, stop=True)
            mm(bank[5][:, 16:24], C("ones"), m0, start=True, stop=False)
            mm(bank[5][:, 16:24], C("ones"), m1, start=False, stop=True).then_inc(rank_ready, 1)

            def gather(i):
                pe.wait_ge(pick_ready, i + 1)
                for k in range(KD):
                    for t in range(2):
                        last = mm(bank[4 + k // 4][:, (k % 4) * CAP:(k % 4 + 1) * CAP], h_tok[:, t, k * P:(k + 1) * P],
                                  pick[:, t, :], start=(t == 0), stop=(t == 1))
                last.then_inc(gathered, 1)

            def expert_up(i, g):
                s = g % SLOTS
                pe.wait_ge(slot_in[s], 32 * i + (slot_base(s) + 16 * (g // SLOTS + 1)))
                if not (isinstance(i, int) and g < 2):
                    pe.wait_ge(e_hidden, GROUPS * i + (g - 1))
                for v in range(2):
                    w = view(ring, s * SLOT + v * KD * PAIR, KD, PAIR)
                    for j in range(2):
                        at = (2 * v + j) * CAP
                        for k in range(KD):
                            last = mm(bank[g % 2][:, at:at + CAP], w[:, k, j * P:(j + 1) * P], h_exp[:, k, :],
                                      start=(k == 0), stop=(k == KD - 1))
                last.then_inc(e_up, 1)

            def expert_down(i, g):
                s = g % SLOTS
                pe.wait_ge(e_hidden, GROUPS * i + (g + 1))
                if g == 0 and not isinstance(i, int):
                    pe.wait_ge(yT_taken, i)
                w = view(ring, s * SLOT + 2 * KD * PAIR, 2, D)
                for j in range(2):
                    for k in range(KD):
                        last = mm(bank[2 + k // 4][:, (k % 4) * CAP:(k % 4 + 1) * CAP], w[:, j, k * P:(k + 1) * P],
                                  hidden_e[:, g % 2, j, :], start=(g == 0 and j == 0 and k % 4 == 0),
                                  stop=(g == GROUPS - 1 and j == 1), skip_group_check=True)
                last.then_inc(e_down, 1)

            def turn_y(i):
                pe.wait_ge(yT_taken, i + 1)
                for k in range(KD):
                    last = nc.tensor.transpose(bank[4 + k // 4][0:CAP, (k % 4) * P:(k % 4 + 1) * P], yT[:, k, :], C("ident"))
                last.then_inc(y_turned, 1)

            def combine(i, half):
                if half == 0:
                    pe.wait_ge(y_taken, i + 1)
                    pe.wait_ge(spread_taken, i + 1)
                for j in range(4):
                    k = 4 * half + j
                    last = mm(bank[(6, 7, 4, 5)[k // 2]][:, (k % 2) * T:(k % 2) * T + T],
                              y_tok[:, k * P:(k + 1) * P], spread, start=True, stop=True)
                    if j % 2:
                        last.then_inc(part_ready, 1)

            def turn_spread(i):
                pe.wait_ge(gated_ready, i + 1)
                if not isinstance(i, int):
                    pe.wait_ge(part_added, KD * i)
                for t in range(2):
                    last = nc.tensor.transpose(bank[6][0:CAP, t * P:(t + 1) * P], pick_gated[:, t, :], C("ident"))
                last.then_inc(spread_turned, 1)

            def expert(i):
                first = isinstance(i, int)
                pe.wait_ge(h_exp_act, i + 1)
                pe.wait_ge(h_exp_dve, i + 1)
                for g in range(GROUPS):
                    expert_up(i, g)
                    if not first:
                        if g == 2:
                            turn_y(i - 1)
                        if g in (3, 4):
                            combine(i - 1, g - 3)
                    if g == 6:
                        turn_spread(i)
                    if g == GROUPS - 1:
                        gather(i + 1)
                    if g >= 1:
                        expert_down(i, g - 1)
                expert_down(i, GROUPS - 1)
                pe.wait_ge(e_down, GROUPS * i + GROUPS)
                pe.nop().then_inc(y_ready, 1)

            pe.wait_ge(tok_act, 2)
            pe.wait_ge(tok_dve, 2)
            pe.wait_ge(loops_ready, 1)
            gather(0)
            expert(0)
            turns = pe.value_load(loops[0:1, 0:1], min_val=EXPERTS, max_val=EXPERTS * MAX_ROUNDS)
            with pe.Fori(1, turns) as i:
                expert(i)
            pe.wait_ge(h_exp_act, turns + 1)
            pe.wait_ge(h_exp_dve, turns + 1)
            turn_y(turns - 1)
            for half in range(2):
                combine(turns - 1, half)
            mean(4, 6, square_l, bank[0][:, 0:T])


def kernel(**inputs):
    import concourse.bacc as _bacc
    from concourse.bass_utils import run_bass_kernel_spmd as _run

    a = {k: np.asarray(v) for k, v in inputs.items()}

    def chunks(v):
        return v.reshape(-1, P).T

    def rows(w, cols):
        return w.reshape(KD, P, -1, cols).transpose(2, 1, 0, 3).reshape(-1, P, KD * cols)

    def ffn(w1, w3, w2, groups):
        down = w2.reshape(groups, 2, P, D).transpose(0, 2, 1, 3).reshape(groups, P, 2 * D)
        return np.concatenate([rows(w1, PAIR), rows(w3, PAIR), down], axis=2)

    con, rope, invcount, dft = constants()
    vec = np.concatenate([
        *[chunks(a["norm_mix_g"][i]) for i in range(2)], *[chunks(a["norm_ffn_g"][i]) for i in range(2)],
        chunks(a["final_g"]), chunks(a["cq_norm_g"][0]), chunks(a["ckv_norm_g"][0]), chunks(a["pool_scale"][0]),
        *[chunks(a["ada_b"][i]) for i in range(2)],
        np.stack([chunks(a["c"][0]), chunks(a["c_ctx"])], axis=2).reshape(P, 2 * KD)], axis=1)
    w_in = a["mix_in_w"][0]
    low = Q_LORA + KV_LORA + ROPE
    ukv = a["w_ukv"][0].reshape(KV_LORA, HEADS, 2, VD).transpose(0, 2, 1, 3).reshape(KV_LORA, -1)
    attn = np.concatenate([
        a["w_uq"][0].reshape(2, P, -1).transpose(1, 0, 2).reshape(P, -1), ukv,
        a["pool_w"][0].transpose(1, 0, 2).reshape(P, -1)], axis=1)
    arrays = {
        "vec": vec, "con": con, "rope": rope, "invcount": invcount,
        "x": a["x"][0].T.reshape(KD, P, T).transpose(1, 0, 2).reshape(P, -1),
        "ctx": a["ctx"][0].T.reshape(KD, P, TC).transpose(1, 0, 2),
        "ada": np.stack([rows(a["ada_w"][i], ADA_COLS) for i in range(2)]),
        "mixa": rows(w_in[:, low:], 512)[0], "mixb": rows(w_in[:, :low], low)[0],
        "attn": attn, "mixout": rows(a["mix_out_w"][0], 512),
        "ffn": ffn(a["ffn_w1"][0], a["ffn_w3"][0], a["ffn_w2"][0], GROUPS_DENSE),
        "dft": dft, "fnet": rows(a["fnet_out_w"][0], 512),
        "router": a["router_w"][0].reshape(KD, P, EXPERTS).transpose(1, 0, 2).reshape(P, -1),
        "moe": np.stack([ffn(a["moe_w1"][0, e], a["moe_w3"][0, e], a["moe_w2"][0, e], GROUPS) for e in range(EXPERTS)]),
    }
    nc = _bacc.Bacc("TRN2", target_bir_lowering=False, num_devices=1)
    given, args = {}, []
    for name, v in arrays.items():
        v = np.ascontiguousarray(v)
        given[f"in_{name}"] = v
        args.append(nc.dram_tensor(f"in_{name}", v.shape, mybir.dt.from_np(v.dtype), kind="ExternalInput").ap())
    args.append(nc.dram_tensor("out_xT", (P, KD * T), F32, kind="ExternalOutput").ap())
    build(nc, *args)
    r = _run(nc, [given], core_ids=[0])
    out = r.results[0]["out_xT"]
    return out.reshape(P, KD, T).transpose(2, 1, 0).reshape(1, T, D)
```

```python
import math
from contextlib import ExitStack

import numpy as np

import concourse.bass as bass
from concourse import mybir

F32 = mybir.dt.float32
F32R = mybir.dt.float32r
I32 = mybir.dt.int32
ALU = mybir.AluOpType
ACT = mybir.ActivationFunctionType
AX_X = mybir.AxisListType.X

P = 128
D = 1024
KD = D // P
T = 256
TC = 256
TA = T + TC
GRID_W = 64
HEADS, NOPE, ROPE, VD = 8, 64, 32, 64
QK = NOPE + ROPE
Q_LORA, KV_LORA = 256, 128
WINDOWS = (2, 4, 8, 16)
NG = 4
GC = D // NG
F_DENSE, F_EXPERT, EXPERTS = 2816, 3584, 8
PAIR = 2 * P
GROUPS = F_DENSE // PAIR
BLOCK = 4 * P
BLOCKS = F_EXPERT // BLOCK
SCALE = float(QK) ** -0.5
EPS = 1e-6

CAP = 96
MAX_ROUNDS = -(-T // CAP)
TABLE = EXPERTS * (MAX_ROUNDS + 1)

UNIT = KD * 512
UNIT_SLOTS = 3
PIECE = 2048
PIECE_SLOTS = 14
RING = PIECE_SLOTS * PIECE
SCRATCH = UNIT_SLOTS * UNIT
ADA_UNITS = 6 * D // 512
PARTS = 3
SPLITS = 3
SPLITS_DENSE = 2
PAD = 8
PADDED = T + 2 * PAD

VEC = {}
_at = 0
for _name, _n in (("mix_g", 16), ("ffn_g", 16), ("final_g", 8), ("cq_g", 2), ("ckv_g", 1), ("pool_scale", 4),
                  ("ada_b", 96), ("cond", 16)):
    VEC[_name] = (_at, _at + _n)
    _at += _n
VECS = _at

CON = {}
_at = 0
for _name, _n in (("ident", P), ("mean", P), ("before", P), ("rot", QK), ("iota8", EXPERTS),
                  ("iota", CAP), ("edge", NG * 2 * PAD), ("eps", 1)):
    CON[_name] = (_at, _at + _n)
    _at += _n
CONS = _at


def dense_pieces():
    order = []
    for g in range(GROUPS):
        order += [("w1", g), ("w3", g)] + ([("w2", g - 1)] if g else [])
    return order + [("w2", GROUPS - 1)]


def expert_pieces():
    order = []
    for b in range(BLOCKS):
        order += [(w, b, n) for w in ("w1", "w3") for n in range(2)] + ([("w2", b - 1, n) for n in range(2)] if b else [])
    return order + [("w2", BLOCKS - 1, n) for n in range(2)]


DENSE = dense_pieces()
EXPERT = expert_pieces()
PIECES = len(EXPERT)


def constants():
    con = np.zeros((P, CONS), np.float32)

    def put(name, a):
        con[:a.shape[0], CON[name][0]:CON[name][1]] = a

    put("ident", np.eye(P))
    put("mean", np.full((P, P), 1.0 / D))
    put("before", np.triu(np.ones((P, P)), 1))
    rot = np.zeros((QK, QK))
    half = ROPE // 4
    for b in (NOPE, NOPE + ROPE // 2):
        for j in range(half):
            rot[b + half + j, b + j] = -1.0
            rot[b + j, b + half + j] = 1.0
    put("rot", rot)
    put("iota8", np.tile(np.arange(EXPERTS), (P, 1)))
    put("iota", np.tile(np.arange(CAP), (P, 1)))
    put("eps", np.full((P, 1), EPS))

    t = np.arange(T)
    inv = (1.0 / (np.float32(10000.0) ** (np.arange(0, ROPE // 2, 2, dtype=np.float32) / np.float32(ROPE // 2))))
    inv = inv.astype(np.float32)
    angle = np.zeros((ROPE, T), np.float32)
    for b, position in ((0, t // GRID_W), (ROPE // 2, t % GRID_W)):
        a = inv[:, None] * position.astype(np.float32)[None, :]
        angle[b:b + half] = a
        angle[b + half:b + 2 * half] = a
    rope = np.concatenate([np.cos(angle), np.sin(angle)], axis=1).astype(np.float32)

    edge = np.ones((NG, 2, PAD))
    for g, w in enumerate(WINDOWS):
        count = np.clip(t - w // 2 + w, 0, T) - np.clip(t - w // 2, 0, T)
        edge[g] = w / np.stack([count[:PAD], count[-PAD:]])
    put("edge", np.tile(edge.reshape(1, -1), (P, 1)))

    c = np.arange(GC)
    a = 2.0 * np.pi * ((c[:, None] * c[None, :]) % GC) / GC
    chan = np.concatenate([np.cos(a), np.sin(a)], axis=1).reshape(2, P, 2 * GC).transpose(1, 0, 2).reshape(P, -1)
    a = 2.0 * np.pi * ((t[:, None] * t[None, :]) % T) / T
    norm = 1.0 / math.sqrt(T * GC)
    row = np.stack([np.cos(a) * norm, -np.sin(a) * norm]).reshape(2, 2, P, T).transpose(2, 0, 1, 3).reshape(P, -1)
    dft = np.concatenate([chan, row], axis=1).astype(np.float32)
    return con, rope, dft


def build(nc, vec_d, con_d, rope_d, x_d, ctx_d, ada_d, mixa_d, mixb_d, attn_d, mixout_d, ffn_d,
          dft_d, fnet_d, router_d, moe_d, out_d):
    ctx = ExitStack()
    with ctx:
        def sb(name, cols, dt=F32):
            return ctx.enter_context(nc.sbuf_tensor(name, [P, cols], dt))

        def sem(name):
            return ctx.enter_context(nc.semaphore(name))

        ring = sb("ring", RING)
        split = sb("split", 6 * PIECE + 2 * KD * CAP + 2 * 4 * CAP, F32R)
        xT = sb("xT", KD * T)
        con = sb("con", CONS)
        vec = sb("vec", VECS)
        ada = sb("ada", 2 * 96)
        moda = sb("moda", 5 * KD)
        rstd = sb("rstd", TA)
        small = sb("small", 240)
        loops = sb("loops", 2, I32)
        condp = sb("condp", KD * 32)
        work = sb("work", 5824)
        bank = [ctx.enter_context(nc.psum_tensor(f"bank{b}", [P, 512], F32)) for b in range(8)]

        def view(t, at, *dims):
            n = int(np.prod(dims))
            v = t[:, at:at + n]
            if len(dims) == 2:
                return v.rearrange("p (a b) -> p a b", a=dims[0])
            if len(dims) == 3:
                return v.rearrange("p (a b c) -> p a b c", a=dims[0], b=dims[1])
            return v

        def C(name):
            return con[:, CON[name][0]:CON[name][1]]

        def V(name):
            return vec[:, VEC[name][0]:VEC[name][1]]

        x = view(xT, 0, KD, T)
        cond = view(condp, 0, KD, 32)
        scratch = SCRATCH
        square = view(ring, scratch, KD, TA)
        keys = view(ring, scratch, HEADS, TA)
        h_all = view(ring, scratch + 4096, KD, TA)
        values = view(ring, scratch + 4096, 4, HEADS * VD)
        probs = view(ring, scratch + 6144, 4, TA)
        ctxT = view(ring, scratch + 8192, KD, TC)
        queries = view(ring, scratch + 8192, HEADS, T)
        lora_sq = view(ring, scratch + 10240, 2, 512)
        rope_tmp = view(ring, scratch + 10240, 512)
        probsT = view(ring, scratch + 10240, 2, 4, T)
        mixed = view(ring, scratch + 12288, KD, T)
        pool0 = view(ring, scratch + 12288, NG, PADDED)
        cqT = view(ring, scratch + 14336, 2, T)
        ckvT = view(ring, scratch + 14848, TA)
        krT = view(ring, scratch + 15360, TA)
        ada_rows = view(ring, scratch + 15872, 512)
        square_l = view(ring, scratch, KD, T)
        h = view(ring, scratch + 4096, KD, T)
        gate_tmp = view(ring, scratch + 6144, 2, 2, T)
        hidden_tmp = view(ring, scratch + 7168, 2, T)
        spectrum = view(ring, scratch + 8192, 2, NG, 2 * GC)
        fourier = view(ring, scratch + 12288, KD, T)
        assert scratch + 16384 == RING
        w_uq = view(work, 0, 2, HEADS * QK)
        w_ukv = view(work, 1536, 2, HEADS * VD)
        pool_w = view(work, 2560, NG, P)
        pool1 = view(work, 3072, NG, PADDED)
        pool2 = view(work, 3072 + NG * PADDED, NG, PADDED)
        rope = view(work, 5248, 2, T)
        router = view(work, 5760, KD, EXPERTS)
        h_tok = view(work, 0, 2, D)
        gate_e = work[0:CAP, 2048:2560]
        hidden_e = work[0:CAP, 2560:3072]
        y_tok = work[0:CAP, 3072:4096]
        pick = view(work, 4096, 2, CAP)
        pick_gated = view(work, 4288, 2, CAP)
        spread = work[0:CAP, 4480:4736]
        rank_at = view(work, 4736, 2, TABLE)
        gate_at = view(work, 4800, 2, TABLE)
        assert TABLE == 32 and 3072 + 2 * NG * PADDED == 5248
        high_d = view(split, 0, SPLITS_DENSE, PIECE)
        low_d = view(split, SPLITS_DENSE * PIECE, SPLITS_DENSE, PIECE)
        h_parts = view(split, 4 * PIECE, 2, KD, T)
        hidden_parts = [view(split, 6 * PIECE + n * 2 * 2 * T, 2, 2, T) for n in range(2)]
        high_e = view(split, 0, SPLITS, PIECE)
        low_e = view(split, SPLITS * PIECE, SPLITS, PIECE)
        x_parts = view(split, 6 * PIECE, 2, KD, CAP)
        hidden_e_parts = view(split, 6 * PIECE + 2 * KD * CAP, 2, 4, CAP)

        def plain(ap):
            return ap.bitcast(F32)

        vec_in, con_in, x_in, ctx_in = sem("vec_in"), sem("con_in"), sem("x_in"), sem("ctx_in")
        attn_in, rope_in, router_in = sem("attn_in"), sem("rope_in"), sem("router_in")
        unit_in = [sem(f"unit_in{i}") for i in range(UNIT_SLOTS)]
        unit_free = [sem(f"unit_free{i}") for i in range(UNIT_SLOTS)]
        piece_in = [sem(f"piece_in{i}") for i in range(PIECE_SLOTS)]
        scratch_free = sem("scratch_free")
        cond_ready = sem("cond_ready")
        rows_ready, rows_taken, ada_ready, ada_taken = (
            sem("rows_ready"), sem("rows_taken"), sem("ada_ready"), sem("ada_taken"))
        rows_zero = sem("rows_zero")
        h_high, h_low = sem("h_high"), sem("h_low")
        squared, mean_ready, root_ready = sem("squared"), sem("mean_ready"), sem("root_ready")
        scaled, h_ready = sem("scaled"), sem("h_ready")
        pads_zero = sem("pads_zero")
        mixa_ready, mixa_taken = sem("mixa_ready"), sem("mixa_taken")
        mixb_ready, cq_taken, kv_taken = sem("mixb_ready"), sem("cq_taken"), sem("kv_taken")
        lora_squared, lora_mean, lora_root, lora_ready = (
            sem("lora_squared"), sem("lora_mean"), sem("lora_root"), sem("lora_ready"))
        prep_ready, prep_act, prep_dve = sem("prep_ready"), sem("prep_act"), sem("prep_dve")
        kr_roped, kr_spread, pooled = sem("kr_roped"), sem("kr_spread"), sem("pooled")
        scores_ready, max_ready, exp_ready, probs_ready = (
            sem("scores_ready"), sem("max_ready"), sem("exp_ready"), sem("probs_ready"))
        probsT_ready, probsT_taken = sem("probsT_ready"), sem("probsT_taken")
        pv_ready, pv_taken = sem("pv_ready"), sem("pv_taken")
        pool_ready, pool_taken = sem("pool_ready"), sem("pool_taken")
        proj_ready, residual = sem("proj_ready"), sem("residual")
        high_ready, low_ready, used = sem("high_ready"), sem("low_ready"), sem("used")
        gate_ready, hidden_ready, hidden_high, hidden_low = (
            sem("gate_ready"), sem("hidden_ready"), sem("hidden_high"), sem("hidden_low"))
        spec_ready, spec_act, spec_dve = sem("spec_ready"), sem("spec_act"), sem("spec_dve")
        four_ready, four_act, four_dve = sem("four_ready"), sem("four_act"), sem("four_dve")
        logits_ready, tok_ready, tok_act, tok_dve = (
            sem("logits_ready"), sem("tok_ready"), sem("tok_act"), sem("tok_dve"))
        gap_ready, odds_ready, mask_ready, rank_ready, loops_ready = (
            sem("gap_ready"), sem("odds_ready"), sem("mask_ready"), sem("rank_ready"), sem("loops_ready"))
        pick_ready, gathered, x_high, x_low = sem("pick_ready"), sem("gathered"), sem("x_high"), sem("x_low")
        e_high, e_low, e_used = sem("e_high"), sem("e_low"), sem("e_used")
        e_gate, e_hidden, e_turned, e_hidden_high, e_hidden_low = (
            sem("e_gate"), sem("e_hidden"), sem("e_turned"), sem("e_hidden_high"), sem("e_hidden_low"))
        y_act, y_dve = sem("y_act"), sem("y_dve")
        gated_ready, spread_turned, spread_taken = (
            sem("gated_ready"), sem("spread_turned"), sem("spread_taken"))
        part_ready, part_added = ([sem(f"{name}{pair}") for pair in range(4)] for name in ("part_ready", "part_added"))
        ada_done = sem("ada_done")
        dve_step, pool_step = sem("dve_step"), sem("pool_step")
        out_ready, stored = sem("out_ready"), sem("stored")

        units, first_unit = [], {}

        def add(name, src, cols):
            first_unit.setdefault(name, len(units))
            units.append((src, cols))

        def add_ada(part):
            for u in range(4):
                add(f"ada{part}", ada_d[part // PARTS, 4 * (part % PARTS) + u], UNIT)

        for part in range(1):
            add_ada(part)
        add("mixa", mixa_d, KD * 512)
        add("mixb", mixb_d, KD * 416)
        for part in (1, 2, 3):
            add_ada(part)
        for n in range(2):
            add("mixout", mixout_d[n], KD * 512)
        add_ada(4)
        for n in range(0, len(DENSE), 2):
            m = min(2, len(DENSE) - n)
            add("ffn", ffn_d[:, n * PIECE:(n + m) * PIECE], m * PIECE)
        add_ada(5)
        add("dft", dft_d, 4 * 512)
        for n in range(2):
            add("fnet", fnet_d[n], KD * 512)
        unit_uses = [len(range(s, len(units), UNIT_SLOTS)) for s in range(UNIT_SLOTS)]

        def unit_slot(n):
            return n % UNIT_SLOTS

        def unit_wait(eng, n):
            eng.wait_ge(unit_in[unit_slot(n)], 16 * (n // UNIT_SLOTS + 1))

        def piece_view(n):
            u = first_unit["ffn"] + n // 2
            return view(ring, unit_slot(u) * UNIT + (n % 2) * PIECE, PIECE)

        ADA_BANKS = [(6, 7)] * 5 + [(0, 1)]

        PREP = [("kr", 0)] + [("q", p) for p in range(4)] + [("k", p) for p in range(4)] \
            + [("rot", p) for p in range(4)] + [("v", p) for p in range(4)]
        PREP_BY = ["act" if kind in ("q", "k") else "dve" for kind, _ in PREP]
        NPREP = 6

        def prep_taken(eng, n):
            s = prep_act if PREP_BY[n] == "act" else prep_dve
            eng.wait_ge(s, sum(b == PREP_BY[n] for b in PREP_BY[:n + 1]))

        ITEMS = [(hd, q) for hd in range(HEADS) for q in range(2)]
        ADA_ITEMS = {n: (2 + (n - 1) // 2 // 4, (n - 1) // 2 % 4) for n in range(1, 16, 2)}
        ADA_TAKES = {8: 2, 10: 2.5, 15: 3}

        def hidden_at(b):
            return 7

        block = ctx.enter_context(nc.Block())

        @block.sync
        def _(sp):
            def unit_load(n):
                src, cols = units[n]
                s = unit_slot(n)
                if n >= UNIT_SLOTS:
                    sp.wait_ge(unit_free[s], n // UNIT_SLOTS)
                sp.dma_start(ring[:, s * UNIT:s * UNIT + cols], src).then_inc(unit_in[s], 16)

            sp.dma_start(vec[:, :], vec_d).then_inc(vec_in, 16)
            sp.dma_start(xT[:, :], x_d).then_inc(x_in, 16)
            sp.dma_start(con[:, :], con_d).then_inc(con_in, 16)
            sp.dma_start(ctxT, ctx_d).then_inc(ctx_in, 16)
            for n in range(first_unit["mixb"] + 1):
                unit_load(n)
            sp.dma_start(work[:, 0:3072], attn_d).then_inc(attn_in, 16)
            sp.dma_start(work[NOPE:QK, 5248:5760], rope_d).then_inc(rope_in, 16)
            sp.dma_start(view(work, 5760, KD * EXPERTS), router_d).then_inc(router_in, 16)
            for n in range(first_unit["mixb"] + 1, len(units)):
                unit_load(n)

            def expert_loads(e, i):
                for q in range(PIECES):
                    s = q % PIECE_SLOTS
                    if not isinstance(i, int):
                        sp.wait_ge(e_low, PIECES * i + (q - PIECE_SLOTS + 1))
                    elif q >= PIECE_SLOTS:
                        sp.wait_ge(e_low, q - PIECE_SLOTS + 1)
                    elif s * PIECE < SCRATCH:
                        u = s * PIECE // UNIT
                        sp.wait_ge(unit_free[u], unit_uses[u])
                    else:
                        sp.wait_ge(scratch_free, 1)
                    sp.dma_start(ring[:, s * PIECE:(s + 1) * PIECE], moe_d[e, q]).then_inc(piece_in[s], 16)

            expert_loads(0, 0)
            with sp.Fori(1, EXPERTS) as e:
                expert_loads(e, e)
            sp.wait_ge(loops_ready, 1)
            rounds = sp.value_load(loops[0:1, 1:2], min_val=1, max_val=MAX_ROUNDS)
            with sp.If(rounds > 1):
                with sp.Fori(1, rounds) as r:
                    with sp.Fori(0, EXPERTS) as e:
                        expert_loads(e, EXPERTS * r + e)
            sp.wait_ge(out_ready, KD)
            sp.dma_start(out_d, view(ring, 0, KD * T)).then_inc(stored, 16)
            sp.wait_ge(stored, 16)

        @block.gpsimd
        def _(pool):
            n_step = [0]

            def link(ins):
                n_step[0] += 1
                ins.then_inc(pool_step, 1)
                pool.wait_ge(pool_step, n_step[0])

            nc.gpsimd.memset(ada_rows, 0.0).then_inc(rows_zero, 1)
            nc.gpsimd.memset(condp[:, :], 0.0).then_inc(rows_zero, 1)
            nc.gpsimd.memset(pool0[:, :, 0:PAD], 0.0).then_inc(pads_zero, 1)
            nc.gpsimd.memset(pool0[:, :, PAD + T:], 0.0).then_inc(pads_zero, 1)
            pool.wait_ge(pads_zero, 2)
            pool.wait_ge(rows_zero, 2)
            pool.wait_ge(mixa_taken, 2)
            pool.wait_ge(con_in, 16)
            n2, n4, n8, n16 = PADDED - 1, PADDED - 3, PADDED - 7, PADDED - 15
            link(nc.gpsimd.tensor_tensor(pool1[:, :, 0:n2], pool0[:, :, 0:n2], pool0[:, :, 1:1 + n2], ALU.add))
            link(nc.gpsimd.tensor_tensor(pool2[:, 1:, 0:n4], pool1[:, 1:, 0:n4], pool1[:, 1:, 2:2 + n4], ALU.add))
            link(nc.gpsimd.tensor_tensor(pool1[:, 2:, 0:n8], pool2[:, 2:, 0:n8], pool2[:, 2:, 4:4 + n8], ALU.add))
            link(nc.gpsimd.tensor_tensor(pool2[:, 3:, 0:n16], pool1[:, 3:, 0:n16], pool1[:, 3:, 8:8 + n16], ALU.add))
            for g, w in enumerate(WINDOWS):
                at = (pool1 if g % 2 == 0 else pool2)[:, g, PAD - w // 2:PAD - w // 2 + T]
                link(nc.gpsimd.tensor_scalar(at, at, 1.0 / w, None, ALU.mult))
                for n, ends in enumerate((at[:, 0:PAD], at[:, T - PAD:T])):
                    fix = C("edge")[:, (2 * g + n) * PAD:(2 * g + n + 1) * PAD]
                    link(nc.gpsimd.tensor_tensor(ends, ends, fix, ALU.mult))
                nc.gpsimd.tensor_tensor(at, at, pool0[:, g, PAD:PAD + T], ALU.subtract).then_inc(pooled, 1)
            pool.wait_ge(pooled, NG)
            pool.wait_ge(kr_roped, 1)
            for hd in range(HEADS):
                nc.gpsimd.tensor_copy(keys[NOPE:QK, hd, :], krT[NOPE:QK, :]).then_inc(kr_spread, 1)
                pool.wait_ge(kr_spread, hd + 1)

        @block.scalar
        def _(act):
            act.wait_ge(vec_in, 16)
            act.wait_ge(rows_zero, 2)
            nc.scalar.activation(cond[:, :, 0:2], V("cond").rearrange("p (a b) -> p a b", a=KD), ACT.Silu).then_inc(cond_ready, 1)
            act.wait_ge(x_in, 16)
            nc.scalar.activation(square[:, :, 0:T], x, ACT.Square).then_inc(squared, 1)
            act.wait_ge(ctx_in, 16)
            nc.scalar.activation(square[:, :, T:TA], ctxT, ACT.Square).then_inc(squared, 1)
            act.wait_ge(con_in, 16)

            def root(stage, source):
                act.wait_ge(mean_ready, stage + 1)
                nc.scalar.activation(rstd[:, 0:source.shape[-1]], source, ACT.Sqrt, bias=C("eps")).then_inc(root_ready, 1)

            def shifts(done, target, halves):
                for k in range(KD):
                    for n, (lo, shift) in enumerate(halves):
                        act.wait_ge(scaled, done + k * len(halves) + n + 1)
                        nc.scalar.activation(target[:, k, lo:lo + T], target[:, k, lo:lo + T], ACT.Identity,
                                             bias=shift(k)).then_inc(h_ready, 1)

            def adac(layer, part, k, who=0):
                at = 96 * layer + 2 * (KD * part + k) + who
                return ada[:, at:at + 1]

            root(0, bank[0][:, :])
            act.wait_ge(ada_taken, 1)
            shifts(0, h_all, [(0, lambda k: adac(0, 0, k)), (T, lambda k: adac(0, 0, k, 1))])
            act.wait_ge(pads_zero, 2)
            for n in range(2):
                act.wait_ge(mixa_ready, n + 1)
                nc.scalar.activation(pool0[:, 2 * n:2 * n + 2, PAD:PAD + T],
                                     bank[1 + n][:, :].rearrange("p (a b) -> p a b", a=2), ACT.Copy).then_inc(mixa_taken, 1)
            act.wait_ge(mixb_ready, 2)
            nc.scalar.activation(lora_sq[:, 0, :], bank[3][:, :], ACT.Square).then_inc(lora_squared, 1)
            nc.scalar.activation(lora_sq[:, 1, :], bank[4][:, :], ACT.Square).then_inc(lora_squared, 1)
            act.wait_ge(lora_mean, 2)
            nc.scalar.activation(rstd[:, 0:T], bank[0][:, 0:T], ACT.Sqrt, bias=C("eps"),
                                 scale=float(D) / Q_LORA).then_inc(lora_root, 1)
            nc.scalar.activation(lora_sq[:, 1, :], bank[1][:, :], ACT.Sqrt, bias=C("eps"),
                                 scale=float(D) / KV_LORA).then_inc(lora_root, 1)
            for n, (kind, p) in enumerate(PREP):
                if PREP_BY[n] != "act":
                    continue
                act.wait_ge(prep_ready, n + 1)
                b = bank[n % NPREP]
                if kind == "q":
                    nc.scalar.activation(queries[0:QK, 2 * p:2 * p + 2, :],
                                         b[0:QK, :].rearrange("p (a b) -> p a b", a=2), ACT.Copy).then_inc(prep_act, 1)
                else:
                    nc.scalar.activation(keys[0:NOPE, 2 * p, :], b[0:NOPE, :], ACT.Copy)
                    nc.scalar.activation(keys[0:NOPE, 2 * p + 1, :], b[NOPE:P, :], ACT.Copy).then_inc(prep_act, 1)

            act.wait_ge(pooled, NG)

            def turn_probs(n):
                hd, q = ITEMS[n]
                act.wait_ge(probsT_ready, n + 1)
                if hd >= 2:
                    act.wait_ge(pv_ready, hd - 1)
                nc.scalar.activation(probsT[:, hd % 2, :, q * P:(q + 1) * P],
                                     bank[3 + n % 2][:, :].rearrange("p (a b) -> p a b", a=4), ACT.Copy).then_inc(probsT_taken, 1)

            for n in range(len(ITEMS)):
                act.wait_ge(max_ready, n + 1)
                if n >= 4:
                    act.wait_ge(probsT_ready, n - 3)
                nc.scalar.activation(probs[:, n % 4, :], bank[n % 3][:, :], ACT.Exp, bias=small[:, 32 + n:33 + n],
                                     scale=SCALE, accum_out=small[:, 48 + n:49 + n]).then_inc(exp_ready, 1)
                if n >= 3:
                    turn_probs(n - 3)
            for n in range(len(ITEMS) - 3, len(ITEMS)):
                turn_probs(n)
            for g in range(NG):
                act.wait_ge(pool_ready, g // 2 + 1)
                nc.scalar.activation(mixed[:, NG + g, :], bank[3 + g // 2][:, (g % 2) * T:(g % 2) * T + T], ACT.Copy,
                                     scale=V("pool_scale")[:, g:g + 1]).then_inc(pool_taken, 1)

            def squares(need):
                for k in range(KD):
                    act.wait_ge(residual, need + k + 1)
                    nc.scalar.activation(square_l[:, k, :], x[:, k, :], ACT.Square).then_inc(squared, 1)

            squares(0)
            root(1, bank[5][:, 0:T])
            act.wait_ge(ada_taken, 2)
            for k in range(KD):
                act.wait_ge(scaled, 16 + k + 1)
                nc.scalar.activation(h_parts[:, 0, k, :], h[:, k, :], ACT.Identity, bias=adac(0, 3, k)).then_inc(h_high, 1)
            for q in range(len(DENSE)):
                if q % 2 == 0:
                    unit_wait(act, first_unit["ffn"] + q // 2)
                if q >= SPLITS_DENSE:
                    act.wait_ge(used, q - SPLITS_DENSE + 1)
                nc.scalar.activation(high_d[:, q % SPLITS_DENSE, :], piece_view(q), ACT.Copy).then_inc(high_ready, 1)
                done = q - SPLITS_DENSE
                if done >= 0 and DENSE[done][0] == "w1":
                    g = DENSE[done][1]
                    if g >= 2:
                        act.wait_ge(hidden_ready, g - 1)
                    nc.scalar.activation(gate_tmp[:, g % 2], bank[2 * (g % 2)][:, :].rearrange("p (a b) -> p a b", a=2),
                                         ACT.Silu).then_inc(gate_ready, 1)
                if done >= 0 and DENSE[done][0] == "w3":
                    g = DENSE[done][1]
                    act.wait_ge(hidden_ready, g + 1)
                    if g >= 2:
                        act.wait_ge(used, DENSE.index(("w2", g - 2)) + 1)
                    nc.scalar.activation(hidden_parts[g % 2][:, 0], hidden_tmp, ACT.Copy).then_inc(hidden_high, 1)
            squares(KD)
            root(2, bank[2][:, 0:T])
            act.wait_ge(ada_taken, 4)
            shifts(24, h, [(0, lambda k: adac(1, 0, k))])
            for f in range(0, 8, 2):
                act.wait_ge(spec_ready, f + 1)
                nc.scalar.activation(spectrum[:, f // NG, f % NG, :], bank[2 + f % 4][:, :], ACT.Copy).then_inc(spec_act, 1)
            for f in (0, 2):
                act.wait_ge(four_ready, f + 1)
                nc.scalar.activation(fourier[:, 2 * f:2 * f + 2, :],
                                     bank[(6, 7, 0, 1)[f]][:, :].rearrange("p (a b) -> p a b", a=2), ACT.Copy).then_inc(four_act, 1)
            squares(2 * KD)
            root(3, bank[6][:, 0:T])
            act.wait_ge(ada_taken, 5)
            shifts(32, h, [(0, lambda k: adac(1, 3, k))])
            for f in (0, 2):
                act.wait_ge(tok_ready, f + 1)
                nc.scalar.activation(h_tok[:, f // 2, (f % 2) * 512:(f % 2) * 512 + 512], bank[f][:, :], ACT.Copy).then_inc(tok_act, 1)
            for t in range(2):
                act.wait_ge(gap_ready, t + 1)
                nc.scalar.activation(small[:, 66 + t:67 + t], small[:, 64 + t:65 + t], ACT.Exp).then_inc(odds_ready, 1)

            def take_gathered(i):
                act.wait_ge(gathered, i + 1)
                for n in range(2):
                    ins = nc.scalar.activation(x_parts[:, 0, 4 * n:4 * n + 4, :],
                                               bank[5 + n][:, 0:4 * CAP].rearrange("p (a b) -> p a b", a=4), ACT.Copy)
                ins.then_inc(x_high, 1)

            def take_y(done):
                act.wait_ge(e_used, PIECES * done)
                nc.scalar.activation(y_tok[:, 0:512], bank[2][0:CAP, :], ACT.Copy).then_inc(y_act, 1)

            def hidden_top(i, b):
                act.wait_ge(e_turned, BLOCKS * i + (b + 1))
                if b > 0:
                    act.wait_ge(e_used, PIECES * i + (EXPERT.index(("w2", b - 1, 1)) + 1))
                nc.scalar.activation(hidden_e_parts[:, 0], bank[4][:, 0:4 * CAP].rearrange("p (a b) -> p a b", a=4),
                                     ACT.Copy).then_inc(e_hidden_high, 1)

            def expert(i):
                first = isinstance(i, int)
                for q in range(PIECES):
                    s = q % PIECE_SLOTS
                    act.wait_ge(piece_in[s], 16 * (PIECES // PIECE_SLOTS) * i + 16 * (q // PIECE_SLOTS + 1))
                    if not (first and q < SPLITS):
                        act.wait_ge(e_used, PIECES * i + (q - SPLITS + 1))
                    nc.scalar.activation(high_e[:, q % SPLITS, :], ring[:, s * PIECE:(s + 1) * PIECE], ACT.Copy).then_inc(e_high, 1)
                    if q == 2 and not first:
                        take_y(i)
                    done = EXPERT[q - SPLITS] if q >= SPLITS else None
                    if done and done[0] == "w1" and done[2] == 1:
                        b = done[1]
                        if not (first and b == 0):
                            act.wait_ge(e_hidden, BLOCKS * i + b)
                        nc.scalar.activation(gate_e, bank[0][0:CAP, :], ACT.Silu).then_inc(e_gate, 1)
                    if q == hidden_at(0):
                        hidden_top(i, 0)
                    if done and done[0] == "w2" and done[2] == 1 and done[1] + 1 < BLOCKS:
                        hidden_top(i, done[1] + 1)
                    if q == 28:
                        act.wait_ge(spread_turned, i + 1)
                        nc.scalar.activation(spread, bank[7][0:CAP, 0:T], ACT.Copy).then_inc(spread_taken, 1)
                hidden_top(i, BLOCKS - 1)
                take_gathered(i + 1)

            take_gathered(0)
            expert(0)
            turns = act.value_load(loops[0:1, 0:1], min_val=EXPERTS, max_val=EXPERTS * MAX_ROUNDS)
            with act.Fori(1, turns) as i:
                expert(i)
            take_y(turns)
            squares(3 * KD)
            root(4, bank[0][:, 0:T])

        @block.vector
        def _(dve):
            n_step = [0]

            def link(ins):
                n_step[0] += 1
                ins.then_inc(dve_step, 1)
                dve.wait_ge(dve_step, n_step[0])

            def modulation(slot, name, lo, layer, part, who=0):
                at = 96 * layer + 2 * KD * part + who
                scale = ada[:, at:at + 2 * KD - who].rearrange("p (a b) -> p a b", b=2)[:, :, 0] if who == 0 else \
                    ada[:, at - 1:at - 1 + 2 * KD].rearrange("p (a b) -> p a b", b=2)[:, :, 1]
                link(nc.vector.scalar_tensor_tensor(out=moda[:, slot * KD:(slot + 1) * KD], in0=scale, scalar=1.0,
                                                    in1=V(name)[:, lo:lo + KD], op0=ALU.add, op1=ALU.mult))

            def take_rows(part):
                dve.wait_ge(rows_ready, part + 1)
                if part == 0:
                    dve.wait_ge(rows_zero, 1)
                nc.vector.tensor_copy(ada_rows, bank[ADA_BANKS[part][0]][:, :]).then_inc(rows_taken, 1)

            def take_ada(part):
                dve.wait_ge(ada_ready, part + 1)
                at = 96 * (part // PARTS) + 32 * (part % PARTS)
                turned = bank[ADA_BANKS[part][1]][:, :].rearrange("p (a b) -> p a b", b=32)
                for who in range(2):
                    out = ada[:, at:at + 32].rearrange("p (a b) -> p a b", b=2)[:, :, who]
                    ins = nc.vector.tensor_tensor(out, turned[:, :, who], V("ada_b")[:, at // 2:at // 2 + 16], ALU.add)
                ins.then_inc(ada_taken, 1)
                dve.wait_ge(ada_taken, part + 1)

            def reciprocal(stage, n):
                dve.wait_ge(root_ready, stage + 1)
                link(nc.vector.reciprocal(rstd[:, 0:n], rstd[:, 0:n]))

            def scale(source, target, slot, lo=0):
                for k in range(KD):
                    nc.vector.scalar_tensor_tensor(out=target[:, k, lo:lo + T], in0=source[:, k, :],
                                                   scalar=moda[:, slot * KD + k:slot * KD + k + 1],
                                                   in1=rstd[:, lo:lo + T], op0=ALU.mult, op1=ALU.mult).then_inc(scaled, 1)

            def add_projected(n, src, layer, part):
                for k in range(KD):
                    if k % 2 == 0 and n is not None:
                        dve.wait_ge(proj_ready, 4 * n + k // 2 + 1)
                    at = 96 * layer + 2 * (KD * part + k)
                    nc.vector.scalar_tensor_tensor(out=x[:, k, :], in0=bank[src + k // 2][:, (k % 2) * T:(k % 2) * T + T],
                                                   scalar=ada[:, at:at + 1], in1=x[:, k, :],
                                                   op0=ALU.mult, op1=ALU.add).then_inc(residual, 1)

            dve.wait_ge(vec_in, 16)
            take_rows(0)
            take_ada(0)
            modulation(0, "mix_g", 0, 0, 1)
            modulation(1, "mix_g", 0, 0, 1, who=1)
            reciprocal(0, TA)
            for k in range(KD):
                for n, source in enumerate((x, ctxT)):
                    nc.vector.scalar_tensor_tensor(out=h_all[:, k, n * T:(n + 1) * T], in0=source[:, k, :],
                                                   scalar=moda[:, n * KD + k:n * KD + k + 1],
                                                   in1=rstd[:, n * T:(n + 1) * T], op0=ALU.mult, op1=ALU.mult).then_inc(scaled, 1)
            dve.wait_ge(mixb_ready, 3)
            dve.wait_ge(lora_squared, 2)
            nc.vector.tensor_copy(cqT, bank[3][:, :].rearrange("p (a b) -> p a b", a=2)).then_inc(cq_taken, 1)
            nc.vector.tensor_copy(ckvT, bank[4][:, :]).then_inc(kv_taken, 1)
            nc.vector.tensor_copy(krT[0:QK, :], bank[5][0:QK, :]).then_inc(kv_taken, 1)
            dve.wait_ge(cq_taken, 1)
            dve.wait_ge(kv_taken, 2)
            dve.wait_ge(lora_root, 2)
            link(nc.vector.reciprocal(rstd[:, 0:T], rstd[:, 0:T]))
            for k in range(2):
                nc.vector.scalar_tensor_tensor(out=cqT[:, k, :], in0=cqT[:, k, :], scalar=V("cq_g")[:, k:k + 1],
                                               in1=rstd[:, 0:T], op0=ALU.mult, op1=ALU.mult).then_inc(lora_ready, 1)
            link(nc.vector.reciprocal(lora_sq[:, 1, :], lora_sq[:, 1, :]))
            nc.vector.scalar_tensor_tensor(out=ckvT, in0=ckvT, scalar=V("ckv_g"), in1=lora_sq[:, 1, :],
                                           op0=ALU.mult, op1=ALU.mult).then_inc(lora_ready, 1)
            take_rows(1)
            take_ada(1)
            dve.wait_ge(rope_in, 16)

            def roped(target, turned, tmp, cols):
                r = slice(NOPE, QK)
                cos, sin = rope[r, 0, :], rope[r, 1, :]
                for c in range(cols):
                    last = nc.vector.tensor_tensor(tmp[r, c * T:(c + 1) * T], turned[r, c * T:(c + 1) * T], sin, ALU.mult)
                for c in range(cols):
                    last = nc.vector.tensor_tensor(target(c), target(c), cos, ALU.mult)
                link(last)
                for c in range(cols):
                    last = nc.vector.tensor_tensor(target(c), target(c), tmp[r, c * T:(c + 1) * T], ALU.add)
                return last

            for n, (kind, p) in enumerate(PREP):
                if PREP_BY[n] != "dve":
                    continue
                dve.wait_ge(prep_ready, n + 1)
                b = bank[n % NPREP]
                if kind == "kr":
                    ins = roped(lambda c: krT[NOPE:QK, 0:T], b, rope_tmp, 1)
                    ins.then_inc(kr_roped, 1)
                    dve.wait_ge(kr_roped, 1)
                    nc.vector.memset(small[:, 30:31], 0.0).then_inc(prep_dve, 1)
                elif kind == "rot":
                    roped(lambda c: queries[NOPE:QK, 2 * p + c, :], b, rope_tmp, 2).then_inc(prep_dve, 1)
                    dve.wait_ge(prep_dve, PREP_BY[:n + 1].count("dve"))
                else:
                    nc.vector.tensor_copy(values[:, p, :], b[:, :]).then_inc(prep_dve, 1)

            def attended(hd):
                dve.wait_ge(pv_ready, hd + 1)
                if hd == 0:
                    dve.wait_ge(pooled, NG)
                lo = (hd % 2) * VD
                nc.vector.tensor_copy(mixed[lo:lo + VD, hd // 2, :], bank[5][lo:lo + VD, 0:T]).then_inc(pv_taken, 1)

            def normalised(n):
                dve.wait_ge(exp_ready, n + 1)
                link(nc.vector.reciprocal(small[:, 48 + n:49 + n], small[:, 48 + n:49 + n]))
                nc.vector.tensor_scalar(probs[:, n % 4, :], probs[:, n % 4, :], small[:, 48 + n:49 + n], None,
                                        ALU.mult).then_inc(probs_ready, 1)

            for n in range(len(ITEMS)):
                dve.wait_ge(scores_ready, n + 1)
                link(nc.vector.tensor_reduce(small[:, 32 + n:33 + n], bank[n % 3][:, :], AX_X, ALU.max))
                nc.vector.tensor_scalar(small[:, 32 + n:33 + n], small[:, 32 + n:33 + n], -SCALE, None,
                                        ALU.mult).then_inc(max_ready, 1)
                if n >= 1:
                    normalised(n - 1)
                if n >= 6 and n % 2 == 0:
                    attended((n - 6) // 2)
                if n in ADA_TAKES:
                    (take_rows if ADA_TAKES[n] % 1 == 0 else take_ada)(int(ADA_TAKES[n]))
            normalised(len(ITEMS) - 1)
            for hd in range(5, HEADS):
                attended(hd)
            take_ada(3)
            modulation(2, "ffn_g", 0, 0, 4)
            modulation(3, "mix_g", KD, 1, 1)
            add_projected(0, 0, 0, 2)
            reciprocal(1, T)
            for k in range(KD):
                nc.vector.scalar_tensor_tensor(out=h[:, k, :], in0=x[:, k, :], scalar=moda[:, 2 * KD + k:2 * KD + k + 1],
                                               in1=rstd[:, 0:T], op0=ALU.mult, op1=ALU.mult).then_inc(scaled, 1)
            dve.wait_ge(scaled, 16 + KD)
            for k in range(KD):
                dve.wait_ge(h_high, k + 1)
                at = 2 * (KD * 3 + k)
                nc.vector.scalar_tensor_tensor(out=h_parts[:, 1, k, :], in0=h[:, k, :], scalar=ada[:, at:at + 1],
                                               in1=plain(h_parts[:, 0, k, :]), op0=ALU.add, op1=ALU.subtract).then_inc(h_low, 1)
            take_rows(4)
            take_ada(4)

            for q in range(len(DENSE)):
                coming = q - SPLITS_DENSE
                if coming >= 0 and DENSE[coming][0] == "w3":
                    g = DENSE[coming][1]
                    dve.wait_ge(gate_ready, g + 1)
                    dve.wait_ge(used, coming + 1)
                    if g >= 1:
                        dve.wait_ge(hidden_high, g)
                        dve.wait_ge(hidden_low, g)
                    nc.vector.tensor_tensor(hidden_tmp, gate_tmp[:, g % 2],
                                            bank[2 * (g % 2) + 1][:, :].rearrange("p (a b) -> p a b", a=2),
                                            ALU.mult).then_inc(hidden_ready, 1)
                dve.wait_ge(high_ready, q + 1)
                nc.vector.tensor_tensor(low_d[:, q % SPLITS_DENSE, :], piece_view(q), plain(high_d[:, q % SPLITS_DENSE, :]),
                                        ALU.subtract).then_inc(low_ready, 1)
                if q % 2 or q == len(DENSE) - 1:
                    u = first_unit["ffn"] + q // 2
                    dve.wait_ge(low_ready, q + 1)
                    dve.sem_inc(unit_free[unit_slot(u)], 1)
                if coming >= 0 and DENSE[coming][0] == "w3":
                    dve.wait_ge(hidden_high, g + 1)
                    nc.vector.tensor_tensor(hidden_parts[g % 2][:, 1], hidden_tmp, plain(hidden_parts[g % 2][:, 0]),
                                            ALU.subtract).then_inc(hidden_low, 1)
            dve.wait_ge(used, len(DENSE))
            add_projected(None, 4, 0, 5)
            reciprocal(2, T)
            scale(x, h, 3)
            take_rows(5)
            take_ada(5)
            modulation(4, "ffn_g", KD, 1, 4)
            for f in range(1, 8, 2):
                dve.wait_ge(spec_ready, f + 1)
                nc.vector.tensor_copy(spectrum[:, f // NG, f % NG, :], bank[2 + f % 4][:, :]).then_inc(spec_dve, 1)
            for f in (1, 3):
                dve.wait_ge(four_ready, f + 1)
                nc.vector.tensor_copy(fourier[:, 2 * f:2 * f + 2, :],
                                      bank[(6, 7, 0, 1)[f]][:, :].rearrange("p (a b) -> p a b", a=2)).then_inc(four_dve, 1)
            add_projected(1, 2, 1, 2)
            reciprocal(3, T)
            scale(x, h, 4)
            for f in (1, 3):
                dve.wait_ge(tok_ready, f + 1)
                nc.vector.tensor_copy(h_tok[:, f // 2, 512:1024], bank[f][:, :]).then_inc(tok_dve, 1)

            dve.wait_ge(logits_ready, 1)

            def cols(at, n):
                return small[:, at:at + n]

            for t in range(2):
                logit, best, key, hot1, hot2 = (cols(72 + 56 * t + 8 * j, 8) for j in range(5))
                top1, top2, kmin = (cols(72 + 56 * t + 40 + j, 1) for j in range(3))
                link(nc.vector.tensor_copy(logit, bank[4][:, 8 * t:8 * t + 8]))
                for hot, top in ((hot1, top1), (hot2, top2)):
                    link(nc.vector.tensor_reduce(top, logit, AX_X, ALU.max))
                    link(nc.vector.tensor_scalar(best, logit, top, None, ALU.is_equal))
                    link(nc.vector.scalar_tensor_tensor(out=key, in0=best, scalar=-64.0, in1=C("iota8"),
                                                        op0=ALU.mult, op1=ALU.add))
                    link(nc.vector.tensor_reduce(kmin, key, AX_X, ALU.min))
                    link(nc.vector.tensor_scalar(hot, key, kmin, None, ALU.is_equal))
                    if hot is hot1:
                        link(nc.vector.scalar_tensor_tensor(out=logit, in0=hot, scalar=-3e38, in1=logit,
                                                            op0=ALU.mult, op1=ALU.add))
                link(nc.vector.tensor_tensor(cols(184 + 8 * t, 8), hot1, hot2, ALU.add))
                nc.vector.tensor_scalar(cols(224 + 8 * t, 8), cols(184 + 8 * t, 8), float(D), None, ALU.mult).then_inc(mask_ready, 1)
                nc.vector.tensor_tensor(cols(64 + t, 1), top2, top1, ALU.subtract).then_inc(gap_ready, 1)
            for t in range(2):
                _, best, key, hot1, hot2 = (cols(72 + 56 * t + 8 * j, 8) for j in range(5))
                odds, share1, share2 = cols(66 + t, 1), cols(72 + 56 * t + 43, 1), cols(72 + 56 * t + 44, 1)
                dve.wait_ge(odds_ready, t + 1)
                link(nc.vector.tensor_scalar(share1, odds, 1.0, None, ALU.add))
                link(nc.vector.reciprocal(share1, share1))
                link(nc.vector.tensor_tensor(share2, odds, share1, ALU.mult))
                link(nc.vector.tensor_scalar(best, hot1, share1, None, ALU.mult))
                link(nc.vector.scalar_tensor_tensor(out=best, in0=hot2, scalar=share2, in1=best,
                                                    op0=ALU.mult, op1=ALU.add))
                for r in range(MAX_ROUNDS + 1):
                    link(nc.vector.tensor_copy(gate_at[:, t, EXPERTS * r:EXPERTS * (r + 1)], best))
            dve.wait_ge(rank_ready, 1)
            for t in range(2):
                key = cols(72 + 56 * t + 16, 8)
                link(nc.vector.scalar_tensor_tensor(out=key, in0=bank[5][:, 8 * t:8 * t + 8], scalar=1.0,
                                                    in1=cols(184 + 8 * t, 8), op0=ALU.add, op1=ALU.mult))
                for r in range(MAX_ROUNDS + 1):
                    link(nc.vector.tensor_scalar(rank_at[:, t, EXPERTS * r:EXPERTS * (r + 1)], key,
                                                 -1.0 - CAP * r, None, ALU.add))
            full, more = cols(200, 1), cols(201, MAX_ROUNDS - 1)
            link(nc.vector.tensor_reduce(full, bank[5][:, 16:24], AX_X, ALU.max))
            for r in range(1, MAX_ROUNDS):
                link(nc.vector.tensor_scalar(cols(200 + r, 1), full, CAP * r + 0.5, None, ALU.is_gt))
            link(nc.vector.tensor_reduce(cols(210, 1), more, AX_X, ALU.add))
            link(nc.vector.tensor_scalar(cols(211, 1), cols(210, 1), float(EXPERTS), float(EXPERTS), ALU.mult, ALU.add))
            link(nc.vector.tensor_scalar(cols(212, 1), cols(210, 1), 1.0, None, ALU.add))
            link(nc.vector.tensor_copy(loops[:, :], cols(211, 2)))
            nc.vector.memset(small[:, 31:32], 0.0).then_inc(loops_ready, 1)

            def picks(i, target, sem_out, gated):
                for t in range(2):
                    if gated:
                        ins = nc.vector.tensor_scalar(target[:, t, :], C("iota"), rank_at[:, t, bass.ds(i, 1)],
                                                      gate_at[:, t, bass.ds(i, 1)], ALU.is_equal, ALU.mult)
                    else:
                        ins = nc.vector.tensor_scalar(target[:, t, :], C("iota"), rank_at[:, t, bass.ds(i, 1)], None,
                                                      ALU.is_equal)
                ins.then_inc(sem_out, 1)

            def take_gathered(i):
                dve.wait_ge(x_high, i + 1)
                for n in range(2):
                    ins = nc.vector.tensor_tensor(x_parts[:, 1, 4 * n:4 * n + 4, :],
                                                  bank[5 + n][:, 0:4 * CAP].rearrange("p (a b) -> p a b", a=4),
                                                  plain(x_parts[:, 0, 4 * n:4 * n + 4, :]), ALU.subtract)
                ins.then_inc(x_low, 1)

            def take_y(done):
                dve.wait_ge(e_used, PIECES * done)
                nc.vector.tensor_copy(y_tok[:, 512:1024], bank[3][0:CAP, :]).then_inc(y_dve, 1)

            def add_part(pair, last_turn=False):
                for k in (2 * pair, 2 * pair + 1):
                    at = 96 + 2 * (KD * 5 + k)
                    ins = nc.vector.scalar_tensor_tensor(out=x[:, k, :], in0=bank[5 + pair % 3][:, (k % 2) * T:(k % 2) * T + T],
                                                   scalar=ada[:, at:at + 1], in1=x[:, k, :],
                                                   op0=ALU.mult, op1=ALU.add)
                    if last_turn:
                        ins.then_inc(residual, 1)
                if not last_turn:
                    ins.then_inc(part_added[pair], 1)

            def hidden_rest(i, b):
                dve.wait_ge(e_hidden_high, BLOCKS * i + (b + 1))
                nc.vector.tensor_tensor(hidden_e_parts[:, 1], bank[4][:, 0:4 * CAP].rearrange("p (a b) -> p a b", a=4),
                                        plain(hidden_e_parts[:, 0]), ALU.subtract).then_inc(e_hidden_low, 1)

            def expert(i):
                first = isinstance(i, int)
                for q in range(PIECES):
                    s = q % PIECE_SLOTS
                    done = EXPERT[q - SPLITS] if q >= SPLITS else None
                    if done and done[0] == "w3" and done[2] == 1:
                        b = done[1]
                        dve.wait_ge(e_gate, BLOCKS * i + (b + 1))
                        dve.wait_ge(e_used, PIECES * i + (q - SPLITS + 1))
                        if not (first and b == 0):
                            dve.wait_ge(e_turned, BLOCKS * i + b)
                        nc.vector.tensor_tensor(hidden_e, gate_e, bank[1][0:CAP, :], ALU.mult).then_inc(e_hidden, 1)
                    dve.wait_ge(e_high, PIECES * i + (q + 1))
                    nc.vector.tensor_tensor(low_e[:, q % SPLITS, :], ring[:, s * PIECE:(s + 1) * PIECE],
                                            plain(high_e[:, q % SPLITS, :]), ALU.subtract).then_inc(e_low, 1)
                    if q == 2 and not first:
                        take_y(i)
                    if q == hidden_at(0):
                        hidden_rest(i, 0)
                    if done and done[0] == "w2" and done[2] == 1 and done[1] + 1 < BLOCKS:
                        hidden_rest(i, done[1] + 1)
                    if not first and q in (9, 11, 13, 15):
                        dve.wait_ge(part_ready[(q - 9) // 2], i)
                        add_part((q - 9) // 2)
                    if q == 20:
                        picks(i, pick_gated, gated_ready, True)
                    if q == 24:
                        picks(i + 1, pick, pick_ready, False)
                hidden_rest(i, BLOCKS - 1)
                take_gathered(i + 1)

            picks(0, pick, pick_ready, False)
            take_gathered(0)
            expert(0)
            turns = dve.value_load(loops[0:1, 0:1], min_val=EXPERTS, max_val=EXPERTS * MAX_ROUNDS)
            with dve.Fori(1, turns) as i:
                expert(i)
            take_y(turns)
            for pair in range(4):
                dve.wait_ge(part_ready[pair], turns)
                add_part(pair, last_turn=True)
            reciprocal(4, T)
            o = view(ring, 0, KD, T)
            for k in range(KD):
                nc.vector.scalar_tensor_tensor(out=o[:, k, :], in0=x[:, k, :], scalar=V("final_g")[:, k:k + 1],
                                               in1=rstd[:, 0:T], op0=ALU.mult, op1=ALU.mult).then_inc(out_ready, 1)

        @block.tensor
        def _(pe):
            mm = nc.tensor.matmul

            def unit(n, cols):
                s = unit_slot(n)
                return view(ring, s * UNIT, KD, cols)

            def ada_unit(part, u):
                n = first_unit[f"ada{part}"] + u
                unit_wait(pe, n)
                if u == 0 and part >= 1:
                    pe.wait_ge(rows_taken, part)
                w = unit(n, 512)
                for k in range(KD):
                    for j in range(4):
                        last = mm(bank[ADA_BANKS[part][0]][32 * j:32 * j + 32, u * P:(u + 1) * P], cond[:, k, :],
                                  w[:, k, j * P:(j + 1) * P], start=(k == 0), stop=(k == KD - 1))
                last.then_inc(ada_done, 1)
                pe.wait_ge(ada_done, 4 * part + u + 1)
                pe.sem_inc(unit_free[unit_slot(n)], 1)
                if u == 3:
                    pe.sem_inc(rows_ready, 1)

            def ada_turn(part):
                pe.wait_ge(rows_taken, part + 1)
                if part >= 1:
                    pe.wait_ge(ada_taken, part)
                for u in range(4):
                    last = nc.tensor.transpose(bank[ADA_BANKS[part][1]][:, u * P:(u + 1) * P],
                                               ada_rows[:, u * P:(u + 1) * P], C("ident"))
                last.then_inc(ada_ready, 1)

            def mean(stage, before, source, out):
                for k in range(KD):
                    if stage:
                        pe.wait_ge(squared, before + k + 1)
                    last = mm(out, C("mean"), source[:, k, :], start=(k == 0), stop=(k == KD - 1))
                last.then_inc(mean_ready, 1)

            def project(name, source, base, ready_sem):
                for n in range(2):
                    u = first_unit[name] + n
                    unit_wait(pe, u)
                    w = unit(u, 512)
                    for j in range(4):
                        c = 4 * n + j
                        for k in range(KD):
                            last = mm(bank[base + c // 2][:, (c % 2) * T:(c % 2) * T + T], w[:, k, j * P:(j + 1) * P],
                                      source[:, k, :], start=(k == 0), stop=(k == KD - 1))
                        if c % 2:
                            last.then_inc(ready_sem, 1)
                    ready_count[0] += 2
                    pe.wait_ge(ready_sem, ready_count[0])
                    pe.sem_inc(unit_free[unit_slot(u)], 1)

            ready_count = [0]

            pe.wait_ge(con_in, 16)
            pe.wait_ge(cond_ready, 1)
            ada_unit(0, 0)
            pe.wait_ge(squared, 2)
            mean(0, 0, square, bank[0][:, :])
            for u in range(1, 4):
                ada_unit(0, u)
            ada_turn(0)
            u = first_unit["mixa"]
            unit_wait(pe, u)
            w = unit(u, 512)
            for c in range(4):
                for k in range(KD):
                    if c == 0:
                        pe.wait_ge(h_ready, 2 * k + 2)
                    last = mm(bank[1 + c // 2][:, (c % 2) * T:(c % 2) * T + T], w[:, k, c * P:(c + 1) * P],
                              h_all[:, k, 0:T], start=(k == 0), stop=(k == KD - 1))
                if c % 2:
                    last.then_inc(mixa_ready, 1)
            pe.wait_ge(mixa_ready, 2)
            pe.sem_inc(unit_free[unit_slot(u)], 1)
            u = first_unit["mixb"]
            unit_wait(pe, u)
            w = unit(u, 416)
            for c in range(2):
                for k in range(KD):
                    last = mm(bank[3][:, c * T:c * T + T], w[:, k, c * P:(c + 1) * P], h_all[:, k, 0:T],
                              start=(k == 0), stop=(k == KD - 1))
            last.then_inc(mixb_ready, 1)
            for k in range(KD):
                last = mm(bank[4][:, :], w[:, k, 256:384], h_all[:, k, :], start=(k == 0), stop=(k == KD - 1))
            last.then_inc(mixb_ready, 1)
            for k in range(KD):
                last = mm(bank[5][0:QK, :], w[:, k, 320:416], h_all[:, k, :], start=(k == 0), stop=(k == KD - 1))
            last.then_inc(mixb_ready, 1)
            pe.wait_ge(mixb_ready, 3)
            pe.sem_inc(unit_free[unit_slot(u)], 1)
            pe.wait_ge(lora_squared, 2)
            for k in range(2):
                last = mm(bank[0][:, 0:T], C("mean"), lora_sq[:, 0, k * T:(k + 1) * T], start=(k == 0), stop=(k == 1))
            last.then_inc(lora_mean, 1)
            pe.wait_ge(mixa_taken, 2)
            mm(bank[1][:, :], C("mean"), lora_sq[:, 1, :], start=True, stop=True).then_inc(lora_mean, 1)
            for u in range(4):
                ada_unit(1, u)
            ada_turn(1)
            pe.wait_ge(attn_in, 16)
            pe.wait_ge(lora_ready, 3)
            pe.wait_ge(kv_taken, 2)
            for n, (kind, p) in enumerate(PREP):
                b = bank[n % NPREP]
                if n >= NPREP:
                    prep_taken(pe, n - NPREP)
                if kind == "kr":
                    last = mm(b[0:QK, 0:T], C("rot")[0:QK, :], krT[0:QK, 0:T], start=True, stop=True)
                elif kind == "q":
                    for j in range(2):
                        hd = 2 * p + j
                        for k in range(2):
                            last = mm(b[0:QK, j * T:(j + 1) * T], w_uq[:, k, hd * QK:(hd + 1) * QK], cqT[:, k, :],
                                      start=(k == 0), stop=(k == 1))
                elif kind == "k":
                    last = mm(b[:, :], w_ukv[:, 0, p * P:(p + 1) * P], ckvT, start=True, stop=True)
                elif kind == "rot":
                    if p == 0:
                        pe.wait_ge(prep_act, 4)
                    last = mm(b[0:QK, :], C("rot")[0:QK, :], queries[0:QK, 2 * p:2 * p + 2, :], start=True, stop=True)
                else:
                    last = mm(b[:, :], ckvT[:, p * P:(p + 1) * P], w_ukv[:, 1, :], start=True, stop=True)
                last.then_inc(prep_ready, 1)

            pe.wait_ge(prep_act, PREP_BY.count("act"))
            pe.wait_ge(prep_dve, PREP_BY.count("dve"))
            pe.wait_ge(kr_spread, HEADS)

            def turn(n):
                pe.wait_ge(probs_ready, n + 1)
                if n >= 2:
                    pe.wait_ge(probsT_taken, n - 1)
                for kt in range(4):
                    last = nc.tensor.transpose(bank[3 + n % 2][:, kt * P:(kt + 1) * P],
                                               probs[:, n % 4, kt * P:(kt + 1) * P], C("ident"))
                last.then_inc(probsT_ready, 1)

            def attend(hd):
                pe.wait_ge(probsT_taken, 2 * hd + 2)
                if hd >= 1:
                    pe.wait_ge(pv_taken, hd)
                lo = (hd % 2) * VD
                for kt in range(4):
                    last = mm(bank[5][lo:lo + VD, 0:T], values[:, kt, hd * VD:(hd + 1) * VD], probsT[:, hd % 2, kt, :],
                              start=(kt == 0), stop=(kt == 3))
                last.then_inc(pv_ready, 1)

            for n, (hd, q) in enumerate(ITEMS):
                if n >= 3:
                    pe.wait_ge(exp_ready, n - 2)
                mm(bank[n % 3][:, :], queries[0:QK, hd, q * P:(q + 1) * P], keys[0:QK, hd, :],
                   start=True, stop=True).then_inc(scores_ready, 1)
                if n >= 2:
                    turn(n - 2)
                if n >= 4 and n % 2 == 0:
                    attend((n - 4) // 2)
                if n in ADA_ITEMS:
                    ada_unit(*ADA_ITEMS[n])
                if n == 9:
                    ada_turn(2)
            for n in range(len(ITEMS) - 2, len(ITEMS)):
                turn(n)
            attend(HEADS - 2)
            ada_turn(3)
            attend(HEADS - 1)
            pe.wait_ge(pooled, NG)
            pe.wait_ge(probsT_taken, len(ITEMS))
            for g, wnd in enumerate(WINDOWS):
                src = (pool1 if g % 2 == 0 else pool2)[:, g, PAD - wnd // 2:PAD - wnd // 2 + T]
                last = mm(bank[3 + g // 2][:, (g % 2) * T:(g % 2) * T + T], pool_w[:, g, :], src, start=True, stop=True)
                if g % 2:
                    last.then_inc(pool_ready, 1)
            pe.wait_ge(pool_taken, NG)
            pe.wait_ge(pv_taken, HEADS)
            project("mixout", mixed, 0, proj_ready)
            for u in range(4):
                ada_unit(4, u)
                if u == 1:
                    mean(1, 2, square_l, bank[5][:, 0:T])
            ada_turn(4)
            for q, (kind, g) in enumerate(DENSE):
                high, low = (view(split, n * PIECE + (q % SPLITS_DENSE) * PIECE, PIECE) for n in (0, SPLITS_DENSE))
                pe.wait_ge(high_ready, q + 1)
                if kind == "w2":
                    pe.wait_ge(hidden_low, g + 1)
                    if g == 0:
                        pe.wait_ge(ada_taken, 5)
                elif g >= 2:
                    pe.wait_ge(hidden_ready, g - 1)
                for n, (w, right) in enumerate(((high, 0), (high, 1), (low, 0))):
                    if n == 2:
                        pe.wait_ge(low_ready, q + 1)
                    if kind == "w2":
                        w = w.rearrange("p (a b) -> p a b", a=2)
                        for j in range(2):
                            for k in range(KD):
                                last = mm(bank[4 + k // 2][:, (k % 2) * T:(k % 2) * T + T], w[:, j, k * P:(k + 1) * P],
                                          hidden_parts[g % 2][:, right, j, :],
                                          start=(g == 0 and n == 0 and j == 0 and k % 2 == 0),
                                          stop=(g == GROUPS - 1 and n == 2 and j == 1), skip_group_check=True)
                    else:
                        w = w.rearrange("p (a b) -> p a b", a=KD)
                        for j in range(2):
                            for k in range(KD):
                                if q == 0 and n < 2 and j == 0:
                                    pe.wait_ge(h_low if n else h_high, k + 1)
                                last = mm(bank[2 * (g % 2) + (kind == "w3")][:, j * T:(j + 1) * T],
                                          w[:, k, j * P:(j + 1) * P], h_parts[:, right, k, :],
                                          start=(n == 0 and j == 0 and k == 0), stop=(n == 2 and k == KD - 1),
                                          skip_group_check=True)
                last.then_inc(used, 1)
            pe.wait_ge(hidden_ready, GROUPS)
            for u in range(4):
                ada_unit(5, u)
                if u == 1:
                    mean(2, 2 + KD, square_l, bank[2][:, 0:T])
            ada_turn(5)
            u = first_unit["dft"]
            unit_wait(pe, u)
            chan = view(ring, unit_slot(u) * UNIT, 2, 2 * GC)
            rows = view(ring, unit_slot(u) * UNIT + 4 * GC, 2, 2, T)
            pe.wait_ge(h_ready, 24)
            for f in range(8):
                t, g = f // NG, f % NG
                if f >= 4:
                    pe.wait_ge(spec_dve if f % 2 else spec_act, f // 2 - 1)
                for k in range(2):
                    last = mm(bank[2 + f % 4][:, :], h[:, 2 * g + k, t * P:(t + 1) * P], chan[:, k, :],
                              start=(k == 0), stop=(k == 1))
                last.then_inc(spec_ready, 1)
            pe.wait_ge(spec_act, 4)
            pe.wait_ge(spec_dve, 4)
            pe.wait_ge(ada_taken, 6)
            for c in range(KD):
                n = 0
                for t in range(2):
                    for part in range(2):
                        at = part * GC + (c % 2) * P
                        last = mm(bank[(6, 7, 0, 1)[c // 2]][:, (c % 2) * T:(c % 2) * T + T],
                                  spectrum[:, t, c // 2, at:at + P], rows[:, part, t, :], start=(n == 0), stop=(n == 3))
                        n += 1
                if c % 2:
                    last.then_inc(four_ready, 1)
            pe.wait_ge(four_ready, 4)
            pe.sem_inc(unit_free[unit_slot(u)], 1)
            pe.wait_ge(four_act, 2)
            pe.wait_ge(four_dve, 2)
            project("fnet", fourier, 2, proj_ready)
            mean(3, 2 + 2 * KD, square_l, bank[6][:, 0:T])
            pe.wait_ge(router_in, 16)
            pe.wait_ge(h_ready, 32)
            for t in range(2):
                for k in range(KD):
                    last = mm(bank[4][:, 8 * t:8 * t + 8], h[:, k, t * P:(t + 1) * P], router[:, k, :],
                              start=(k == 0), stop=(k == KD - 1))
            last.then_inc(logits_ready, 1)
            for f in range(4):
                for j in range(4):
                    last = nc.tensor.transpose(bank[f][:, j * P:(j + 1) * P],
                                               h[:, 4 * (f % 2) + j, (f // 2) * P:(f // 2 + 1) * P], C("ident"))
                last.then_inc(tok_ready, 1)
            pe.wait_ge(tok_ready, 4)
            pe.sem_inc(scratch_free, 1)
            pe.wait_ge(mask_ready, 2)
            m0, m1, all0, all1 = (small[:, at:at + 8] for at in (184, 192, 224, 232))
            mm(bank[5][:, 0:8], C("before"), m0, start=True, stop=True)
            mm(bank[5][:, 8:16], C("mean"), all0, start=True, stop=False)
            mm(bank[5][:, 8:16], C("before"), m1, start=False, stop=True)
            mm(bank[5][:, 16:24], C("mean"), all0, start=True, stop=False)
            mm(bank[5][:, 16:24], C("mean"), all1, start=False, stop=True).then_inc(rank_ready, 1)

            def gather(i):
                pe.wait_ge(pick_ready, i + 1)
                for k in range(KD):
                    for t in range(2):
                        last = mm(bank[5 + k // 4][:, (k % 4) * CAP:(k % 4 + 1) * CAP], h_tok[:, t, k * P:(k + 1) * P],
                                  pick[:, t, :], start=(t == 0), stop=(t == 1))
                last.then_inc(gathered, 1)

            def combine(done, pair):
                if pair == 0:
                    pe.wait_ge(y_act, done)
                    pe.wait_ge(y_dve, done)
                    pe.wait_ge(spread_taken, done)
                for k in (2 * pair, 2 * pair + 1):
                    last = mm(bank[5 + pair % 3][:, (k % 2) * T:(k % 2) * T + T],
                              y_tok[:, k * P:(k + 1) * P], spread, start=True, stop=True)
                last.then_inc(part_ready[pair], 1)

            def expert(i):
                first = isinstance(i, int)
                pe.wait_ge(x_high, i + 1)
                for q, (kind, b, half) in enumerate(EXPERT):
                    high = view(split, (q % SPLITS) * PIECE, PIECE)
                    low = view(split, (SPLITS + q % SPLITS) * PIECE, PIECE)
                    pe.wait_ge(e_high, PIECES * i + (q + 1))
                    if kind == "w2":
                        if half == 0:
                            pe.wait_ge(e_hidden_low, BLOCKS * i + (b + 1))
                            if b == 0 and not first:
                                pe.wait_ge(y_act, i)
                                pe.wait_ge(y_dve, i)
                    elif half == 0 and not (first and b == 0):
                        pe.wait_ge(e_gate if kind == "w1" else e_hidden, BLOCKS * i + b)
                    for n, (w, right) in enumerate(((high, 0), (high, 1), (low, 0))):
                        if n == 1 and q == 0:
                            pe.wait_ge(x_low, i + 1)
                        if n == 2:
                            pe.wait_ge(e_low, PIECES * i + (q + 1))
                        if kind == "w2":
                            w = w.rearrange("p (a b) -> p a b", a=2)
                            for j in range(2):
                                for m in range(2):
                                    last = mm(bank[2 + m][0:CAP, :], hidden_e_parts[:, right, 2 * half + j, :],
                                              w[:, j, m * 512:(m + 1) * 512], start=(b == 0 and half == 0 and n == 0 and j == 0),
                                              stop=(b == BLOCKS - 1 and half == 1 and n == 2 and j == 1))
                        else:
                            w = w.rearrange("p (a b) -> p a b", a=4)
                            for k in range(4):
                                last = mm(bank[kind == "w3"][0:CAP, :], x_parts[:, right, 4 * half + k, :], w[:, k, :],
                                          start=(half == 0 and n == 0 and k == 0), stop=(half == 1 and n == 2 and k == 3))
                    last.then_inc(e_used, 1)
                    if q == 4 or (kind == "w2" and half == 0 and b + 1 < BLOCKS):
                        turned = 0 if q == 4 else b + 1
                        pe.wait_ge(e_hidden, BLOCKS * i + (turned + 1))
                        for j in range(4):
                            last = nc.tensor.transpose(bank[4][:, j * CAP:(j + 1) * CAP], hidden_e[:, j * P:(j + 1) * P],
                                                       C("ident")[0:CAP, 0:CAP])
                        last.then_inc(e_turned, 1)
                    if not first and q in (5, 7, 9, 11):
                        if q == 11:
                            pe.wait_ge(part_added[0], i)
                        combine(i, (q - 5) // 2)
                    if q == 24:
                        pe.wait_ge(gated_ready, i + 1)
                        if not first:
                            pe.wait_ge(part_added[2], i)
                        for t in range(2):
                            last = nc.tensor.transpose(bank[7][0:CAP, t * P:(t + 1) * P], pick_gated[:, t, :], C("ident"))
                        last.then_inc(spread_turned, 1)
                    if q == PIECES - 3:
                        gather(i + 1)

            pe.wait_ge(tok_act, 2)
            pe.wait_ge(tok_dve, 2)
            pe.wait_ge(loops_ready, 1)
            gather(0)
            expert(0)
            turns = pe.value_load(loops[0:1, 0:1], min_val=EXPERTS, max_val=EXPERTS * MAX_ROUNDS)
            with pe.Fori(1, turns) as i:
                expert(i)
            pe.wait_ge(x_low, turns + 1)
            for pair in range(4):
                if pair == 3:
                    pe.wait_ge(residual, 3 * KD + 2)
                combine(turns, pair)
            mean(4, 2 + 3 * KD, square_l, bank[0][:, 0:T])


def kernel(**inputs):
    import concourse.bacc as _bacc
    from concourse.bass_utils import run_bass_kernel_spmd as _run

    a = {k: np.asarray(v) for k, v in inputs.items()}

    def chunks(v):
        return v.reshape(-1, P).T

    def rows(w, cols):
        return w.reshape(KD, P, -1, cols).transpose(2, 1, 0, 3).reshape(-1, P, KD * cols)

    def dense(w1, w3, w2):
        of = {"w1": rows(w1, PAIR), "w3": rows(w3, PAIR),
              "w2": w2.reshape(GROUPS, 2, P, D).transpose(0, 2, 1, 3).reshape(GROUPS, P, PIECE)}
        return np.concatenate([of[w][g] for w, g in DENSE], axis=1)

    def expert(w1, w3, w2):
        of = {"w1": w1.reshape(2, 4, P, BLOCKS, BLOCK).transpose(3, 0, 2, 1, 4).reshape(BLOCKS, 2, P, PIECE),
              "w3": w3.reshape(2, 4, P, BLOCKS, BLOCK).transpose(3, 0, 2, 1, 4).reshape(BLOCKS, 2, P, PIECE),
              "w2": w2.reshape(BLOCKS, 2, 2, P, D).transpose(0, 1, 3, 2, 4).reshape(BLOCKS, 2, P, PIECE)}
        return np.stack([of[w][b, n] for w, b, n in EXPERT])

    con, rope, dft = constants()
    vec = np.concatenate([
        *[chunks(a["norm_mix_g"][i]) for i in range(2)], *[chunks(a["norm_ffn_g"][i]) for i in range(2)],
        chunks(a["final_g"]), chunks(a["cq_norm_g"][0]), chunks(a["ckv_norm_g"][0]), chunks(a["pool_scale"][0]),
        *[chunks(a["ada_b"][i]) for i in range(2)],
        np.stack([chunks(a["c"][0]), chunks(a["c_ctx"])], axis=2).reshape(P, 2 * KD)], axis=1)
    w_in = a["mix_in_w"][0]
    low = Q_LORA + KV_LORA + ROPE
    ukv = a["w_ukv"][0].reshape(KV_LORA, HEADS, 2, VD).transpose(0, 2, 1, 3).reshape(KV_LORA, -1)
    attn = np.concatenate([
        a["w_uq"][0].reshape(2, P, -1).transpose(1, 0, 2).reshape(P, -1), ukv,
        a["pool_w"][0].transpose(1, 0, 2).reshape(P, -1)], axis=1)
    arrays = {
        "vec": vec, "con": con, "rope": rope,
        "x": a["x"][0].T.reshape(KD, P, T).transpose(1, 0, 2).reshape(P, -1),
        "ctx": a["ctx"][0].T.reshape(KD, P, TC).transpose(1, 0, 2),
        "ada": np.stack([rows(a["ada_w"][i], 512) for i in range(2)]),
        "mixa": rows(w_in[:, low:], 512)[0], "mixb": rows(w_in[:, :low], low)[0],
        "attn": attn, "mixout": rows(a["mix_out_w"][0], 512),
        "ffn": dense(a["ffn_w1"][0], a["ffn_w3"][0], a["ffn_w2"][0]),
        "dft": dft, "fnet": rows(a["fnet_out_w"][0], 512),
        "router": a["router_w"][0].reshape(KD, P, EXPERTS).transpose(1, 0, 2).reshape(P, -1),
        "moe": np.stack([expert(a["moe_w1"][0, e], a["moe_w3"][0, e], a["moe_w2"][0, e]) for e in range(EXPERTS)]),
    }
    nc = _bacc.Bacc("TRN2", target_bir_lowering=False, num_devices=1)
    given, args = {}, []
    for name, v in arrays.items():
        v = np.ascontiguousarray(v)
        given[f"in_{name}"] = v
        args.append(nc.dram_tensor(f"in_{name}", v.shape, mybir.dt.from_np(v.dtype), kind="ExternalInput").ap())
    args.append(nc.dram_tensor("out_xT", (P, KD * T), F32, kind="ExternalOutput").ap())
    build(nc, *args)
    r = _run(nc, [given], core_ids=[0])
    out = r.results[0]["out_xT"]
    return out.reshape(P, KD, T).transpose(2, 1, 0).reshape(1, T, D)
```

```python
import math
from contextlib import ExitStack

import numpy as np

import concourse.bass as bass
from concourse import mybir

F32 = mybir.dt.float32
F32R = mybir.dt.float32r
I32 = mybir.dt.int32
ALU = mybir.AluOpType
ACT = mybir.ActivationFunctionType
AX_X = mybir.AxisListType.X

P = 128
D = 1024
KD = D // P
T = 256
TC = 256
TA = T + TC
GRID_W = 64
HEADS, NOPE, ROPE, VD = 8, 64, 32, 64
QK = NOPE + ROPE
Q_LORA, KV_LORA = 256, 128
WINDOWS = (2, 4, 8, 16)
NG = 4
GC = D // NG
F_DENSE, F_EXPERT, EXPERTS = 2816, 3584, 8
PAIR = 2 * P
GROUPS = F_DENSE // PAIR
BLOCK = 4 * P
BLOCKS = F_EXPERT // BLOCK
SCALE = float(QK) ** -0.5
EPS = 1e-6

CAP = 96
MAX_ROUNDS = -(-T // CAP)
TABLE = EXPERTS * (MAX_ROUNDS + 1)

UNIT = KD * 512
UNIT_SLOTS = 3
PIECE = 2048
PIECE_SLOTS = 14
RING = PIECE_SLOTS * PIECE
SCRATCH = UNIT_SLOTS * UNIT
ADA_UNITS = 6 * D // 512
PARTS = 3
SPLITS = 3
SPLITS_DENSE = 2
MIXER_BUFFERS = 3
PRODUCTS = ((0, 0), (0, 1), (1, 0))
PAD = 8
PADDED = T + 2 * PAD

VEC = {}
_at = 0
for _name, _n in (("mix_g", 16), ("ffn_g", 16), ("final_g", 8), ("cq_g", 2), ("ckv_g", 1), ("pool_scale", 4),
                  ("ada_b", 96), ("cond", 16)):
    VEC[_name] = (_at, _at + _n)
    _at += _n
VECS = _at

CON = {}
_at = 0
for _name, _n in (("ident", P), ("mean", P), ("before", P), ("rot", QK), ("iota8", EXPERTS),
                  ("iota", CAP), ("edge", NG * 2 * PAD), ("first_slot", MAX_ROUNDS + 1), ("eps", 1)):
    CON[_name] = (_at, _at + _n)
    _at += _n
CONS = _at


def dense_pieces():
    order = []
    for g in range(GROUPS):
        order += [("w1", g), ("w3", g)] + ([("w2", g - 1)] if g else [])
    return order + [("w2", GROUPS - 1)]


def expert_pieces():
    order = []
    for b in range(BLOCKS):
        order += [(w, b, n) for w in ("w1", "w3") for n in range(2)] + ([("w2", b - 1, n) for n in range(2)] if b else [])
    return order + [("w2", BLOCKS - 1, n) for n in range(2)]


DENSE = dense_pieces()
EXPERT = expert_pieces()
PIECES = len(EXPERT)
DENSE_UNITS = -(-len(DENSE) // 2)
ADA_DENSE = {0: ((4, 0), (4, 1)), 2: ((4, 2),), 4: ((4, 3),), 8: ((5, 2),), 10: ((5, 3),)}


def constants():
    con = np.zeros((P, CONS), np.float32)

    def put(name, a):
        con[:a.shape[0], CON[name][0]:CON[name][1]] = a

    put("ident", np.eye(P))
    put("mean", np.full((P, P), 1.0 / D))
    put("before", np.triu(np.ones((P, P)), 1))
    rot = np.zeros((QK, QK))
    half = ROPE // 4
    for b in (NOPE, NOPE + ROPE // 2):
        for j in range(half):
            rot[b + half + j, b + j] = -1.0
            rot[b + j, b + half + j] = 1.0
    put("rot", rot)
    put("iota8", np.tile(np.arange(EXPERTS), (P, 1)))
    put("iota", np.tile(np.arange(CAP), (P, 1)))
    put("first_slot", np.tile(1.0 + CAP * np.arange(MAX_ROUNDS + 1), (P, 1)))
    put("eps", np.full((P, 1), EPS))

    t = np.arange(T)
    inv = (1.0 / (np.float32(10000.0) ** (np.arange(0, ROPE // 2, 2, dtype=np.float32) / np.float32(ROPE // 2))))
    inv = inv.astype(np.float32)
    angle = np.zeros((ROPE, T), np.float32)
    for b, position in ((0, t // GRID_W), (ROPE // 2, t % GRID_W)):
        a = inv[:, None] * position.astype(np.float32)[None, :]
        angle[b:b + half] = a
        angle[b + half:b + 2 * half] = a
    rope = np.concatenate([np.cos(angle), np.sin(angle)], axis=1).astype(np.float32)

    edge = np.ones((NG, 2, PAD))
    for g, w in enumerate(WINDOWS):
        count = np.clip(t - w // 2 + w, 0, T) - np.clip(t - w // 2, 0, T)
        edge[g] = w / np.stack([count[:PAD], count[-PAD:]])
    put("edge", np.tile(edge.reshape(1, -1), (P, 1)))

    c = np.arange(GC)
    a = 2.0 * np.pi * ((c[:, None] * c[None, :]) % GC) / GC
    chan = np.concatenate([np.cos(a), np.sin(a)], axis=1).reshape(2, P, 2 * GC).transpose(1, 0, 2).reshape(P, -1)
    a = 2.0 * np.pi * ((t[:, None] * t[None, :]) % T) / T
    norm = 1.0 / math.sqrt(T * GC)
    row = np.stack([np.cos(a) * norm, -np.sin(a) * norm]).reshape(2, 2, P, T).transpose(2, 0, 1, 3).reshape(P, -1)
    dft = np.concatenate([chan, row], axis=1).astype(np.float32)
    return con, rope, dft


def build(nc, vec_d, con_d, rope_d, x_d, ctx_d, ada_d, mixa_d, mixb_d, attn_d, mixout_d, ffn_d,
          dft_d, fnet_d, router_d, moe_d, out_d):
    ctx = ExitStack()
    with ctx:
        def sb(name, cols, dt=F32):
            return ctx.enter_context(nc.sbuf_tensor(name, [P, cols], dt))

        def sem(name):
            return ctx.enter_context(nc.semaphore(name))

        ring = sb("ring", RING)
        split = sb("split", 6 * PIECE + 2 * KD * CAP + 2 * 4 * CAP + 2 * D + T, F32R)
        xT = sb("xT", KD * T)
        con = sb("con", CONS)
        vec = sb("vec", VECS)
        ada = sb("ada", 2 * 96)
        moda = sb("moda", 5 * KD)
        rstd = sb("rstd", TA)
        small = sb("small", 240)
        loops = sb("loops", 2, I32)
        condp = sb("condp", KD * 32)
        work = sb("work", 3520)
        bank = [ctx.enter_context(nc.psum_tensor(f"bank{b}", [P, 512], F32)) for b in range(8)]

        def view(t, at, *dims):
            n = int(np.prod(dims))
            v = t[:, at:at + n]
            if len(dims) == 2:
                return v.rearrange("p (a b) -> p a b", a=dims[0])
            if len(dims) == 3:
                return v.rearrange("p (a b c) -> p a b c", a=dims[0], b=dims[1])
            return v

        def C(name):
            return con[:, CON[name][0]:CON[name][1]]

        def V(name):
            return vec[:, VEC[name][0]:VEC[name][1]]

        x = view(xT, 0, KD, T)
        cond = view(condp, 0, KD, 32)
        scratch = SCRATCH
        square = view(ring, scratch, KD, TA)
        keys = view(ring, scratch, HEADS, TA)
        h_all = view(ring, scratch + 4096, KD, TA)
        values = view(ring, scratch + 4096, 4, HEADS * VD)
        probs = view(ring, scratch + 6144, 4, TA)
        ctxT = view(ring, scratch + 8192, KD, TC)
        queries = view(ring, scratch + 8192, HEADS, T)
        lora_sq = view(ring, scratch + 10240, 2, 512)
        rope_tmp = view(ring, scratch + 10240, 512)
        probsT = view(ring, scratch + 10240, 2, 4, T)
        h_plain = view(ring, scratch, KD, TA)
        pool0 = view(ring, scratch + 12288, NG, PADDED)
        pool_w = view(ring, scratch + 13376, NG, P)
        pool1 = view(ring, scratch + 4096, NG, PADDED)
        pool2 = view(ring, scratch + 4096 + NG * PADDED, NG, PADDED)
        cqT = view(ring, scratch + 14336, 2, T)
        ckvT = view(ring, scratch + 14848, TA)
        krT = view(ring, scratch + 15360, TA)
        ada_rows = view(ring, scratch + 15872, 512)
        square_l = view(ring, scratch, KD, T)
        h = view(ring, scratch + 4096, KD, T)
        gate_tmp = view(ring, scratch + 6144, 2, 2, T)
        hidden_tmp = view(ring, scratch + 7168, 2, T)
        assert scratch + 16384 == RING
        w_uq = view(work, 0, 2, HEADS * QK)
        w_ukv = view(work, 1536, 2, HEADS * VD)
        rope = view(work, 2560, 2, T)
        router = view(work, 3456, KD, EXPERTS)
        h_tok = view(work, 0, 2, D)
        gate_e = work[0:CAP, 2048:2560]
        hidden_e = work[0:CAP, 2560:3072]
        logits_e = work[0:EXPERTS, 2048:2304]
        pick = view(work, 3072, 2, CAP)
        rank_at = view(work, 3264, 2, TABLE)
        gate_at = view(work, 3328, 2, TABLE)
        assert TABLE == 32 and NG * PADDED == 1088
        slot_gate = small[0:CAP, 27:28]
        high_d = view(split, 0, SPLITS_DENSE, PIECE)
        low_d = view(split, SPLITS_DENSE * PIECE, SPLITS_DENSE, PIECE)
        h_parts = view(split, 4 * PIECE, 2, KD, T)
        hidden_parts = [view(split, 6 * PIECE + n * 2 * 2 * T, 2, 2, T) for n in range(2)]
        h_in = [view(split, n * 4096, KD, TA) for n in range(2)]
        mixed = [view(split, 8192 + n * KD * T, KD, T) for n in range(2)]
        spectrum = [view(split, n * 4096, 2, NG, 2 * GC) for n in range(2)]
        rows_parts = [view(split, 8192 + n * 4 * T, 2, 2, T) for n in range(2)]
        fourier = [view(split, 10240 + n * KD * T, KD, T) for n in range(2)]
        high_e = [view(split, 2 * n * PIECE, PIECE) for n in range(SPLITS)]
        low_e = [view(split, (2 * n + 1) * PIECE, PIECE) for n in range(SPLITS)]
        x_parts = view(split, 6 * PIECE, 2, KD, CAP)
        y_at = 6 * PIECE + 2 * KD * CAP + 2 * 4 * CAP
        y_parts = [split[0:CAP, y_at + n * D:y_at + (n + 1) * D] for n in range(2)]
        spread = split[0:CAP, y_at + 2 * D:y_at + 2 * D + T]
        hidden_e_parts = view(split, 6 * PIECE + 2 * KD * CAP, 2, 4, CAP)

        def plain(ap):
            return ap.bitcast(F32)

        vec_in, con_in, x_in, ctx_in = sem("vec_in"), sem("con_in"), sem("x_in"), sem("ctx_in")
        pool_in = sem("pool_in")
        attn_in, rope_in, router_in = sem("attn_in"), sem("rope_in"), sem("router_in")
        unit_in = [sem(f"unit_in{i}") for i in range(UNIT_SLOTS)]
        unit_free = [sem(f"unit_free{i}") for i in range(UNIT_SLOTS)]
        piece_in = [sem(f"piece_in{i}") for i in range(PIECE_SLOTS)]
        scratch_free = sem("scratch_free")
        cond_ready = sem("cond_ready")
        rows_ready, rows_taken, ada_ready, ada_taken = (
            sem("rows_ready"), sem("rows_taken"), sem("ada_ready"), sem("ada_taken"))
        rows_zero = sem("rows_zero")
        h_high, h_low = sem("h_high"), sem("h_low")
        squared, mean_ready, root_ready = sem("squared"), sem("mean_ready"), sem("root_ready")
        scaled, h_ready = sem("scaled"), sem("h_ready")
        rooted, context_scaled = sem("rooted"), sem("context_scaled")
        gain_ready, in_high, in_low, pool_high = sem("gain_ready"), sem("in_high"), sem("in_low"), sem("pool_high")
        pads_zero = sem("pads_zero")
        mixa_ready, mixa_taken = sem("mixa_ready"), sem("mixa_taken")
        cq_taken, kv_taken = sem("cq_taken"), sem("kv_taken")
        lora_squared, lora_mean, lora_root, lora_ready = (
            sem("lora_squared"), sem("lora_mean"), sem("lora_root"), sem("lora_ready"))
        prep_ready, prep_act, prep_dve = sem("prep_ready"), sem("prep_act"), sem("prep_dve")
        kr_roped, kr_spread, pooled = sem("kr_roped"), sem("kr_spread"), sem("pooled")
        scores_ready, max_ready, exp_ready, probs_ready = (
            sem("scores_ready"), sem("max_ready"), sem("exp_ready"), sem("probs_ready"))
        probsT_ready, probsT_taken = sem("probsT_ready"), sem("probsT_taken")
        pv_ready, pv_taken = sem("pv_ready"), sem("pv_taken")
        pool_ready, pool_taken = sem("pool_ready"), sem("pool_taken")
        proj_ready, residual = sem("proj_ready"), sem("residual")
        high_ready, low_ready, used = sem("high_ready"), sem("low_ready"), sem("used")
        gate_ready, hidden_ready, hidden_high, hidden_low = (
            sem("gate_ready"), sem("hidden_ready"), sem("hidden_high"), sem("hidden_low"))
        mixer_high, mixer_low, mixer_used = sem("mixer_high"), sem("mixer_low"), sem("mixer_used")
        spec_ready, spec_high, spec_low = sem("spec_ready"), sem("spec_high"), sem("spec_low")
        rows_high, rows_low = sem("rows_high"), sem("rows_low")
        four_ready, four_high, four_low = sem("four_ready"), sem("four_high"), sem("four_low")
        logits_ready, logits_taken, logits_turned = sem("logits_ready"), sem("logits_taken"), sem("logits_turned")
        tok_ready, tok_taken, counts_ready = sem("tok_ready"), sem("tok_taken"), sem("counts_ready")
        gap_ready, odds_ready, mask_ready, rank_ready, loops_ready = (
            sem("gap_ready"), sem("odds_ready"), sem("mask_ready"), sem("rank_ready"), sem("loops_ready"))
        pick_ready, gathered, x_high, x_low = sem("pick_ready"), sem("gathered"), sem("x_high"), sem("x_low")
        e_high, e_low, e_used = sem("e_high"), sem("e_low"), sem("e_used")
        e_gate, e_hidden, e_turned, e_hidden_high, e_hidden_low = (
            sem("e_gate"), sem("e_hidden"), sem("e_turned"), sem("e_hidden_high"), sem("e_hidden_low"))
        y_high, y_low = ([sem(f"{name}{n}") for n in range(2)] for name in ("y_high", "y_low"))
        spread_turned, spread_taken = sem("spread_turned"), sem("spread_taken")
        part_ready, part_added = ([sem(f"{name}{pair}") for pair in range(4)] for name in ("part_ready", "part_added"))
        ada_done = sem("ada_done")
        dve_step, pool_step = sem("dve_step"), sem("pool_step")
        out_ready, stored = sem("out_ready"), sem("stored")

        units, first_unit = [], {}

        def add(name, src, cols):
            first_unit.setdefault(name, len(units))
            units.append((src, cols))

        def add_ada(part):
            for u in range(4):
                add(f"ada{part}_{u}", ada_d[part // PARTS, 4 * (part % PARTS) + u], UNIT)

        add_ada(0)
        add("mixa", mixa_d, KD * 512)
        add("mixb", mixb_d, KD * 416)
        for part in (1, 2, 3):
            add_ada(part)
        for n in range(2):
            add("mixout", mixout_d[n], KD * 512)
        for n in range(DENSE_UNITS):
            m = min(2, len(DENSE) - 2 * n)
            if n in ADA_DENSE:
                for part, u in ADA_DENSE[n]:
                    add(f"ada{part}_{u}", ada_d[1, 4 * (part - PARTS) + u], UNIT)
            add(f"ffn{n}", ffn_d[n][:, 0:m * PIECE], m * PIECE)
        for u in range(2):
            add(f"ada5_{u}", ada_d[1, 8 + u], UNIT)
        add("dft", dft_d, 4 * 512)
        for n in range(2):
            add("fnet", fnet_d[n], KD * 512)
        unit_uses = [len(range(s, len(units), UNIT_SLOTS)) for s in range(UNIT_SLOTS)]

        def unit_slot(n):
            return n % UNIT_SLOTS

        def unit_wait(eng, n):
            eng.wait_ge(unit_in[unit_slot(n)], 16 * (n // UNIT_SLOTS + 1))

        def rows_of(run):
            return ada_rows[:, 0:P * len(RUNS[run][1])]

        def piece_view(n):
            u = first_unit[f"ffn{n // 2}"]
            return view(ring, unit_slot(u) * UNIT + (n % 2) * PIECE, PIECE)

        last_slots = [unit_slot(len(units) - n) for n in (3, 2, 1)]
        SLOT_ORDER = [7, 10, 11, 12, 9, 13] + [2 * u + n for u in last_slots for n in range(2)] + [6, 8]
        assert sorted(SLOT_ORDER) == list(range(PIECE_SLOTS))

        PIECES_AFTER = {first_unit[f"ffn{n}"]: (q,) for q, n in enumerate((8, 10, 12, 14))}
        PIECES_AFTER[first_unit["fnet"] + 1] = (4, 5)

        MIXER = {"mixin": [(first_unit[name], k, cols) for name, cols in (("mixa", 512), ("mixb", 416))
                           for k in range(0, KD, 2)]}
        for name in ("mixout", "fnet"):
            MIXER[name] = [(first_unit[name] + n, k, 512) for n in range(2) for k in range(0, KD, 2)]
        MIXER_AT = {"mixin": 8192, "mixout": 0, "fnet": 4096}
        mixer_pieces, first_piece = [], {}
        for name, pieces in MIXER.items():
            first_piece[name] = len(mixer_pieces)
            mixer_pieces += [(u, k, cols, MIXER_AT[name] + 2048 * (n % MIXER_BUFFERS))
                             for n, (u, k, cols) in enumerate(pieces)]

        def mixer_source(m):
            u, k, cols, _ = mixer_pieces[m]
            return view(ring, unit_slot(u) * UNIT + k * cols, 2 * cols)

        def mixer_part(m, n):
            _, _, cols, at = mixer_pieces[m]
            return view(split, at + 1024 * n, 2 * cols)

        dft_at = unit_slot(first_unit["dft"]) * UNIT
        dft_rows = view(ring, dft_at + 4 * GC, 2, 2, T)

        def landed(q):
            return view(ring, SLOT_ORDER[q % PIECE_SLOTS] * PIECE, PIECE)

        MIX_BANKS, FFN_BANKS, FNET_BANKS = (0, 1, 4, 5), (4, 5, 6, 7), (2, 3, 4, 5)
        RUNS = [(part, (0, 1, 2, 3), 6, 7) for part in range(4)] + [(4, (0, 1, 2, 3), 2, 3), (5, (2, 3), 2, 3), (5, (0, 1), 0, 1)]
        ADA_TURNS = {12: 4, 24: 5}
        RUN_OF = {(part, u): n for n, (part, us, _, _) in enumerate(RUNS) for u in us}

        PREP = [("kr", 0)] + [("q", p) for p in range(4)] + [(kind, p) for p in range(4) for kind in ("rot", "k")] \
            + [("v", p) for p in range(4)]
        PREP_BY = ["act" if kind in ("q", "k", "v") else "dve" for kind, _ in PREP]
        NPREP = 6

        def prep_taken(eng, n):
            s = prep_act if PREP_BY[n] == "act" else prep_dve
            eng.wait_ge(s, sum(b == PREP_BY[n] for b in PREP_BY[:n + 1]))

        ITEMS = [(hd, q) for hd in range(HEADS) for q in range(2)]
        ADA_ITEMS = {n: (2 + (n - 1) // 2 // 4, (n - 1) // 2 % 4) for n in range(1, 16, 2)}
        ADA_TAKES = {2: 1.5, 8: 2, 10: 2.5, 15: 3}

        def hidden_at(b):
            return 7

        block = ctx.enter_context(nc.Block())

        @block.sync
        def _(sp):
            def unit_load(n):
                src, cols = units[n]
                s = unit_slot(n)
                if n >= UNIT_SLOTS:
                    sp.wait_ge(unit_free[s], n // UNIT_SLOTS)
                sp.dma_start(ring[:, s * UNIT:s * UNIT + cols], src).then_inc(unit_in[s], 16)

            def slot_free(q):
                slot = SLOT_ORDER[q]
                if slot in (7, 10, 11, 12):
                    sp.wait_ge(mean_ready, 2)
                elif slot == 9:
                    sp.wait_ge(hidden_low, GROUPS)
                elif slot == 13:
                    sp.wait_ge(ada_ready, len(RUNS))
                elif slot < 2 * UNIT_SLOTS:
                    sp.wait_ge(unit_free[slot // 2], unit_uses[slot // 2])
                elif slot == 6:
                    sp.wait_ge(mean_ready, 4)
                else:
                    sp.wait_ge(scratch_free, 1)

            sp.dma_start(vec[:, :], vec_d).then_inc(vec_in, 16)
            sp.dma_start(xT[:, :], x_d).then_inc(x_in, 16)
            sp.dma_start(con[:, :], con_d).then_inc(con_in, 16)
            sp.dma_start(ctxT, ctx_d).then_inc(ctx_in, 16)
            for n in range(first_unit["mixb"] + 1):
                unit_load(n)
            sp.dma_start(work[:, 0:2560], attn_d[:, 0:2560]).then_inc(attn_in, 16)
            sp.dma_start(view(ring, scratch + 13376, NG * P), attn_d[:, 2560:]).then_inc(pool_in, 16)
            sp.dma_start(work[NOPE:QK, 2560:3072], rope_d).then_inc(rope_in, 16)
            sp.dma_start(view(work, 3456, KD * EXPERTS), router_d).then_inc(router_in, 16)
            for n in range(first_unit["mixb"] + 1, len(units)):
                unit_load(n)
                for q in PIECES_AFTER.get(n, ()):
                    slot_free(q)
                    sp.dma_start(landed(q), moe_d[0, q]).then_inc(piece_in[q], 16)

            def expert_loads(e, i, start=0):
                for q in range(start, PIECES):
                    if not isinstance(i, int):
                        sp.wait_ge(e_low, PIECES * i + (q - PIECE_SLOTS + 1))
                    elif q >= PIECE_SLOTS:
                        sp.wait_ge(e_low, q - PIECE_SLOTS + 1)
                    else:
                        slot_free(q)
                    sp.dma_start(landed(q), moe_d[e, q]).then_inc(piece_in[q % PIECE_SLOTS], 16)

            expert_loads(0, 0, start=6)
            with sp.Fori(1, EXPERTS) as e:
                expert_loads(e, e)
            sp.wait_ge(loops_ready, 1)
            rounds = sp.value_load(loops[0:1, 1:2], min_val=1, max_val=MAX_ROUNDS)
            with sp.If(rounds > 1):
                with sp.Fori(1, rounds) as r:
                    with sp.Fori(0, EXPERTS) as e:
                        expert_loads(e, EXPERTS * r + e)
            for c in range(4):
                sp.wait_ge(out_ready, 2 * c + 2)
                at = 2 * c * T
                sp.dma_start(out_d[:, at:at + 2 * T], view(ring, at, 2 * T)).then_inc(stored, 16)
            sp.wait_ge(stored, 4 * 16)

        @block.gpsimd
        def _(pool):
            n_step = [0]

            def link(ins):
                n_step[0] += 1
                ins.then_inc(pool_step, 1)
                pool.wait_ge(pool_step, n_step[0])

            nc.gpsimd.memset(ada_rows, 0.0).then_inc(rows_zero, 1)
            nc.gpsimd.memset(condp[:, :], 0.0).then_inc(rows_zero, 1)
            nc.gpsimd.memset(pool0[:, :, 0:PAD], 0.0).then_inc(pads_zero, 1)
            nc.gpsimd.memset(pool0[:, :, PAD + T:], 0.0).then_inc(pads_zero, 1)
            pool.wait_ge(rooted, 1)
            pool.wait_ge(ctx_in, 16)
            for k in range(KD):
                nc.gpsimd.tensor_tensor(h_all[:, k, T:TA], ctxT[:, k, :], rstd[:, T:TA], ALU.mult).then_inc(context_scaled, 1)
            pool.wait_ge(pads_zero, 2)
            pool.wait_ge(rows_zero, 2)
            pool.wait_ge(mixa_taken, 2)
            pool.wait_ge(in_high, KD)
            pool.wait_ge(in_low, KD)
            pool.wait_ge(con_in, 16)
            n2, n4, n8, n16 = PADDED - 1, PADDED - 3, PADDED - 7, PADDED - 15
            link(nc.gpsimd.tensor_tensor(pool1[:, :, 0:n2], pool0[:, :, 0:n2], pool0[:, :, 1:1 + n2], ALU.add))
            link(nc.gpsimd.tensor_tensor(pool2[:, 1:, 0:n4], pool1[:, 1:, 0:n4], pool1[:, 1:, 2:2 + n4], ALU.add))
            link(nc.gpsimd.tensor_tensor(pool1[:, 2:, 0:n8], pool2[:, 2:, 0:n8], pool2[:, 2:, 4:4 + n8], ALU.add))
            link(nc.gpsimd.tensor_tensor(pool2[:, 3:, 0:n16], pool1[:, 3:, 0:n16], pool1[:, 3:, 8:8 + n16], ALU.add))
            for g, w in enumerate(WINDOWS):
                at = (pool1 if g % 2 == 0 else pool2)[:, g, PAD - w // 2:PAD - w // 2 + T]
                link(nc.gpsimd.tensor_scalar(at, at, 1.0 / w, None, ALU.mult))
                for n, ends in enumerate((at[:, 0:PAD], at[:, T - PAD:T])):
                    fix = C("edge")[:, (2 * g + n) * PAD:(2 * g + n + 1) * PAD]
                    link(nc.gpsimd.tensor_tensor(ends, ends, fix, ALU.mult))
                rows = pool0[:, g, PAD:PAD + T]
                nc.gpsimd.tensor_tensor(rows, at, rows, ALU.subtract).then_inc(pooled, 1)

        @block.scalar
        def _(act):
            act.wait_ge(vec_in, 16)
            act.wait_ge(rows_zero, 2)
            nc.scalar.activation(cond[:, :, 0:2], V("cond").rearrange("p (a b) -> p a b", a=KD), ACT.Silu).then_inc(cond_ready, 1)
            act.wait_ge(x_in, 16)
            nc.scalar.activation(square[:, :, 0:T], x, ACT.Square).then_inc(squared, 1)
            act.wait_ge(ctx_in, 16)
            nc.scalar.activation(square[:, :, T:TA], ctxT, ACT.Square).then_inc(squared, 1)
            act.wait_ge(con_in, 16)

            def mixer_highs(name, lo=0, hi=None):
                for m in range(first_piece[name] + lo, first_piece[name] + (len(MIXER[name]) if hi is None else hi)):
                    if m - first_piece[name] >= MIXER_BUFFERS:
                        act.wait_ge(mixer_used, m - MIXER_BUFFERS + 1)
                    unit_wait(act, mixer_pieces[m][0])
                    nc.scalar.activation(mixer_part(m, 0), mixer_source(m), ACT.Copy).then_inc(mixer_high, 1)

            def root(stage, source):
                act.wait_ge(mean_ready, stage + 1)
                nc.scalar.activation(rstd[:, 0:source.shape[-1]], source, ACT.Sqrt, bias=C("eps")).then_inc(root_ready, 1)

            def shifts(done, target, halves):
                for k in range(KD):
                    for n, (lo, shift) in enumerate(halves):
                        act.wait_ge(scaled, done + k * len(halves) + n + 1)
                        nc.scalar.activation(target[:, k, lo:lo + T], target[:, k, lo:lo + T], ACT.Identity,
                                             bias=shift(k)).then_inc(h_ready, 1)

            def adac(layer, part, k, who=0):
                at = 96 * layer + 2 * (KD * part + k) + who
                return ada[:, at:at + 1]

            root(0, bank[0][:, :])
            act.wait_ge(scaled, KD)
            act.wait_ge(context_scaled, KD)
            act.wait_ge(gain_ready, 1)
            for k in range(KD):
                for n in range(2):
                    ins = nc.scalar.activation(h_in[0][:, k, n * T:(n + 1) * T], h_all[:, k, n * T:(n + 1) * T], ACT.Identity,
                                               bias=adac(0, 0, k, n), scale=moda[:, n * KD + k:n * KD + k + 1])
                ins.then_inc(in_high, 1)
                if k % 2:
                    mixer_highs("mixin", k // 2, k // 2 + 1)
            mixer_highs("mixin", 4, 7)
            act.wait_ge(pads_zero, 2)
            for n in range(2):
                if n:
                    act.wait_ge(mixer_used, 4)
                else:
                    act.wait_ge(mixa_ready, 1)
                nc.scalar.activation(pool0[:, 2 * n:2 * n + 2, PAD:PAD + T],
                                     bank[1 + n][:, :].rearrange("p (a b) -> p a b", a=2), ACT.Copy).then_inc(mixa_taken, 1)
            mixer_highs("mixin", 7)
            act.wait_ge(mixer_used, 8)
            nc.scalar.activation(lora_sq[:, 0, :], bank[3][:, :], ACT.Square).then_inc(lora_squared, 1)
            nc.scalar.activation(lora_sq[:, 1, :], bank[4][:, :], ACT.Square).then_inc(lora_squared, 1)
            act.wait_ge(lora_mean, 2)
            nc.scalar.activation(rstd[:, 0:T], bank[0][:, 0:T], ACT.Sqrt, bias=C("eps"),
                                 scale=float(D) / Q_LORA).then_inc(lora_root, 1)
            nc.scalar.activation(lora_sq[:, 1, :], bank[1][:, :], ACT.Sqrt, bias=C("eps"),
                                 scale=float(D) / KV_LORA).then_inc(lora_root, 1)
            for n, (kind, p) in enumerate(PREP):
                if PREP_BY[n] != "act":
                    continue
                act.wait_ge(prep_ready, n + 1)
                b = bank[n % NPREP]
                if kind == "q":
                    nc.scalar.activation(queries[0:QK, 2 * p:2 * p + 2, :],
                                         b[0:QK, :].rearrange("p (a b) -> p a b", a=2), ACT.Copy).then_inc(prep_act, 1)
                elif kind == "k":
                    nc.scalar.activation(keys[0:NOPE, 2 * p, :], b[0:NOPE, :], ACT.Copy)
                    nc.scalar.activation(keys[0:NOPE, 2 * p + 1, :], b[NOPE:P, :], ACT.Copy).then_inc(prep_act, 1)
                else:
                    if p == 0:
                        act.wait_ge(pooled, NG)
                    nc.scalar.activation(values[:, p, :], b[:, :], ACT.Copy).then_inc(prep_act, 1)
                if (kind, p) == ("q", 3):
                    act.wait_ge(kr_roped, 1)
                    for hd in range(HEADS):
                        nc.scalar.activation(keys[NOPE:QK, hd, :], krT[NOPE:QK, :], ACT.Copy).then_inc(kr_spread, 1)

            act.wait_ge(pooled, NG)

            def turn_probs(n):
                hd, q = ITEMS[n]
                act.wait_ge(probsT_ready, n + 1)
                if hd >= 2:
                    act.wait_ge(pv_ready, hd - 1)
                nc.scalar.activation(probsT[:, hd % 2, :, q * P:(q + 1) * P],
                                     bank[3 + n % 2][:, :].rearrange("p (a b) -> p a b", a=4), ACT.Copy).then_inc(probsT_taken, 1)

            for n in range(len(ITEMS)):
                if n >= 3:
                    turn_probs(n - 3)
                act.wait_ge(max_ready, n + 1)
                if n >= 4:
                    act.wait_ge(probsT_ready, n - 3)
                nc.scalar.activation(probs[:, n % 4, :], bank[n % 3][:, :], ACT.Exp, bias=small[:, 32 + n:33 + n],
                                     scale=SCALE, accum_out=small[:, 48 + n:49 + n]).then_inc(exp_ready, 1)
            for n in range(len(ITEMS) - 3, len(ITEMS)):
                turn_probs(n)
            mixer_highs("mixout", 0, MIXER_BUFFERS)
            for g in range(NG):
                act.wait_ge(pool_ready, g // 2 + 1)
                nc.scalar.activation(mixed[0][:, NG + g, :], bank[3 + g // 2][:, (g % 2) * T:(g % 2) * T + T], ACT.Copy,
                                     scale=V("pool_scale")[:, g:g + 1]).then_inc(pool_high, 1)
            mixer_highs("mixout", MIXER_BUFFERS)

            def squares(need):
                for k in range(KD):
                    act.wait_ge(residual, need + k + 1)
                    nc.scalar.activation(square_l[:, k, :], x[:, k, :], ACT.Square).then_inc(squared, 1)

            squares(0)
            root(1, bank[6][:, 0:T])
            act.wait_ge(ada_taken, 2)
            for k in range(KD):
                act.wait_ge(scaled, KD + k + 1)
                nc.scalar.activation(h_parts[:, 0, k, :], h[:, k, :], ACT.Identity, bias=adac(0, 3, k)).then_inc(h_high, 1)
            for q in range(len(DENSE)):
                if q % 2 == 0:
                    unit_wait(act, first_unit[f"ffn{q // 2}"])
                if q >= SPLITS_DENSE:
                    act.wait_ge(used, q - SPLITS_DENSE + 1)
                nc.scalar.activation(high_d[:, q % SPLITS_DENSE, :], piece_view(q), ACT.Copy).then_inc(high_ready, 1)
                done = q - SPLITS_DENSE
                if done >= 0 and DENSE[done][0] == "w1":
                    g = DENSE[done][1]
                    if g >= 2:
                        act.wait_ge(hidden_ready, g - 1)
                    nc.scalar.activation(gate_tmp[:, g % 2], bank[0][:, :].rearrange("p (a b) -> p a b", a=2),
                                         ACT.Silu).then_inc(gate_ready, 1)
                if done >= 0 and DENSE[done][0] == "w3":
                    g = DENSE[done][1]
                    act.wait_ge(hidden_ready, g + 1)
                    if g >= 2:
                        act.wait_ge(used, DENSE.index(("w2", g - 2)) + 1)
                    nc.scalar.activation(hidden_parts[g % 2][:, 0], hidden_tmp, ACT.Copy).then_inc(hidden_high, 1)
            squares(KD)
            root(2, bank[2][:, 0:T])
            act.wait_ge(ada_taken, 4)
            shifts(2 * KD, h, [(0, lambda k: adac(1, 0, k))])
            unit_wait(act, first_unit["dft"])
            nc.scalar.activation(rows_parts[0], dft_rows, ACT.Copy).then_inc(rows_high, 1)
            for f in range(8):
                act.wait_ge(spec_ready, f + 1)
                nc.scalar.activation(spectrum[0][:, f // NG, f % NG, :], bank[2 + f % 4][:, :], ACT.Copy).then_inc(spec_high, 1)
            for f in range(4):
                act.wait_ge(four_ready, f + 1)
                nc.scalar.activation(fourier[0][:, 2 * f:2 * f + 2, :],
                                     bank[(6, 7, 0, 1)[f]][:, :].rearrange("p (a b) -> p a b", a=2), ACT.Copy).then_inc(four_high, 1)
            mixer_highs("fnet")

            def make_high(i, q):
                act.wait_ge(piece_in[q % PIECE_SLOTS], 16 * (PIECES // PIECE_SLOTS) * i + 16 * (q // PIECE_SLOTS + 1))
                nc.scalar.activation(high_e[q % SPLITS], landed(q), ACT.Copy).then_inc(e_high, 1)

            make_high(0, 0)
            squares(2 * KD)
            make_high(0, 1)
            root(3, bank[6][:, 0:T])
            act.wait_ge(ada_taken, 5)
            shifts(3 * KD, h, [(0, lambda k: adac(1, 3, k))])
            make_high(0, 2)
            act.wait_ge(logits_ready, 1)
            nc.scalar.activation(logits_e, bank[4][0:EXPERTS, 0:T], ACT.Copy).then_inc(logits_taken, 1)
            for f in range(4):
                act.wait_ge(tok_ready, f + 1)
                nc.scalar.activation(h_tok[:, f // 2, (f % 2) * 512:(f % 2) * 512 + 512], bank[f][:, :], ACT.Copy).then_inc(tok_taken, 1)
            act.wait_ge(gap_ready, 1)
            nc.scalar.activation(small[:, 66:68], small[:, 64:66], ACT.Exp).then_inc(odds_ready, 1)

            def take_gathered(i):
                act.wait_ge(gathered, i + 1)
                for n in range(2):
                    ins = nc.scalar.activation(x_parts[:, 0, 4 * n:4 * n + 4, :],
                                               bank[5 + n][:, 0:4 * CAP].rearrange("p (a b) -> p a b", a=4), ACT.Copy)
                ins.then_inc(x_high, 1)

            def take_y(done):
                act.wait_ge(e_used, PIECES * done)
                for n in range(2):
                    nc.scalar.activation(y_parts[0][:, n * 512:(n + 1) * 512], bank[2 + n][0:CAP, :], ACT.Copy,
                                         scale=slot_gate).then_inc(y_high[n], 1)

            def hidden_top(i, b):
                act.wait_ge(e_turned, BLOCKS * i + (b + 1))
                if b > 0:
                    act.wait_ge(e_used, PIECES * i + (EXPERT.index(("w2", b - 1, 1)) + 1))
                nc.scalar.activation(hidden_e_parts[:, 0], bank[4][:, 0:4 * CAP].rearrange("p (a b) -> p a b", a=4),
                                     ACT.Copy).then_inc(e_hidden_high, 1)

            def expert(i):
                first = isinstance(i, int)
                for q in range(PIECES):
                    if not (first and q < SPLITS):
                        act.wait_ge(e_used, PIECES * i + (q - SPLITS + 1))
                        make_high(i, q)
                    if q == 2 and not first:
                        take_y(i)
                    done = EXPERT[q - SPLITS] if q >= SPLITS else None
                    if done and done[0] == "w1" and done[2] == 1:
                        b = done[1]
                        if not (first and b == 0):
                            act.wait_ge(e_hidden, BLOCKS * i + b)
                        nc.scalar.activation(gate_e, bank[0][0:CAP, :], ACT.Silu).then_inc(e_gate, 1)
                    if q == hidden_at(0):
                        hidden_top(i, 0)
                    if done and done[0] == "w2" and done[2] == 1 and done[1] + 1 < BLOCKS:
                        hidden_top(i, done[1] + 1)
                    if q == 28:
                        act.wait_ge(spread_turned, i + 1)
                        nc.scalar.activation(slot_gate, bank[7][0:CAP, T:T + 1], ACT.Copy)
                        nc.scalar.activation(spread, bank[7][0:CAP, 0:T], ACT.Copy).then_inc(spread_taken, 1)
                hidden_top(i, BLOCKS - 1)
                take_gathered(i + 1)

            take_gathered(0)
            expert(0)
            act.wait_ge(loops_ready, 1)
            turns = act.value_load(loops[0:1, 0:1], min_val=EXPERTS, max_val=EXPERTS * MAX_ROUNDS)
            with act.Fori(1, turns) as i:
                expert(i)
            take_y(turns)
            squares(3 * KD)
            root(4, bank[0][:, 0:T])

        @block.vector
        def _(dve):
            n_step = [0]

            def link(ins):
                n_step[0] += 1
                ins.then_inc(dve_step, 1)
                dve.wait_ge(dve_step, n_step[0])

            def rest(source, parts):
                return nc.vector.tensor_tensor(parts[1], source, plain(parts[0]), ALU.subtract)

            def mixer_lows(name, lo=0, hi=None):
                for m in range(first_piece[name] + lo, first_piece[name] + (len(MIXER[name]) if hi is None else hi)):
                    dve.wait_ge(mixer_high, m + 1)
                    nc.vector.tensor_tensor(mixer_part(m, 1), mixer_source(m), plain(mixer_part(m, 0)),
                                            ALU.subtract).then_inc(mixer_low, 1)
                    u = mixer_pieces[m][0]
                    if m + 1 == len(mixer_pieces) or mixer_pieces[m + 1][0] != u:
                        dve.wait_ge(mixer_low, m + 1)
                        dve.sem_inc(unit_free[unit_slot(u)], 1)

            def modulation(slot, name, lo, layer, part, who=0):
                at = 96 * layer + 2 * KD * part + who
                scale = ada[:, at:at + 2 * KD - who].rearrange("p (a b) -> p a b", b=2)[:, :, 0] if who == 0 else \
                    ada[:, at - 1:at - 1 + 2 * KD].rearrange("p (a b) -> p a b", b=2)[:, :, 1]
                link(nc.vector.scalar_tensor_tensor(out=moda[:, slot * KD:(slot + 1) * KD], in0=scale, scalar=1.0,
                                                    in1=V(name)[:, lo:lo + KD], op0=ALU.add, op1=ALU.mult))

            def take_rows(run):
                dve.wait_ge(rows_ready, run + 1)
                if run == 0:
                    dve.wait_ge(rows_zero, 1)
                us = RUNS[run][1]
                nc.vector.tensor_copy(rows_of(run), bank[RUNS[run][2]][:, us[0] * P:(us[-1] + 1) * P]).then_inc(rows_taken, 1)

            def take_ada(run):
                dve.wait_ge(ada_ready, run + 1)
                part, us, _, b = RUNS[run]
                at, n = 96 * (part // PARTS) + 32 * (part % PARTS) + 8 * us[0], 8 * len(us)
                turned = bank[b][:, 0:16 * n].rearrange("p (a b) -> p a b", b=32)
                for who in range(2):
                    out = ada[:, at:at + n].rearrange("p (a b) -> p a b", b=2)[:, :, who]
                    ins = nc.vector.tensor_tensor(out, turned[:, :, who], V("ada_b")[:, at // 2:(at + n) // 2], ALU.add)
                ins.then_inc(ada_taken, 1)
                dve.wait_ge(ada_taken, run + 1)

            def reciprocal(stage, n):
                dve.wait_ge(root_ready, stage + 1)
                link(nc.vector.reciprocal(rstd[:, 0:n], rstd[:, 0:n]))

            def scale(source, target, slot, lo=0):
                for k in range(KD):
                    nc.vector.scalar_tensor_tensor(out=target[:, k, lo:lo + T], in0=source[:, k, :],
                                                   scalar=moda[:, slot * KD + k:slot * KD + k + 1],
                                                   in1=rstd[:, lo:lo + T], op0=ALU.mult, op1=ALU.mult).then_inc(scaled, 1)

            def add_projected(name, banks, layer, part):
                for k in range(KD):
                    if name and k % 4 == 0:
                        dve.wait_ge(proj_ready, 2 * (name == "fnet") + k // 4 + 1)
                    elif name and k % 4 == 2:
                        dve.wait_ge(mixer_used, first_piece[name] + 4 * (k // 4 + 1))
                    at = 96 * layer + 2 * (KD * part + k)
                    nc.vector.scalar_tensor_tensor(out=x[:, k, :], in0=bank[banks[k // 2]][:, (k % 2) * T:(k % 2) * T + T],
                                                   scalar=ada[:, at:at + 1], in1=x[:, k, :],
                                                   op0=ALU.mult, op1=ALU.add).then_inc(residual, 1)

            dve.wait_ge(vec_in, 16)
            reciprocal(0, TA)
            nc.vector.memset(small[:, 28:29], 0.0).then_inc(rooted, 1)
            for k in range(KD):
                nc.vector.tensor_tensor(h_all[:, k, 0:T], x[:, k, :], rstd[:, 0:T], ALU.mult).then_inc(scaled, 1)
            take_rows(0)
            take_ada(0)
            modulation(0, "mix_g", 0, 0, 1)
            modulation(1, "mix_g", 0, 0, 1, who=1)
            nc.vector.memset(small[:, 29:30], 0.0).then_inc(gain_ready, 1)
            dve.wait_ge(scaled, KD)
            dve.wait_ge(context_scaled, KD)
            for k in range(KD):
                for n in range(2):
                    link(nc.vector.tensor_scalar(h_plain[:, k, n * T:(n + 1) * T], h_all[:, k, n * T:(n + 1) * T],
                                                 moda[:, n * KD + k:n * KD + k + 1], ada[:, 2 * k + n:2 * k + n + 1],
                                                 ALU.mult, ALU.add))
                dve.wait_ge(in_high, k + 1)
                rest(h_plain[:, k, :], [p[:, k, :] for p in h_in]).then_inc(in_low, 1)
                if k % 2:
                    mixer_lows("mixin", k // 2, k // 2 + 1)
            mixer_lows("mixin", 4)
            dve.wait_ge(mixer_used, 8)
            dve.wait_ge(lora_squared, 2)
            nc.vector.tensor_copy(cqT, bank[3][:, :].rearrange("p (a b) -> p a b", a=2)).then_inc(cq_taken, 1)
            nc.vector.tensor_copy(ckvT, bank[4][:, :]).then_inc(kv_taken, 1)
            nc.vector.tensor_copy(krT[0:QK, :], bank[5][0:QK, :]).then_inc(kv_taken, 1)
            dve.wait_ge(cq_taken, 1)
            dve.wait_ge(kv_taken, 2)
            dve.wait_ge(lora_root, 2)
            link(nc.vector.reciprocal(rstd[:, 0:T], rstd[:, 0:T]))
            for k in range(2):
                nc.vector.scalar_tensor_tensor(out=cqT[:, k, :], in0=cqT[:, k, :], scalar=V("cq_g")[:, k:k + 1],
                                               in1=rstd[:, 0:T], op0=ALU.mult, op1=ALU.mult).then_inc(lora_ready, 1)
            link(nc.vector.reciprocal(lora_sq[:, 1, :], lora_sq[:, 1, :]))
            nc.vector.scalar_tensor_tensor(out=ckvT, in0=ckvT, scalar=V("ckv_g"), in1=lora_sq[:, 1, :],
                                           op0=ALU.mult, op1=ALU.mult).then_inc(lora_ready, 1)
            dve.wait_ge(rope_in, 16)

            def roped(target, turned, tmp, cols):
                r = slice(NOPE, QK)
                cos, sin = rope[r, 0, :], rope[r, 1, :]
                for c in range(cols):
                    last = nc.vector.tensor_tensor(tmp[r, c * T:(c + 1) * T], turned[r, c * T:(c + 1) * T], sin, ALU.mult)
                for c in range(cols):
                    last = nc.vector.tensor_tensor(target(c), target(c), cos, ALU.mult)
                link(last)
                for c in range(cols):
                    last = nc.vector.tensor_tensor(target(c), target(c), tmp[r, c * T:(c + 1) * T], ALU.add)
                return last

            for n, (kind, p) in enumerate(PREP):
                if PREP_BY[n] != "dve":
                    continue
                dve.wait_ge(prep_ready, n + 1)
                b = bank[n % NPREP]
                if kind == "kr":
                    ins = roped(lambda c: krT[NOPE:QK, 0:T], b, rope_tmp, 1)
                    ins.then_inc(kr_roped, 1)
                    dve.wait_ge(kr_roped, 1)
                    nc.vector.memset(small[:, 30:31], 0.0).then_inc(prep_dve, 1)
                else:
                    roped(lambda c: queries[NOPE:QK, 2 * p + c, :], b, rope_tmp, 2).then_inc(prep_dve, 1)
                    dve.wait_ge(prep_dve, PREP_BY[:n + 1].count("dve"))
            take_rows(1)

            def attended(hd):
                dve.wait_ge(pv_ready, hd + 1)
                if hd == 0:
                    dve.wait_ge(pooled, NG)
                lo = (hd % 2) * VD
                parts = [p[lo:lo + VD, hd // 2, :] for p in mixed]
                link(nc.vector.tensor_copy(parts[0], bank[5][lo:lo + VD, 0:T]))
                rest(bank[5][lo:lo + VD, 0:T], parts).then_inc(pv_taken, 1)

            def normalised(n):
                dve.wait_ge(exp_ready, n + 1)
                link(nc.vector.reciprocal(small[:, 48 + n:49 + n], small[:, 48 + n:49 + n]))
                nc.vector.tensor_scalar(probs[:, n % 4, :], probs[:, n % 4, :], small[:, 48 + n:49 + n], None,
                                        ALU.mult).then_inc(probs_ready, 1)

            for n in range(len(ITEMS)):
                if n >= 5 and n % 2:
                    attended((n - 5) // 2)
                dve.wait_ge(scores_ready, n + 1)
                link(nc.vector.tensor_reduce(small[:, 32 + n:33 + n], bank[n % 3][:, :], AX_X, ALU.max))
                nc.vector.tensor_scalar(small[:, 32 + n:33 + n], small[:, 32 + n:33 + n], -SCALE, None,
                                        ALU.mult).then_inc(max_ready, 1)
                if n >= 1:
                    normalised(n - 1)
                if n in ADA_TAKES:
                    (take_rows if ADA_TAKES[n] % 1 == 0 else take_ada)(int(ADA_TAKES[n]))
            normalised(len(ITEMS) - 1)
            for hd in range(6, HEADS):
                attended(hd)
            take_ada(3)
            modulation(2, "ffn_g", 0, 0, 4)
            modulation(3, "mix_g", KD, 1, 1)
            for g in range(NG):
                dve.wait_ge(pool_high, 2 * (g // 2) + 2)
                nc.vector.scalar_tensor_tensor(out=mixed[1][:, NG + g, :], in0=bank[3 + g // 2][:, (g % 2) * T:(g % 2) * T + T],
                                               scalar=V("pool_scale")[:, g:g + 1], in1=plain(mixed[0][:, NG + g, :]),
                                               op0=ALU.mult, op1=ALU.subtract).then_inc(pool_taken, 1)
            mixer_lows("mixout")
            add_projected("mixout", MIX_BANKS, 0, 2)
            reciprocal(1, T)
            for k in range(KD):
                nc.vector.scalar_tensor_tensor(out=h[:, k, :], in0=x[:, k, :], scalar=moda[:, 2 * KD + k:2 * KD + k + 1],
                                               in1=rstd[:, 0:T], op0=ALU.mult, op1=ALU.mult).then_inc(scaled, 1)
            dve.wait_ge(scaled, 2 * KD)
            for k in range(KD):
                dve.wait_ge(h_high, k + 1)
                at = 2 * (KD * 3 + k)
                nc.vector.scalar_tensor_tensor(out=h_parts[:, 1, k, :], in0=h[:, k, :], scalar=ada[:, at:at + 1],
                                               in1=plain(h_parts[:, 0, k, :]), op0=ALU.add, op1=ALU.subtract).then_inc(h_low, 1)
            for q in range(len(DENSE)):
                coming = q - SPLITS_DENSE
                if coming >= 0 and DENSE[coming][0] == "w3":
                    g = DENSE[coming][1]
                    dve.wait_ge(gate_ready, g + 1)
                    dve.wait_ge(used, coming + 1)
                    if g >= 1:
                        dve.wait_ge(hidden_high, g)
                        dve.wait_ge(hidden_low, g)
                    nc.vector.tensor_tensor(hidden_tmp, gate_tmp[:, g % 2],
                                            bank[1][:, :].rearrange("p (a b) -> p a b", a=2),
                                            ALU.mult).then_inc(hidden_ready, 1)
                dve.wait_ge(high_ready, q + 1)
                nc.vector.tensor_tensor(low_d[:, q % SPLITS_DENSE, :], piece_view(q), plain(high_d[:, q % SPLITS_DENSE, :]),
                                        ALU.subtract).then_inc(low_ready, 1)
                if q % 2 or q == len(DENSE) - 1:
                    u = first_unit[f"ffn{q // 2}"]
                    dve.wait_ge(low_ready, q + 1)
                    dve.sem_inc(unit_free[unit_slot(u)], 1)
                if coming >= 0 and DENSE[coming][0] == "w3":
                    dve.wait_ge(hidden_high, g + 1)
                    nc.vector.tensor_tensor(hidden_parts[g % 2][:, 1], hidden_tmp, plain(hidden_parts[g % 2][:, 0]),
                                            ALU.subtract).then_inc(hidden_low, 1)
                if q + 1 in ADA_TURNS:
                    take_rows(ADA_TURNS[q + 1])
                if q - 3 in ADA_TURNS:
                    take_ada(ADA_TURNS[q - 3])
            dve.wait_ge(used, len(DENSE))
            add_projected(None, FFN_BANKS, 0, 5)
            reciprocal(2, T)
            scale(x, h, 3)
            take_rows(6)
            take_ada(6)
            modulation(4, "ffn_g", KD, 1, 4)
            dve.wait_ge(rows_high, 1)
            rest(dft_rows, rows_parts).then_inc(rows_low, 1)
            for f in range(8):
                dve.wait_ge(spec_high, f + 1)
                rest(bank[2 + f % 4][:, :], [p[:, f // NG, f % NG, :] for p in spectrum]).then_inc(spec_low, 1)
            for f in range(4):
                dve.wait_ge(four_high, f + 1)
                rest(bank[(6, 7, 0, 1)[f]][:, :].rearrange("p (a b) -> p a b", a=2),
                     [p[:, 2 * f:2 * f + 2, :] for p in fourier]).then_inc(four_low, 1)
            mixer_lows("fnet")

            def make_low(i, q):
                dve.wait_ge(e_high, PIECES * i + (q + 1))
                nc.vector.tensor_tensor(low_e[q % SPLITS], landed(q), plain(high_e[q % SPLITS]),
                                        ALU.subtract).then_inc(e_low, 1)

            make_low(0, 0)
            add_projected("fnet", FNET_BANKS, 1, 2)
            reciprocal(3, T)
            scale(x, h, 4)
            make_low(0, 1)
            dve.wait_ge(logits_turned, 1)

            def cols(at, n):
                return small[:, at:at + n]

            def eights(at):
                return cols(at, 16).rearrange("p (a b) -> p a b", a=2)

            def one(at):
                return cols(at, 2).rearrange("p (a b) -> p a b", a=2)

            logit, best, key, hot1, hot2, rank = (eights(72 + 16 * j) for j in range(6))
            top1, top2, kmin, share1, share2 = (one(168 + 2 * j) for j in range(5))
            mask, mask_all = eights(184), eights(224)
            wide = [P, 2, EXPERTS]
            link(nc.vector.tensor_copy(logit, bank[4][:, T:T + 16].rearrange("p (a b) -> p a b", a=2)))
            for hot, top in ((hot1, top1), (hot2, top2)):
                link(nc.vector.tensor_reduce(top[:, :, 0], logit, AX_X, ALU.max))
                link(nc.vector.tensor_tensor(best, logit, top.to_broadcast(wide), ALU.is_equal))
                link(nc.vector.scalar_tensor_tensor(out=key, in0=best, scalar=-64.0,
                                                    in1=C("iota8").unsqueeze(1).to_broadcast(wide),
                                                    op0=ALU.mult, op1=ALU.add))
                link(nc.vector.tensor_reduce(kmin[:, :, 0], key, AX_X, ALU.min))
                link(nc.vector.tensor_tensor(hot, key, kmin.to_broadcast(wide), ALU.is_equal))
                if hot is hot1:
                    link(nc.vector.scalar_tensor_tensor(out=logit, in0=hot, scalar=-3e38, in1=logit,
                                                        op0=ALU.mult, op1=ALU.add))
            link(nc.vector.tensor_tensor(mask, hot1, hot2, ALU.add))
            nc.vector.tensor_scalar(mask_all, mask, float(D), None, ALU.mult).then_inc(mask_ready, 1)
            nc.vector.tensor_tensor(cols(64, 2), top2[:, :, 0], top1[:, :, 0], ALU.subtract).then_inc(gap_ready, 1)

            dve.wait_ge(rank_ready, 1)
            link(nc.vector.scalar_tensor_tensor(out=rank, in0=bank[5][:, 0:16].rearrange("p (a b) -> p a b", a=2),
                                                scalar=1.0, in1=mask, op0=ALU.add, op1=ALU.mult))
            full, more = cols(200, 1), cols(201, MAX_ROUNDS - 1)
            by_round = [P, 2, MAX_ROUNDS + 1, EXPERTS]

            def table(at):
                return at.rearrange("p a (b c) -> p a b c", b=MAX_ROUNDS + 1)

            link(nc.vector.tensor_tensor(table(rank_at), rank.unsqueeze(2).to_broadcast(by_round),
                                         C("first_slot").unsqueeze(1).unsqueeze(3).to_broadcast(by_round),
                                         ALU.subtract))

            def gates():
                dve.wait_ge(odds_ready, 1)
                odds = one(66)
                link(nc.vector.tensor_scalar(share1, odds, 1.0, None, ALU.add))
                link(nc.vector.reciprocal(share1, share1))
                link(nc.vector.tensor_tensor(share2, odds, share1, ALU.mult))
                link(nc.vector.tensor_tensor(best, hot1, share1.to_broadcast(wide), ALU.mult))
                link(nc.vector.tensor_tensor(key, hot2, share2.to_broadcast(wide), ALU.mult))
                link(nc.vector.tensor_tensor(best, best, key, ALU.add))
                link(nc.vector.tensor_copy(table(gate_at), best.unsqueeze(2).to_broadcast(by_round)))
                dve.wait_ge(counts_ready, 1)
                link(nc.vector.tensor_reduce(full, bank[4][:, 0:8], AX_X, ALU.max))
                for r in range(1, MAX_ROUNDS):
                    link(nc.vector.tensor_scalar(cols(200 + r, 1), full, CAP * r + 0.5, None, ALU.is_gt))
                link(nc.vector.tensor_reduce(cols(210, 1), more, AX_X, ALU.add))
                link(nc.vector.tensor_scalar(cols(211, 1), cols(210, 1), float(EXPERTS), float(EXPERTS), ALU.mult, ALU.add))
                link(nc.vector.tensor_scalar(cols(212, 1), cols(210, 1), 1.0, None, ALU.add))
                link(nc.vector.tensor_copy(loops[:, :], cols(211, 2)))
                nc.vector.memset(small[:, 31:32], 0.0).then_inc(loops_ready, 1)

            def picks(i, target, sem_out):
                for t in range(2):
                    ins = nc.vector.tensor_scalar(target[:, t, :], C("iota"), rank_at[:, t, bass.ds(i, 1)], None,
                                                  ALU.is_equal)
                ins.then_inc(sem_out, 1)

            def take_gathered(i):
                dve.wait_ge(x_high, i + 1)
                for n in range(2):
                    ins = nc.vector.tensor_tensor(x_parts[:, 1, 4 * n:4 * n + 4, :],
                                                  bank[5 + n][:, 0:4 * CAP].rearrange("p (a b) -> p a b", a=4),
                                                  plain(x_parts[:, 0, 4 * n:4 * n + 4, :]), ALU.subtract)
                ins.then_inc(x_low, 1)

            def take_y(done):
                for n in range(2):
                    dve.wait_ge(y_high[n], done)
                    half = slice(n * 512, (n + 1) * 512)
                    nc.vector.scalar_tensor_tensor(out=y_parts[1][:, half], in0=bank[2 + n][0:CAP, :], scalar=slot_gate,
                                                   in1=plain(y_parts[0][:, half]), op0=ALU.mult,
                                                   op1=ALU.subtract).then_inc(y_low[n], 1)

            def add_part(pair, last_turn=False):
                for k in (2 * pair, 2 * pair + 1):
                    at = 96 + 2 * (KD * 5 + k)
                    ins = nc.vector.scalar_tensor_tensor(out=x[:, k, :], in0=bank[5 + pair % 3][:, (k % 2) * T:(k % 2) * T + T],
                                                   scalar=ada[:, at:at + 1], in1=x[:, k, :],
                                                   op0=ALU.mult, op1=ALU.add)
                    if last_turn:
                        ins.then_inc(residual, 1)
                if not last_turn:
                    ins.then_inc(part_added[pair], 1)

            def hidden_rest(i, b):
                dve.wait_ge(e_hidden_high, BLOCKS * i + (b + 1))
                nc.vector.tensor_tensor(hidden_e_parts[:, 1], bank[4][:, 0:4 * CAP].rearrange("p (a b) -> p a b", a=4),
                                        plain(hidden_e_parts[:, 0]), ALU.subtract).then_inc(e_hidden_low, 1)

            def expert(i):
                first = isinstance(i, int)
                for q in range(PIECES):
                    done = EXPERT[q - SPLITS] if q >= SPLITS else None
                    if done and done[0] == "w3" and done[2] == 1:
                        b = done[1]
                        dve.wait_ge(e_gate, BLOCKS * i + (b + 1))
                        dve.wait_ge(e_used, PIECES * i + (q - SPLITS + 1))
                        if not (first and b == 0):
                            dve.wait_ge(e_turned, BLOCKS * i + b)
                        nc.vector.tensor_tensor(hidden_e, gate_e, bank[1][0:CAP, :], ALU.mult).then_inc(e_hidden, 1)
                    if not (first and q < SPLITS):
                        make_low(i, q)
                    if q == 2 and not first:
                        take_y(i)
                    if q == hidden_at(0):
                        hidden_rest(i, 0)
                    if done and done[0] == "w2" and done[2] == 1 and done[1] + 1 < BLOCKS:
                        hidden_rest(i, done[1] + 1)
                    if not first and q in (9, 11, 13, 15):
                        dve.wait_ge(part_ready[(q - 9) // 2], i)
                        add_part((q - 9) // 2)
                    if q == 27:
                        dve.wait_ge(spread_turned, i + 1)
                        picks(i + 1, pick, pick_ready)
                hidden_rest(i, BLOCKS - 1)
                take_gathered(i + 1)

            picks(0, pick, pick_ready)
            gates()
            make_low(0, 2)
            take_gathered(0)
            expert(0)
            turns = dve.value_load(loops[0:1, 0:1], min_val=EXPERTS, max_val=EXPERTS * MAX_ROUNDS)
            with dve.Fori(1, turns) as i:
                expert(i)
            take_y(turns)
            for pair in range(4):
                dve.wait_ge(part_ready[pair], turns)
                add_part(pair, last_turn=True)
            reciprocal(4, T)
            o = view(ring, 0, KD, T)
            for k in range(KD):
                nc.vector.scalar_tensor_tensor(out=o[:, k, :], in0=x[:, k, :], scalar=V("final_g")[:, k:k + 1],
                                               in1=rstd[:, 0:T], op0=ALU.mult, op1=ALU.mult).then_inc(out_ready, 1)

        @block.tensor
        def _(pe):
            mm = nc.tensor.matmul

            def unit(n, cols):
                s = unit_slot(n)
                return view(ring, s * UNIT, KD, cols)

            def ada_unit(part, u):
                n, run = first_unit[f"ada{part}_{u}"], RUN_OF[part, u]
                unit_wait(pe, n)
                if u == RUNS[run][1][0] and run >= 1:
                    pe.wait_ge(rows_taken, run)
                w = unit(n, 512)
                for k in range(KD):
                    for j in range(4):
                        last = mm(bank[RUNS[run][2]][32 * j:32 * j + 32, u * P:(u + 1) * P], cond[:, k, :],
                                  w[:, k, j * P:(j + 1) * P], start=(k == 0), stop=(k == KD - 1))
                last.then_inc(ada_done, 1)
                pe.wait_ge(ada_done, sum(len(RUNS[r][1]) for r in range(run)) + RUNS[run][1].index(u) + 1)
                pe.sem_inc(unit_free[unit_slot(n)], 1)
                if u == RUNS[run][1][-1]:
                    pe.sem_inc(rows_ready, 1)

            def ada_turn(run):
                pe.wait_ge(rows_taken, run + 1)
                if run >= 1:
                    pe.wait_ge(ada_taken, run)
                rows = rows_of(run)
                for n in range(len(RUNS[run][1])):
                    last = nc.tensor.transpose(bank[RUNS[run][3]][:, n * P:(n + 1) * P], rows[:, n * P:(n + 1) * P], C("ident"))
                last.then_inc(ada_ready, 1)

            def keep_warm(n, b):
                for _ in range(n):
                    mm(bank[b][:, 0:T], C("ident"), con[:, 0:T], start=True, stop=True)

            def mean(stage, before, source, out):
                for k in range(KD):
                    if stage:
                        pe.wait_ge(squared, before + k + 1)
                    last = mm(out, C("mean"), source[:, k, :], start=(k == 0), stop=(k == KD - 1))
                last.then_inc(mean_ready, 1)

            def project(name, source, banks):
                for m in range(first_piece[name], first_piece[name] + len(MIXER[name])):
                    u, k0, cols, _ = mixer_pieces[m]
                    n = u - first_unit[name]
                    parts = [mixer_part(m, part).rearrange("p (a b) -> p a b", a=2) for part in range(2)]
                    pe.wait_ge(mixer_high, m + 1)
                    for left, right in PRODUCTS:
                        if left == 1:
                            pe.wait_ge(mixer_low, m + 1)
                        for j in range(4):
                            c = 4 * n + j
                            for k in range(2):
                                last = mm(bank[banks[c // 2]][:, (c % 2) * T:(c % 2) * T + T], parts[left][:, k, j * P:(j + 1) * P],
                                          source[right][:, k0 + k, :],
                                          start=((left, right) == PRODUCTS[0] and k0 + k == 0 and c % 2 == 0),
                                          stop=((left, right) == PRODUCTS[-1] and k0 + k == KD - 1), skip_group_check=True)
                            if (left, right) == PRODUCTS[-1] and k0 == KD - 2 and j == 1:
                                last.then_inc(proj_ready, 1)
                    last.then_inc(mixer_used, 1)

            pe.wait_ge(con_in, 16)
            pe.wait_ge(cond_ready, 1)
            pe.wait_ge(squared, 2)
            mean(0, 0, square, bank[0][:, :])
            for u in range(4):
                ada_unit(0, u)
            ada_turn(0)
            for m in range(len(MIXER["mixin"])):
                u, k0, cols, _ = mixer_pieces[m]
                parts = [mixer_part(m, part).rearrange("p (a b) -> p a b", a=2) for part in range(2)]
                if m < 4:
                    outs = [(bank[1 + j // 2][:, (j % 2) * T:(j % 2) * T + T], j * P, (j + 1) * P, T, j % 2 == 0) for j in range(4)]
                else:
                    outs = [(bank[3][:, j * T:j * T + T], j * P, (j + 1) * P, T, j == 0) for j in range(2)] \
                        + [(bank[4][:, :], 256, 384, TA, True), (bank[5][0:QK, :], 320, 416, TA, True)]
                pe.wait_ge(mixer_high, m + 1)
                for left, right in PRODUCTS:
                    if left == 1:
                        pe.wait_ge(mixer_low, m + 1)
                    elif m < 4:
                        pe.wait_ge(in_low if right else in_high, k0 + 2)
                    for j, (out, lo, hi, n, opens) in enumerate(outs):
                        for k in range(2):
                            last = mm(out, parts[left][:, k, lo:hi], h_in[right][:, k0 + k, 0:n],
                                      start=((left, right) == PRODUCTS[0] and k0 + k == 0 and opens),
                                      stop=((left, right) == PRODUCTS[-1] and k0 + k == KD - 1), skip_group_check=True)
                        if m == 3 and j == 1 and (left, right) == PRODUCTS[-1]:
                            last.then_inc(mixa_ready, 1)
                last.then_inc(mixer_used, 1)
            pe.wait_ge(lora_squared, 2)
            for k in range(2):
                last = mm(bank[0][:, 0:T], C("mean"), lora_sq[:, 0, k * T:(k + 1) * T], start=(k == 0), stop=(k == 1))
            last.then_inc(lora_mean, 1)
            pe.wait_ge(mixa_taken, 2)
            mm(bank[1][:, :], C("mean"), lora_sq[:, 1, :], start=True, stop=True).then_inc(lora_mean, 1)
            for u in range(2):
                ada_unit(1, u)
            pe.wait_ge(attn_in, 16)
            pe.wait_ge(kv_taken, 2)
            for n, (kind, p) in enumerate(PREP):
                b = bank[n % NPREP]
                if n >= NPREP:
                    prep_taken(pe, n - NPREP)
                if kind == "kr":
                    pe.wait_ge(lora_root, 1)
                    last = mm(b[0:QK, 0:T], C("rot")[0:QK, :], krT[0:QK, 0:T], start=True, stop=True)
                elif kind == "q":
                    if p == 0:
                        pe.wait_ge(lora_root, 2)
                        pe.wait_ge(lora_ready, 2)
                    for j in range(2):
                        hd = 2 * p + j
                        for k in range(2):
                            last = mm(b[0:QK, j * T:(j + 1) * T], w_uq[:, k, hd * QK:(hd + 1) * QK], cqT[:, k, :],
                                      start=(k == 0), stop=(k == 1))
                elif kind == "k":
                    if p == 0:
                        pe.wait_ge(lora_ready, 3)
                    last = mm(b[:, :], w_ukv[:, 0, p * P:(p + 1) * P], ckvT, start=True, stop=True)
                elif kind == "rot":
                    pe.wait_ge(prep_act, p + 1)
                    last = mm(b[0:QK, :], C("rot")[0:QK, :], queries[0:QK, 2 * p:2 * p + 2, :], start=True, stop=True)
                else:
                    last = mm(b[:, :], ckvT[:, p * P:(p + 1) * P], w_ukv[:, 1, :], start=True, stop=True)
                last.then_inc(prep_ready, 1)
                if (kind, p) in (("q", 3), ("rot", 3)):
                    ada_unit(1, 2 + (kind == "rot"))

            pe.wait_ge(prep_act, PREP_BY.count("act"))
            pe.wait_ge(prep_dve, PREP_BY.count("dve"))
            pe.wait_ge(kr_spread, HEADS)

            def turn(n):
                pe.wait_ge(probs_ready, n + 1)
                if n >= 2:
                    pe.wait_ge(probsT_taken, n - 1)
                for kt in range(4):
                    last = nc.tensor.transpose(bank[3 + n % 2][:, kt * P:(kt + 1) * P],
                                               probs[:, n % 4, kt * P:(kt + 1) * P], C("ident"))
                last.then_inc(probsT_ready, 1)

            def attend(hd):
                pe.wait_ge(probsT_taken, 2 * hd + 2)
                if hd >= 1:
                    pe.wait_ge(pv_taken, hd)
                lo = (hd % 2) * VD
                for kt in range(4):
                    last = mm(bank[5][lo:lo + VD, 0:T], values[:, kt, hd * VD:(hd + 1) * VD], probsT[:, hd % 2, kt, :],
                              start=(kt == 0), stop=(kt == 3))
                last.then_inc(pv_ready, 1)

            for n, (hd, q) in enumerate(ITEMS):
                if n >= 3:
                    pe.wait_ge(exp_ready, n - 2)
                mm(bank[n % 3][:, :], queries[0:QK, hd, q * P:(q + 1) * P], keys[0:QK, hd, :],
                   start=True, stop=True).then_inc(scores_ready, 1)
                if n >= 2:
                    turn(n - 2)
                if n >= 4 and n % 2 == 0:
                    attend((n - 4) // 2)
                if n == 1:
                    ada_turn(1)
                if n in ADA_ITEMS:
                    ada_unit(*ADA_ITEMS[n])
                if n == 9:
                    ada_turn(2)
            for n in range(len(ITEMS) - 2, len(ITEMS)):
                turn(n)
            attend(HEADS - 2)
            ada_turn(3)
            attend(HEADS - 1)
            pe.wait_ge(pooled, NG)
            pe.wait_ge(pool_in, 16)
            pe.wait_ge(probsT_taken, len(ITEMS))
            for g, wnd in enumerate(WINDOWS):
                src = pool0[:, g, PAD:PAD + T]
                last = mm(bank[3 + g // 2][:, (g % 2) * T:(g % 2) * T + T], pool_w[:, g, :], src, start=True, stop=True)
                if g % 2:
                    last.then_inc(pool_ready, 1)
            pe.wait_ge(pool_taken, NG)
            pe.wait_ge(pv_taken, HEADS)
            project("mixout", mixed, MIX_BANKS)
            mean(1, 2, square_l, bank[6][:, 0:T])
            for u in range(2):
                ada_unit(4, u)
            keep_warm(5, 7)
            for q, (kind, g) in enumerate(DENSE):
                high, low = (view(split, n * PIECE + (q % SPLITS_DENSE) * PIECE, PIECE) for n in (0, SPLITS_DENSE))
                pe.wait_ge(high_ready, q + 1)
                if kind == "w2":
                    pe.wait_ge(hidden_low, g + 1)
                    if g == 0:
                        pe.wait_ge(ada_taken, 4)
                elif g >= 1:
                    pe.wait_ge(gate_ready if kind == "w1" else hidden_ready, g)
                for n, (w, right) in enumerate(((high, 0), (high, 1), (low, 0))):
                    if n == 2:
                        pe.wait_ge(low_ready, q + 1)
                    if kind == "w2":
                        w = w.rearrange("p (a b) -> p a b", a=2)
                        for j in range(2):
                            for k in range(KD):
                                last = mm(bank[FFN_BANKS[k // 2]][:, (k % 2) * T:(k % 2) * T + T], w[:, j, k * P:(k + 1) * P],
                                          hidden_parts[g % 2][:, right, j, :],
                                          start=(g == 0 and n == 0 and j == 0 and k % 2 == 0),
                                          stop=(g == GROUPS - 1 and n == 2 and j == 1), skip_group_check=True)
                    else:
                        w = w.rearrange("p (a b) -> p a b", a=KD)
                        for j in range(2):
                            for k in range(KD):
                                if q == 0 and n < 2 and j == 0:
                                    pe.wait_ge(h_low if n else h_high, k + 1)
                                last = mm(bank[kind == "w3"][:, j * T:(j + 1) * T],
                                          w[:, k, j * P:(j + 1) * P], h_parts[:, right, k, :],
                                          start=(n == 0 and j == 0 and k == 0), stop=(n == 2 and k == KD - 1),
                                          skip_group_check=True)
                last.then_inc(used, 1)
                for part, u in ADA_DENSE.get((q + 1) // 2, ()) if q % 2 else ():
                    ada_unit(part, u)
                if q in ADA_TURNS:
                    ada_turn(ADA_TURNS[q])
            pe.wait_ge(hidden_ready, GROUPS)
            mean(2, 2 + KD, square_l, bank[2][:, 0:T])
            for u in range(2):
                ada_unit(5, u)
            ada_turn(6)
            u = first_unit["dft"]
            unit_wait(pe, u)
            chan = view(ring, unit_slot(u) * UNIT, 2, 2 * GC)
            pe.wait_ge(h_ready, KD)
            for f in range(8):
                t, g = f // NG, f % NG
                if f >= 4:
                    pe.wait_ge(spec_low, f - 3)
                for k in range(2):
                    last = mm(bank[2 + f % 4][:, :], h[:, 2 * g + k, t * P:(t + 1) * P], chan[:, k, :],
                              start=(k == 0), stop=(k == 1))
                last.then_inc(spec_ready, 1)
            pe.wait_ge(spec_low, 8)
            pe.wait_ge(rows_low, 1)
            pe.sem_inc(unit_free[unit_slot(u)], 1)
            pe.wait_ge(ada_taken, 7)
            for c in range(KD):
                n = 0
                for part in range(2):
                    for t in range(2):
                        at = part * GC + (c % 2) * P
                        for left, right in PRODUCTS:
                            last = mm(bank[(6, 7, 0, 1)[c // 2]][:, (c % 2) * T:(c % 2) * T + T],
                                      spectrum[left][:, t, c // 2, at:at + P], rows_parts[right][:, part, t, :],
                                      start=(n == 0), stop=(n == 11))
                            n += 1
                if c % 2:
                    last.then_inc(four_ready, 1)
            pe.wait_ge(four_low, 4)
            project("fnet", fourier, FNET_BANKS)
            mean(3, 2 + 2 * KD, square_l, bank[6][:, 0:T])
            keep_warm(7, 7)
            pe.wait_ge(router_in, 16)
            for k in range(KD):
                pe.wait_ge(h_ready, KD + k + 1)
                last = mm(bank[4][0:EXPERTS, 0:T], router[:, k, :], h[:, k, :], start=(k == 0), stop=(k == KD - 1))
            last.then_inc(logits_ready, 1)
            pe.wait_ge(logits_taken, 1)
            for t in range(2):
                last = nc.tensor.transpose(bank[4][:, T + 8 * t:T + 8 * t + 8], logits_e[:, t * P:(t + 1) * P],
                                           C("ident")[0:EXPERTS, 0:EXPERTS])
            last.then_inc(logits_turned, 1)
            for f in range(4):
                for j in range(4):
                    last = nc.tensor.transpose(bank[f][:, j * P:(j + 1) * P],
                                               h[:, 4 * (f % 2) + j, (f // 2) * P:(f // 2 + 1) * P], C("ident"))
                last.then_inc(tok_ready, 1)
            pe.wait_ge(tok_ready, 4)
            pe.sem_inc(scratch_free, 1)
            keep_warm(3, 7)
            pe.wait_ge(mask_ready, 1)
            mask, all0, all1 = small[:, 184:200], small[:, 224:232], small[:, 232:240]
            mm(bank[5][:, 0:16], C("before"), mask, start=True, stop=False)
            mm(bank[5][:, 8:16], C("mean"), all0, start=False, stop=True).then_inc(rank_ready, 1)
            mm(bank[4][:, 0:8], C("mean"), all0, start=True, stop=False)
            mm(bank[4][:, 0:8], C("mean"), all1, start=False, stop=True).then_inc(counts_ready, 1)

            def gather(i):
                pe.wait_ge(pick_ready, i + 1)
                for k in range(KD):
                    for t in range(2):
                        last = mm(bank[5 + k // 4][:, (k % 4) * CAP:(k % 4 + 1) * CAP], h_tok[:, t, k * P:(k + 1) * P],
                                  pick[:, t, :], start=(t == 0), stop=(t == 1))
                last.then_inc(gathered, 1)

            def combine(done, pair):
                if pair == 0:
                    pe.wait_ge(spread_taken, done)
                pe.wait_ge(y_low[pair // 2], done)
                for k in (2 * pair, 2 * pair + 1):
                    for n in range(2):
                        last = mm(bank[5 + pair % 3][:, (k % 2) * T:(k % 2) * T + T],
                                  y_parts[n][:, k * P:(k + 1) * P], spread, start=(n == 0), stop=(n == 1))
                last.then_inc(part_ready[pair], 1)

            def expert(i):
                first = isinstance(i, int)
                pe.wait_ge(x_high, i + 1)
                for q, (kind, b, half) in enumerate(EXPERT):
                    high, low = high_e[q % SPLITS], low_e[q % SPLITS]
                    pe.wait_ge(e_high, PIECES * i + (q + 1))
                    if kind == "w2":
                        if half == 0:
                            pe.wait_ge(e_hidden_low, BLOCKS * i + (b + 1))
                            if b == 0 and not first:
                                pe.wait_ge(y_low[0], i)
                                pe.wait_ge(y_low[1], i)
                    elif half == 0 and not (first and b == 0):
                        pe.wait_ge(e_gate if kind == "w1" else e_hidden, BLOCKS * i + b)
                    for n, (w, right) in enumerate(((high, 0), (high, 1), (low, 0))):
                        if n == 1 and q == 0:
                            pe.wait_ge(x_low, i + 1)
                        if n == 2:
                            pe.wait_ge(e_low, PIECES * i + (q + 1))
                        if kind == "w2":
                            w = w.rearrange("p (a b) -> p a b", a=2)
                            for j in range(2):
                                for m in range(2):
                                    last = mm(bank[2 + m][0:CAP, :], hidden_e_parts[:, right, 2 * half + j, :],
                                              w[:, j, m * 512:(m + 1) * 512], start=(b == 0 and half == 0 and n == 0 and j == 0),
                                              stop=(b == BLOCKS - 1 and half == 1 and n == 2 and j == 1))
                        else:
                            w = w.rearrange("p (a b) -> p a b", a=4)
                            for k in range(4):
                                last = mm(bank[kind == "w3"][0:CAP, :], x_parts[:, right, 4 * half + k, :], w[:, k, :],
                                          start=(half == 0 and n == 0 and k == 0), stop=(half == 1 and n == 2 and k == 3))
                    last.then_inc(e_used, 1)
                    if q == PIECES - 4:
                        gather(i + 1)
                    if q == 5 or (kind == "w2" and b + 1 < BLOCKS and half == (b + 2 < BLOCKS)):
                        turned = 0 if q == 5 else b + 1
                        pe.wait_ge(e_hidden, BLOCKS * i + (turned + 1))
                        for j in range(4):
                            last = nc.tensor.transpose(bank[4][:, j * CAP:(j + 1) * CAP], hidden_e[:, j * P:(j + 1) * P],
                                                       C("ident")[0:CAP, 0:CAP])
                        last.then_inc(e_turned, 1)
                    if not first and q in (5, 7, 9, 11):
                        if q == 11:
                            pe.wait_ge(part_added[0], i)
                        combine(i, (q - 5) // 2)
                    if q == 22:
                        if not first:
                            pe.wait_ge(part_added[2], i)
                        for t in range(2):
                            mm(bank[7][0:CAP, T:T + 1], pick[:, t, :], gate_at[:, t, bass.ds(i, 1)], start=(t == 0), stop=(t == 1))
                        for t in range(2):
                            last = nc.tensor.transpose(bank[7][0:CAP, t * P:(t + 1) * P], pick[:, t, :], C("ident"))
                        last.then_inc(spread_turned, 1)

            pe.wait_ge(tok_taken, 4)
            keep_warm(2, 7)
            gather(0)
            expert(0)
            pe.wait_ge(loops_ready, 1)
            turns = pe.value_load(loops[0:1, 0:1], min_val=EXPERTS, max_val=EXPERTS * MAX_ROUNDS)
            with pe.Fori(1, turns) as i:
                expert(i)
            pe.wait_ge(x_low, turns + 1)
            for pair in range(4):
                if pair == 3:
                    pe.wait_ge(residual, 3 * KD + 2)
                combine(turns, pair)
            mean(4, 2 + 3 * KD, square_l, bank[0][:, 0:T])


def kernel(**inputs):
    import concourse.bacc as _bacc
    from concourse.bass_utils import run_bass_kernel_spmd as _run

    a = {k: np.asarray(v) for k, v in inputs.items()}

    def chunks(v):
        return v.reshape(-1, P).T

    def rows(w, cols):
        return w.reshape(KD, P, -1, cols).transpose(2, 1, 0, 3).reshape(-1, P, KD * cols)

    def dense(w1, w3, w2):
        of = {"w1": rows(w1, PAIR), "w3": rows(w3, PAIR),
              "w2": w2.reshape(GROUPS, 2, P, D).transpose(0, 2, 1, 3).reshape(GROUPS, P, PIECE)}
        pieces = [of[w][g] for w, g in DENSE] + [np.zeros((P, PIECE), np.float32)] * (len(DENSE) % 2)
        return np.stack(pieces).reshape(DENSE_UNITS, 2, P, PIECE).transpose(0, 2, 1, 3).reshape(DENSE_UNITS, P, UNIT)

    def expert(w1, w3, w2):
        of = {"w1": w1.reshape(2, 4, P, BLOCKS, BLOCK).transpose(3, 0, 2, 1, 4).reshape(BLOCKS, 2, P, PIECE),
              "w3": w3.reshape(2, 4, P, BLOCKS, BLOCK).transpose(3, 0, 2, 1, 4).reshape(BLOCKS, 2, P, PIECE),
              "w2": w2.reshape(BLOCKS, 2, 2, P, D).transpose(0, 1, 3, 2, 4).reshape(BLOCKS, 2, P, PIECE)}
        return np.stack([of[w][b, n] for w, b, n in EXPERT])

    con, rope, dft = constants()
    vec = np.concatenate([
        *[chunks(a["norm_mix_g"][i]) for i in range(2)], *[chunks(a["norm_ffn_g"][i]) for i in range(2)],
        chunks(a["final_g"]), chunks(a["cq_norm_g"][0]), chunks(a["ckv_norm_g"][0]), chunks(a["pool_scale"][0]),
        *[chunks(a["ada_b"][i]) for i in range(2)],
        np.stack([chunks(a["c"][0]), chunks(a["c_ctx"])], axis=2).reshape(P, 2 * KD)], axis=1)
    w_in = a["mix_in_w"][0]
    low = Q_LORA + KV_LORA + ROPE
    ukv = a["w_ukv"][0].reshape(KV_LORA, HEADS, 2, VD).transpose(0, 2, 1, 3).reshape(KV_LORA, -1)
    attn = np.concatenate([
        a["w_uq"][0].reshape(2, P, -1).transpose(1, 0, 2).reshape(P, -1), ukv,
        a["pool_w"][0].transpose(1, 0, 2).reshape(P, -1)], axis=1)
    arrays = {
        "vec": vec, "con": con, "rope": rope,
        "x": a["x"][0].T.reshape(KD, P, T).transpose(1, 0, 2).reshape(P, -1),
        "ctx": a["ctx"][0].T.reshape(KD, P, TC).transpose(1, 0, 2),
        "ada": np.stack([rows(a["ada_w"][i], 512) for i in range(2)]),
        "mixa": rows(w_in[:, low:], 512)[0], "mixb": rows(w_in[:, :low], low)[0],
        "attn": attn, "mixout": rows(a["mix_out_w"][0], 512),
        "ffn": dense(a["ffn_w1"][0], a["ffn_w3"][0], a["ffn_w2"][0]),
        "dft": dft, "fnet": rows(a["fnet_out_w"][0], 512),
        "router": a["router_w"][0].reshape(KD, P, EXPERTS).transpose(1, 0, 2).reshape(P, -1),
        "moe": np.stack([expert(a["moe_w1"][0, e], a["moe_w3"][0, e], a["moe_w2"][0, e]) for e in range(EXPERTS)]),
    }
    nc = _bacc.Bacc("TRN2", target_bir_lowering=False, num_devices=1)
    given, args = {}, []
    for name, v in arrays.items():
        v = np.ascontiguousarray(v)
        given[f"in_{name}"] = v
        args.append(nc.dram_tensor(f"in_{name}", v.shape, mybir.dt.from_np(v.dtype), kind="ExternalInput").ap())
    args.append(nc.dram_tensor("out_xT", (P, KD * T), F32, kind="ExternalOutput").ap())
    build(nc, *args)
    r = _run(nc, [given], core_ids=[0])
    out = r.results[0]["out_xT"]
    return out.reshape(P, KD, T).transpose(2, 1, 0).reshape(1, T, D)
```
